# Optimizing a Trainium2 kernel written in Bass

```python
import math
import jax, jax.numpy as jnp
from jax import lax
import numpy as np

D_MODEL = 1024
BATCH = 1
SEQ = 1024
DEPTH = 2

N_MIXERS = 2
EPS = 1e-6
ATTN_HEADS = 16
ATTN_KV_HEADS = 4
ATTN_HEAD_DIM = D_MODEL // ATTN_HEADS
ATTN_GROUP = ATTN_HEADS // ATTN_KV_HEADS
WINDOW = 128
BLOCK = 128
ROPE_THETA = 500000.0
ROPE_DIM = ATTN_HEAD_DIM // 4
Q_W = ATTN_HEADS * ATTN_HEAD_DIM
KV_W = ATTN_KV_HEADS * ATTN_HEAD_DIM
MEM_LEN = 256
MEM_HEADS = 4
MEM_HEAD_DIM = 128
MEM_W = MEM_HEADS * MEM_HEAD_DIM
LRU_WIDTH = D_MODEL
LRU_BLOCKS = 8
LRU_BLOCK_DIM = LRU_WIDTH // LRU_BLOCKS
LRU_C = 8.0
CONV_WIDTH = 4
CONV_LEFT = (CONV_WIDTH - 1) // 2
ATTN_IN_W = Q_W + 2 * KV_W + MEM_W
LRU_IN_W = 2 * LRU_WIDTH + MEM_W
MIX_OUT_W = Q_W + MEM_W
D_FF = 4 * D_MODEL
NEG = -1e30


def rms_norm(x, g):
    xf = x.astype(jnp.float32)
    y = xf * lax.rsqrt(jnp.mean(xf * xf, axis=-1, keepdims=True) + EPS) * g.astype(jnp.float32)
    return y.astype(x.dtype)

def partial_rotary(t, positions):
    half = ROPE_DIM // 2
    inv_freq = ROPE_THETA ** (-2.0 * jnp.arange(half, dtype=jnp.float32) / ROPE_DIM)
    ang = positions.astype(jnp.float32)[..., None] * inv_freq
    cos = jnp.cos(ang)[:, :, None, :]
    sin = jnp.sin(ang)[:, :, None, :]
    tr = t[..., :ROPE_DIM].astype(jnp.float32)
    t1, t2 = tr[..., :half], tr[..., half:]
    rot = jnp.concatenate([t1 * cos - t2 * sin, t2 * cos + t1 * sin], axis=-1)
    return jnp.concatenate([rot.astype(t.dtype), t[..., ROPE_DIM:]], axis=-1)

def window_gqa(q, k, v, sinks):
    B, S = q.shape[0], q.shape[1]
    nb = S // BLOCK
    qb = q.reshape(B, nb, BLOCK, ATTN_KV_HEADS, ATTN_GROUP, ATTN_HEAD_DIM)
    pad = ((0, 0), (BLOCK, BLOCK), (0, 0), (0, 0))

    def bands(t):
        tb = jnp.pad(t, pad).reshape(B, nb + 2, BLOCK, ATTN_KV_HEADS, ATTN_HEAD_DIM)
        return jnp.concatenate([tb[:, :nb], tb[:, 1:nb + 1], tb[:, 2:]], axis=2)

    kb, vb = bands(k), bands(v)
    scores = jnp.einsum('bnqhgd,bnkhd->bnhgqk', qb, kb,
                        preferred_element_type=jnp.float32) * (ATTN_HEAD_DIM ** -0.5)
    q_idx = jnp.arange(BLOCK)
    k_idx = jnp.arange(3 * BLOCK)
    rel = k_idx[None, :] - BLOCK - q_idx[:, None]
    k_abs = jnp.arange(nb)[:, None] * BLOCK - BLOCK + k_idx[None, :]
    mask = (jnp.abs(rel) <= WINDOW)[None] & ((k_abs >= 0) & (k_abs < S))[:, None, :]
    scores = jnp.where(mask[None, :, None, None], scores, NEG)
    s = sinks.astype(jnp.float32).reshape(ATTN_KV_HEADS, ATTN_GROUP)[None, None, :, :, None, None]
    m = jnp.maximum(jnp.max(scores, axis=-1, keepdims=True), s)
    p = jnp.exp(scores - m)
    probs = p / (jnp.sum(p, axis=-1, keepdims=True) + jnp.exp(s - m))
    out = jnp.einsum('bnhgqk,bnkhd->bnqhgd', probs.astype(v.dtype), vb)
    return out.reshape(B, S, Q_W)

def memory_attention(mq, mk, mv):
    B, S = mq.shape[0], mq.shape[1]
    sc = jnp.einsum('bshd,bmhd->bhsm', mq, mk,
                    preferred_element_type=jnp.float32) * (MEM_HEAD_DIM ** -0.5)
    p = jax.nn.softmax(sc, axis=-1)
    out = jnp.einsum('bhsm,bmhd->bshd', p.astype(mv.dtype), mv)
    return out.reshape(B, S, MEM_W)

def centred_depthwise_conv(x, w, b):
    S = x.shape[1]
    xp = jnp.pad(x, ((0, 0), (CONV_LEFT, CONV_WIDTH - 1 - CONV_LEFT), (0, 0)))
    y = b
    for tap in range(CONV_WIDTH):
        y = y + xp[:, tap:tap + S] * w[tap]
    return y

def block_diag_linear(x, w, b):
    B, S = x.shape[0], x.shape[1]
    xr = x.reshape(B, S, LRU_BLOCKS, LRU_BLOCK_DIM)
    return jnp.einsum('bsnd,nde->bsne', xr, w).reshape(B, S, LRU_WIDTH) + b

def _linear_combine(c1, c2):
    a1, b1 = c1
    a2, b2 = c2
    return a1 * a2, a2 * b1 + b2

def rg_lru(x, wa, ba, wx, bx, lam, reverse):
    xf = x.astype(jnp.float32)
    r = jax.nn.sigmoid(block_diag_linear(x, wa, ba).astype(jnp.float32))
    i = jax.nn.sigmoid(block_diag_linear(x, wx, bx).astype(jnp.float32))
    log_a = -LRU_C * r * jax.nn.softplus(-lam.astype(jnp.float32))
    a = jnp.exp(log_a)
    u = jnp.sqrt(-jnp.expm1(2.0 * log_a)) * (i * xf)
    _, h = lax.associative_scan(_linear_combine, (a, u), axis=1, reverse=reverse)
    return h.astype(x.dtype)

def attn_mixer(h, positions, w_in, sinks):
    B, S = h.shape[0], h.shape[1]
    p = h @ w_in
    q, k, v, mq = jnp.split(p, [Q_W, Q_W + KV_W, Q_W + 2 * KV_W], axis=-1)
    q = partial_rotary(q.reshape(B, S, ATTN_HEADS, ATTN_HEAD_DIM), positions)
    k = partial_rotary(k.reshape(B, S, ATTN_KV_HEADS, ATTN_HEAD_DIM), positions)
    v = v.reshape(B, S, ATTN_KV_HEADS, ATTN_HEAD_DIM)
    return window_gqa(q, k, v, sinks), mq.reshape(B, S, MEM_HEADS, MEM_HEAD_DIM)

def lru_mixer(h, w_in, conv_w, conv_b, wa, ba, wx, bx, lam):
    B, S = h.shape[0], h.shape[1]
    p = h @ w_in
    xb, gate, mq = jnp.split(p, [LRU_WIDTH, 2 * LRU_WIDTH], axis=-1)
    xc = centred_depthwise_conv(xb, conv_w, conv_b)
    y = (rg_lru(xc, wa[0], ba[0], wx[0], bx[0], lam[0], False)
         + rg_lru(xc, wa[1], ba[1], wx[1], bx[1], lam[1], True))
    y = y * jax.nn.gelu(gate)
    return y, mq.reshape(B, S, MEM_HEADS, MEM_HEAD_DIM)

def squared_relu_mlp(h, w_up, w_down):
    return jnp.square(jax.nn.relu(h @ w_up)) @ w_down

def first_inputs(seed: int = 0) -> dict:
    key = jax.random.key(seed)
    ks = jax.random.split(key, 24)
    n_attn = (DEPTH + N_MIXERS - 1) // N_MIXERS
    n_lru = DEPTH // N_MIXERS
    f32 = jnp.float32

    def nrm(k, shape, scale):
        return jax.random.normal(k, shape, f32) * scale

    u = jax.random.uniform(ks[20], (n_lru, 2, LRU_WIDTH), f32, minval=0.9, maxval=0.999)
    s = u ** (1.0 / LRU_C)
    lam = jnp.log(s) - jnp.log1p(-s)
    positions = (jnp.arange(SEQ, dtype=jnp.int32)[None, :]
                 + jax.random.randint(ks[21], (BATCH, 1), 0, 1024, dtype=jnp.int32))
    return {
        "x": nrm(ks[0], (BATCH, SEQ, D_MODEL), 1.0),
        "mem": nrm(ks[1], (BATCH, MEM_LEN, D_MODEL), 1.0),
        "positions": positions,
        "mix_norm": 1.0 + nrm(ks[2], (DEPTH, D_MODEL), 0.05),
        "mlp_norm": 1.0 + nrm(ks[3], (DEPTH, D_MODEL), 0.05),
        "mem_norm": 1.0 + nrm(ks[4], (D_MODEL,), 0.05),
        "final_norm": 1.0 + nrm(ks[5], (D_MODEL,), 0.05),
        "w_mem_kv": nrm(ks[6], (DEPTH, D_MODEL, 2 * MEM_W), D_MODEL ** -0.5),
        "w_out": nrm(ks[7], (DEPTH, MIX_OUT_W, D_MODEL), MIX_OUT_W ** -0.5),
        "w_up": nrm(ks[8], (DEPTH, D_MODEL, D_FF), D_MODEL ** -0.5),
        "w_down": nrm(ks[9], (DEPTH, D_FF, D_MODEL), D_FF ** -0.5),
        "attn_w_in": nrm(ks[10], (n_attn, D_MODEL, ATTN_IN_W), D_MODEL ** -0.5),
        "attn_sinks": nrm(ks[11], (n_attn, ATTN_HEADS), 0.5),
        "lru_w_in": nrm(ks[12], (n_lru, D_MODEL, LRU_IN_W), D_MODEL ** -0.5),
        "lru_conv_w": nrm(ks[13], (n_lru, CONV_WIDTH, LRU_WIDTH), CONV_WIDTH ** -0.5),
        "lru_conv_b": nrm(ks[14], (n_lru, LRU_WIDTH), 0.02),
        "lru_wa": nrm(ks[15], (n_lru, 2, LRU_BLOCKS, LRU_BLOCK_DIM, LRU_BLOCK_DIM), LRU_BLOCK_DIM ** -0.5),
        "lru_ba": nrm(ks[16], (n_lru, 2, LRU_WIDTH), 0.02),
        "lru_wx": nrm(ks[17], (n_lru, 2, LRU_BLOCKS, LRU_BLOCK_DIM, LRU_BLOCK_DIM), LRU_BLOCK_DIM ** -0.5),
        "lru_bx": nrm(ks[18], (n_lru, 2, LRU_WIDTH), 0.02),
        "lru_lambda": lam,
    }

def first_block(x, mem, positions, mix_norm, mlp_norm, mem_norm, final_norm, w_mem_kv, w_out,
              w_up, w_down, attn_w_in, attn_sinks, lru_w_in, lru_conv_w, lru_conv_b,
              lru_wa, lru_ba, lru_wx, lru_bx, lru_lambda):
    B = mem.shape[0]
    mem_n = rms_norm(mem, mem_norm)
    for l in range(DEPTH):
        kind = l % N_MIXERS
        j = l // N_MIXERS
        h = rms_norm(x, mix_norm[l])
        kv = mem_n @ w_mem_kv[l]
        mk = kv[..., :MEM_W].reshape(B, MEM_LEN, MEM_HEADS, MEM_HEAD_DIM)
        mv = kv[..., MEM_W:].reshape(B, MEM_LEN, MEM_HEADS, MEM_HEAD_DIM)
        if kind == 0:
            mixed, mq = attn_mixer(h, positions, attn_w_in[j], attn_sinks[j])
        else:
            mixed, mq = lru_mixer(h, lru_w_in[j], lru_conv_w[j], lru_conv_b[j], lru_wa[j],
                                  lru_ba[j], lru_wx[j], lru_bx[j], lru_lambda[j])
        mo = memory_attention(mq, mk, mv)
        x = x + jnp.concatenate([mixed, mo], axis=-1) @ w_out[l]
        x = x + squared_relu_mlp(rms_norm(x, mlp_norm[l]), w_up[l], w_down[l])
    return rms_norm(x, final_norm)


DEPTH_2 = 1

CHUNK = 64
GLA_HEADS = 4
GLA_DK = D_MODEL // 2
GLA_DV = D_MODEL
GLA_HEAD_DK = GLA_DK // GLA_HEADS
GLA_HEAD_DV = GLA_DV // GLA_HEADS
GATE_RANK = 16
GATE_TAU = 16.0
POOL_WIDTH = D_MODEL
POOL_WINDOWS = (2, 4, 8, 16)
POOL_GROUPS = len(POOL_WINDOWS)
POOL_GROUP_DIM = POOL_WIDTH // POOL_GROUPS
N_BRANCHES = 2
IN_SPLITS = (GLA_DK, GLA_DK, GLA_DV, GLA_DV, GATE_RANK, POOL_WIDTH, POOL_WIDTH, N_BRANCHES * D_MODEL)
IN_COLS = sum(IN_SPLITS)
IN_OFFSETS = tuple(int(v) for v in np.cumsum(IN_SPLITS)[:-1])
DEEPNORM_ALPHA = (2.0 * DEPTH_2) ** 0.25
DEEPNORM_BETA = (8.0 * DEPTH_2) ** -0.25
EPS_2 = 1e-5


def _layernorm(x, g, b):
    x32 = x.astype(jnp.float32)
    mu = jnp.mean(x32, axis=-1, keepdims=True)
    var = jnp.mean(jnp.square(x32 - mu), axis=-1, keepdims=True)
    return ((x32 - mu) * lax.rsqrt(var + EPS_2) * g + b).astype(x.dtype)

def _gla_chunked(q, k, v, log_alpha):
    B, S, H, dk = q.shape
    dv = v.shape[-1]
    nc = S // CHUNK

    def to_chunks(a):
        return a.reshape(B, nc, CHUNK, H, a.shape[-1]).transpose(1, 0, 3, 2, 4)

    qc, kc, vc, lac = to_chunks(q), to_chunks(k), to_chunks(v), to_chunks(log_alpha)

    def step(state, inp):
        qb, kb, vb, lab = inp
        G = jnp.cumsum(lab, axis=2)
        decay = jnp.exp(-jnp.abs(G[:, :, :, None, :] - G[:, :, None, :, :]))
        scores = jnp.einsum('bhtd,bhsd,bhtsd->bhts', qb, kb, decay)
        o_intra = jnp.einsum('bhts,bhsv->bhtv', scores, vb)
        o_inter = jnp.einsum('bhtd,bhdv->bhtv', qb * jnp.exp(G), state)
        G_last = G[:, :, -1:, :]
        new_state = jnp.exp(G_last)[:, :, 0, :, None] * state + jnp.einsum(
            'bhsd,bhsv->bhdv', kb * jnp.exp(G_last - G), vb)
        return new_state, o_intra + o_inter

    state0 = jnp.zeros((B, H, dk, dv), jnp.float32)
    _, o = lax.scan(step, state0, (qc, kc, vc, lac))
    return o.transpose(1, 0, 3, 2, 4).reshape(B, S, H, dv)

def _multiscale_pool(u, w_grp, scale):
    B, S, _ = u.shape
    ug = u.astype(jnp.float32).reshape(B, S, POOL_GROUPS, POOL_GROUP_DIM)
    csum = jnp.cumsum(ug, axis=1)
    pos = jnp.arange(1, S + 1)
    means = []
    for g, w in enumerate(POOL_WINDOWS):
        c = csum[:, :, g]
        shifted = jnp.pad(c, ((0, 0), (w, 0), (0, 0)))[:, :S]
        cnt = jnp.minimum(pos, w).astype(jnp.float32)
        means.append((c - shifted) / cnt[None, :, None])
    pooled = jnp.stack(means, axis=2) - ug
    mixed = jnp.einsum('bsgi,gio->bsgo', pooled, w_grp)
    return mixed.reshape(B, S, POOL_WIDTH) * scale

def _layer(x, w_in, w_alpha_up, b_alpha, gla_norm_g, w_pool_grp, pool_scale,
           b_merge, w_proj_a, w_proj_b, w_out, ln_g, ln_b):
    B, S, _ = x.shape
    h = x @ w_in
    q, k, v, gate_a, alpha_low, pool_in, gate_b, merge_logits = jnp.split(h, IN_OFFSETS, axis=-1)

    log_alpha = jax.nn.log_sigmoid((alpha_low @ w_alpha_up + b_alpha).astype(jnp.float32)) / GATE_TAU
    qh = q.reshape(B, S, GLA_HEADS, GLA_HEAD_DK) * (GLA_HEAD_DK ** -0.5)
    kh = k.reshape(B, S, GLA_HEADS, GLA_HEAD_DK)
    vh = v.reshape(B, S, GLA_HEADS, GLA_HEAD_DV)
    lah = log_alpha.reshape(B, S, GLA_HEADS, GLA_HEAD_DK)
    o = _gla_chunked(qh, kh, vh, lah)
    o = o * lax.rsqrt(jnp.mean(jnp.square(o), axis=-1, keepdims=True) + EPS_2) * gla_norm_g
    y_a = o.reshape(B, S, GLA_DV).astype(x.dtype) * jax.nn.silu(gate_a)

    y_b = _multiscale_pool(pool_in, w_pool_grp, pool_scale).astype(x.dtype) * jax.nn.silu(gate_b)

    gates = jax.nn.sigmoid(merge_logits + b_merge)
    g_a, g_b = jnp.split(gates, N_BRANCHES, axis=-1)
    merged = g_a * (y_a @ w_proj_a) + g_b * (y_b @ w_proj_b)
    y = merged @ w_out

    return _layernorm(DEEPNORM_ALPHA * x + y, ln_g, ln_b)

def second_inputs(seed: int = 0) -> dict:
    key = jax.random.key(seed)
    ks = jax.random.split(key, 14)
    f32 = jnp.float32
    nrm = lambda k, shape, s: jax.random.normal(k, shape, f32) * s
    return {
        "x": jax.random.normal(ks[0], (BATCH, SEQ, D_MODEL), f32),
        "w_in": nrm(ks[1], (DEPTH_2, D_MODEL, IN_COLS), D_MODEL ** -0.5),
        "w_alpha_up": nrm(ks[2], (DEPTH_2, GATE_RANK, GLA_DK), GATE_RANK ** -0.5),
        "b_alpha": nrm(ks[3], (DEPTH_2, GLA_DK), 0.01),
        "gla_norm_g": 1.0 + nrm(ks[4], (DEPTH_2, GLA_HEADS, GLA_HEAD_DV), 0.02),
        "w_pool_grp": nrm(ks[5], (DEPTH_2, POOL_GROUPS, POOL_GROUP_DIM, POOL_GROUP_DIM), POOL_GROUP_DIM ** -0.5),
        "pool_scale": 1.0 + nrm(ks[6], (DEPTH_2, POOL_WIDTH), 0.02),
        "b_merge": nrm(ks[7], (DEPTH_2, N_BRANCHES * D_MODEL), 0.01),
        "w_proj_a": nrm(ks[8], (DEPTH_2, GLA_DV, D_MODEL), DEEPNORM_BETA * GLA_DV ** -0.5),
        "w_proj_b": nrm(ks[9], (DEPTH_2, POOL_WIDTH, D_MODEL), DEEPNORM_BETA * POOL_WIDTH ** -0.5),
        "w_out": nrm(ks[10], (DEPTH_2, D_MODEL, D_MODEL), DEEPNORM_BETA * D_MODEL ** -0.5),
        "ln_g": 1.0 + nrm(ks[11], (DEPTH_2, D_MODEL), 0.02),
        "ln_b": nrm(ks[12], (DEPTH_2, D_MODEL), 0.01),
    }

def second_block(x, w_in, w_alpha_up, b_alpha, gla_norm_g, w_pool_grp, pool_scale,
              b_merge, w_proj_a, w_proj_b, w_out, ln_g, ln_b):
    for l in range(DEPTH_2):
        x = _layer(x, w_in[l], w_alpha_up[l], b_alpha[l], gla_norm_g[l], w_pool_grp[l],
                   pool_scale[l], b_merge[l], w_proj_a[l], w_proj_b[l], w_out[l],
                   ln_g[l], ln_b[l])
    return x


_first_inputs = second_inputs


def second_inputs(seed=0):
    import zlib

    import numpy as np

    out = dict(_first_inputs(seed))
    spreads = {}
    factors = {'w_alpha_up': 5.955,
     'b_alpha': 64.0,
     'gla_norm_g': 42.717,
     'pool_scale': 46.851,
     'b_merge': 8.0,
     'ln_g': 7.996,
     'ln_b': 16.331}
    for name, (base, spread) in spreads.items():
        noise = np.random.default_rng([zlib.crc32(name.encode()), seed]).standard_normal(out[name].shape)
        drawn = base * np.exp(spread * noise) if base else spread * noise
        out[name] = __import__('jax').numpy.asarray(drawn.astype(out[name].dtype))
    for name, factor in factors.items():
        out[name] = (out[name] * factor).astype(out[name].dtype)
    return out


_narrow_inputs = second_inputs


def second_inputs(seed=0):

    out = dict(_narrow_inputs(seed))
    wider = {'gla_norm_g': 4.54, 'pool_scale': 4.55, 'ln_g': 3.18, 'ln_b': 3.18}
    for name, times in wider.items():
        mean = out[name].mean()
        out[name] = (mean + times * (out[name] - mean)).astype(out[name].dtype)
    return out


def setup_inputs(seed=0):
    out = dict(first_inputs(seed))
    for name, value in second_inputs(seed + 1).items():
        if name != "x":
            out[name + "_2"] = value
    return out


def reference(
    x, mem, positions, mix_norm, mlp_norm, mem_norm, final_norm, w_mem_kv, w_out, w_up, w_down,
    attn_w_in, attn_sinks, lru_w_in, lru_conv_w, lru_conv_b, lru_wa, lru_ba, lru_wx, lru_bx,
    lru_lambda, w_in_2, w_alpha_up_2, b_alpha_2, gla_norm_g_2, w_pool_grp_2, pool_scale_2,
    b_merge_2, w_proj_a_2, w_proj_b_2, w_out_2, ln_g_2, ln_b_2,
):
    x = first_block(
        x, mem, positions, mix_norm, mlp_norm, mem_norm, final_norm, w_mem_kv, w_out, w_up,
        w_down, attn_w_in, attn_sinks, lru_w_in, lru_conv_w, lru_conv_b, lru_wa, lru_ba, lru_wx,
        lru_bx, lru_lambda,
    )
    return second_block(
        x, w_in_2, w_alpha_up_2, b_alpha_2, gla_norm_g_2, w_pool_grp_2, pool_scale_2, b_merge_2,
        w_proj_a_2, w_proj_b_2, w_out_2, ln_g_2, ln_b_2,
    )


_drawn_inputs = setup_inputs


def setup_inputs(seed=0):
    import zlib

    import numpy as np

    out = dict(_drawn_inputs(seed))
    spreads = {}
    factors = {'mem_norm': 4.922, 'attn_sinks': 8.0, 'lru_ba': 28.822, 'lru_bx': 6.35}
    for name, (base, spread) in spreads.items():
        noise = np.random.default_rng([zlib.crc32(name.encode()), seed]).standard_normal(out[name].shape)
        drawn = base * np.exp(spread * noise) if base else spread * noise
        out[name] = __import__('jax').numpy.asarray(drawn.astype(out[name].dtype))
    for name, factor in factors.items():
        out[name] = (out[name] * factor).astype(out[name].dtype)
    return out
```

```python
from contextlib import ExitStack, contextmanager

import numpy as np
import concourse.bass as bass
from concourse import mybir

F32 = mybir.dt.float32
F32R = mybir.dt.float32r
I32 = mybir.dt.int32
ALU = mybir.AluOpType
ACT = mybir.ActivationFunctionType
AX_X = mybir.AxisListType.X

P = 128
D = 1024
S = 1024
KT = D // P
NBLK = S // P
MEM = 256
MEM_HEADS = 4
HEADS = 16
KV = 4
HD = 64
SINK_SCALE = HD ** -0.5
MEM_SCALE = 128 ** -0.5
NEG = -1e30
EPS = 1e-6
EPS_2 = 1e-5
ALPHA = 2.0 ** 0.25
CHUNK = 64
TAU = 16.0
RANK = 16
LEVELS = 6
WINDOWS = (2, 4, 8, 16)

PHASES = []
for _l in range(2):
    PHASES += [(f"mem{_l}", 8, "act"), (f"mq{_l}", 4, "act")]
    PHASES += [("k", 2, "act"), ("v", 2, "act"), ("q", 8, "act")] if _l == 0 else [("lru", 16, "act")]
    PHASES += [(f"wo_mixed{_l}", 8, "dve"), (f"wo_mem{_l}", 8, "dve")]
    for _c in range(4):
        PHASES += [(f"up{_l}{_c}", 8, "act"), (f"down{_l}{_c}", 8, "dve")]
PHASES += [("gla", 24, "act"), ("pool", 8, "act"), ("gate_b", 8, "act"), ("merge", 16, "act"),
           ("proj_a", 8, "dve"), ("proj_b", 8, "dve"), ("out", 8, "dve")]
START, BASE, PREV = {}, {}, {}
_n, _done, _before = 0, {"act": 0, "dve": 0}, None
for _name, _count, _eng in PHASES:
    START[_name], BASE[_name], PREV[_name] = _n, dict(_done), _before
    _n += _count
    _done[_eng] += _count
    _before = _eng
N_JOBS = _n
EVAC = {name: eng for name, _, eng in PHASES}

NORMS = ["nmem0", "nmix0", "nmlp0", "nmem1", "nmix1", "nmlp1", "nfin"]

VCOLS, _at = {}, 0
for _name, _n in (("mix_norm", 16), ("mlp_norm", 16), ("mem_norm", 8), ("final_norm", 8), ("sinks", 16),
                  ("conv_w", 32), ("conv_b", 8), ("lru_ba", 16), ("lru_bx", 16), ("lam", 16),
                  ("b_alpha", 4), ("gla_norm", 8), ("pool_scale", 8), ("b_merge", 16), ("ln_g", 8),
                  ("ln_b", 8)):
    VCOLS[_name] = _at
    _at += _n
N_VEC = _at

CCOLS, _at = {}, 0
for _name, _n in (("ident", 128), ("ones", 128), ("perm", 128), ("dup", 256), ("freq", 1), ("half", 2)):
    CCOLS[_name] = _at
    _at += _n
N_CONST = _at


class Chain:

    def __init__(self, eng, sem):
        self.eng, self.sem, self.turn, self.per, self.n = eng, sem, None, 0, 0

    def link(self, ins):
        ins.then_inc(self.sem, 1)
        self.n += 1
        self.eng.wait_ge(self.sem, self.n if self.turn is None else self.turn * self.per + self.n)

    @contextmanager
    def loop(self, count, per):
        first = self.n
        with self.eng.Fori(0, count) as i:
            self.turn, self.per = i, per
            yield i
            assert self.n == first + per, (self.n - first, per)
        self.turn, self.n = None, first + per * count


def build(nc, xT, memT, pos, wjobs, lru_w, alpha_w, alpha_up, pool_w, vec, const, masks, pair_masks, inv_count,
          scratch, gate_tiles, out):
    with ExitStack() as ctx:
        base = (nc.sbuf_base + 31) // 32 * 32

        def sb(name, shape, dt, at):
            return nc.alloc_sbuf_tensor_at(name, shape, dt, offset=base + at)

        def sem(name):
            return ctx.enter_context(nc.semaphore(name))

        KB = 1024
        X_AT, H_AT, U_AT, W_AT, R_AT = 0, 32 * KB, 96 * KB, 160 * KB, 184 * KB
        X = sb("X", [P, KT, S], F32, X_AT)
        Hhi = sb("Hhi", [P, KT, S], F32R, H_AT)
        Hlo = sb("Hlo", [P, KT, S], F32R, H_AT + 32 * KB)
        Uhi = sb("Uhi", [P, KT, S], F32R, U_AT)
        Ulo = sb("Ulo", [P, KT, S], F32R, U_AT + 32 * KB)
        wraw = sb("wraw", [P, 2, KT, P], F32, W_AT)
        whi = sb("whi", [P, 2, KT, P], F32R, W_AT + 8 * KB)
        wlo = sb("wlo", [P, 2, KT, P], F32R, W_AT + 16 * KB)
        T = sb("T", [P, 2, S], F32, R_AT)
        MK = sb("MK", [P, MEM_HEADS, MEM], F32, R_AT + 8 * KB)
        MV = sb("MV", [P, 2, MEM_HEADS, P], F32, R_AT + 12 * KB)
        vecs = sb("vecs", [P, N_VEC], F32, R_AT + 16 * KB)
        cst = sb("cst", [P, N_CONST], F32, R_AT + 17 * KB)
        stat = sb("stat", [P, 48], F32, R_AT + 19 * KB + 640)
        O_sb = sb("O_sb", [P, 2, P], F32, R_AT + 19 * KB + 832)
        probsT = sb("probsT", [P, 2, 3 * P], F32, R_AT + 20 * KB + 832)
        acc = sb("acc", [P, S], F32, U_AT + 32 * KB)
        squares = sb("squares", [P, 2, S], F32, U_AT + 36 * KB)
        rstd = sb("rstd", [P, S], F32, U_AT + 44 * KB)
        mraw = sb("mraw", [P, KT, MEM], F32, U_AT)
        Mhi = sb("Mhi", [P, KT, MEM], F32R, U_AT + 8 * KB)
        Mlo = sb("Mlo", [P, KT, MEM], F32R, U_AT + 16 * KB)
        mixed = sb("mixed", [P, KT, S], F32, U_AT + 32 * KB)
        mo = sb("mo", [P, MEM_HEADS, S], F32, X_AT)
        MOhi = sb("MOhi", [P, MEM_HEADS, S], F32R, U_AT)
        MOlo = sb("MOlo", [P, MEM_HEADS, S], F32R, U_AT + 16 * KB)
        keys = sb("keys", [P, KV, S + 2 * P], F32, U_AT)
        vals = sb("vals", [P, NBLK + 2, KV * HD], F32, U_AT + 20 * KB)
        cos = sb("cos", [P, S], F32, X_AT + 16 * KB)
        sin = sb("sin", [P, S], F32, X_AT + 20 * KB)
        wmask = sb("wmask", [P, 3, 3 * P], F32, X_AT + 24 * KB)
        probs = sb("probs", [P, 2, 3 * P], F32, X_AT + 29 * KB)
        lw = sb("lw", [P, 2, 4, P], F32, U_AT)
        xb = sb("xb", [P, S + 8], F32, U_AT + 4 * KB)
        xc = [sb("xc0", [P, S], F32, U_AT + 9 * KB), sb("xc1", [P, S], F32, X_AT + 28 * KB)]
        rg = sb("rg", [P, 2, S], F32, U_AT + 13 * KB)
        ig = sb("ig", [P, 2, S], F32, U_AT + 21 * KB)
        decay_c = sb("decay_c", [P, 96], F32, U_AT + 29 * KB)
        av = sb("av", [P, 2, S], F32, X_AT + 16 * KB)
        gl = sb("gl", [P, S], F32, X_AT + 24 * KB)

        gsum = sb("gsum", [P, KV, S], F32, U_AT)
        gq = sb("gq", [P, S], F32, U_AT + 16 * KB)
        gk = sb("gk", [P, S], F32, U_AT + 20 * KB)
        dec = sb("dec", [P, S], F32, U_AT + 24 * KB)
        dq = sb("dq", [P, S], F32, U_AT + 28 * KB)
        dk = sb("dk", [P, S], F32, U_AT + 32 * KB)
        vtok = sb("vtok", [P, NBLK, 2 * P], F32, U_AT + 36 * KB)
        results = sb("results", [P, 2, 2, S // 2], F32, U_AT + 36 * KB)
        ktok = sb("ktok", [P, NBLK, P], F32, U_AT + 44 * KB)
        wts = sb("wts", [P, NBLK, P], F32, U_AT + 48 * KB)
        state = sb("state", [P, 2, 2 * P], F32, U_AT + 52 * KB)
        pmask = sb("pmask", [P, LEVELS + 1, P], I32, U_AT + 54 * KB)
        chunk_decay = sb("chunk_decay", [P, S // CHUNK], F32, U_AT + 57 * KB + 512)
        alow_w = sb("alow_w", [P, KT, RANK], F32, U_AT + 58 * KB)
        aup_w = sb("aup_w", [RANK, KV * P], F32, U_AT + 59 * KB)
        alow = sb("alow", [RANK, S], F32, U_AT + 28 * KB)
        starts = sb("starts", [P, S], F32, U_AT + 24 * KB)
        ya = sb("ya", [P, KT, S], F32, X_AT)
        yb = sb("yb", [P, KT, S], F32, U_AT + 32 * KB)
        unit = sb("unit", [P, S], F32, U_AT)
        csum = sb("csum", [P, 16 + S], F32, U_AT + 4 * KB)
        pooled = sb("pooled", [P, 2, S], F32, U_AT + 9 * KB)
        pool_m = sb("pool_m", [P, 2, 2 * P], F32, U_AT + 17 * KB)
        inv_cnt = sb("inv_cnt", [P, KV, 16], F32, U_AT + 19 * KB)
        X2 = sb("X2", [P, KT, S], F32, H_AT)

        G = ctx.enter_context(nc.psum_tensor("G", [P, 2, S], F32))
        AUX = ctx.enter_context(nc.psum_tensor("AUX", [P, 4, 512], F32))
        ident = cst[:, CCOLS["ident"]:CCOLS["ident"] + P]
        ones = cst[:, CCOLS["ones"]:CCOLS["ones"] + P]
        perm = cst[:, CCOLS["perm"]:CCOLS["perm"] + P]
        freq = cst[:, CCOLS["freq"]:CCOLS["freq"] + 1]

        def vcol(name, i):
            return vecs[:, VCOLS[name] + i:VCOLS[name] + i + 1]

        def dcol(name, i, width=1):
            return vecs[:, bass.ds(VCOLS[name] + i, width)]

        w_loaded = [sem("w_loaded0"), sem("w_loaded1")]
        w_hi = sem("w_hi")
        w_split = sem("w_split")
        job_done = sem("job_done")
        evac = {"act": sem("evac_act"), "dve": sem("evac_dve")}
        act_chain, dve_chain, pool_chain = sem("act_chain"), sem("dve_chain"), sem("pool_chain")
        tables = sem("tables")
        x_loaded = sem("x_loaded")
        x_back = [sem("x_back0"), sem("x_back1")]
        x_saved = sem("x_saved")
        mem_in = [sem("mem_in0"), sem("mem_in1")]
        pos_in, masks_in, pads = sem("pos_in"), sem("masks_in"), sem("pads")
        out_done = sem("out_done")

        norm_s = {k: sem(f"norm_{k}") for k in ("sq", "acc", "ssq", "var", "r", "t", "hi", "lo")}

        def attn_sems(name):
            return {k: sem(f"{name}_{k}") for k in ("sc", "mx", "pr", "pt", "pc", "pv", "os", "ot", "oc")}

        attns = {n: attn_sems(n) for n in ("am", "aw")}
        mvt, mvc = [sem("mvt0"), sem("mvt1")], [sem("mvc0"), sem("mvc1")]
        trig, rot_sw, rot_ok = sem("trig"), sem("rot_sw"), sem("rot_ok")
        kdup, kcopied, vt, vcopied = sem("kdup"), sem("kcopied"), sem("vt"), sem("vcopied")
        split_hi, split_lo = [sem("split_hi0"), sem("split_hi1")], [sem("split_lo0"), sem("split_lo1")]
        up_hi, up_lo, up_sq = [sem("up_hi0"), sem("up_hi1")], [sem("up_lo0"), sem("up_lo1")], [sem("up_sq0"), sem("up_sq1")]
        lw_in = [sem("lw_in0"), sem("lw_in1")]
        l_dec, l_xc, l_mm, l_sig, l_exp, l_a2, l_e, l_sq, l_ix, l_h, l_sum, l_y = (
            sem("l_" + k) for k in ("dec", "xc", "mm", "sig", "exp", "a2", "e", "sq", "ix", "h", "sum", "y"))
        l_dx, l_de = sem("l_dx"), sem("l_de")
        g_in, g_low, g_lowc, g_z, g_abs, g_min, g_zero = (sem("g_" + k) for k in ("in", "low", "lowc", "z", "abs", "min", "zero"))
        g_diff, g_exp, g_dq, g_dk, g_w, g_keep = (sem("g_" + k) for k in ("diff", "exp", "dq", "dk", "w", "keep"))
        g_vt, g_vc, g_kt, g_kc, g_up, g_st, g_o, g_oc = (sem("g_" + k) for k in ("vt", "vc", "kt", "kc", "up", "st", "o", "oc"))
        g_s0 = sem("g_s0")
        g_cd, g_sq, g_ss, g_ssq, g_var, g_r, g_y = (sem("g_" + k) for k in ("cd", "sq", "ss", "ssq", "var", "r", "y"))
        p_in, p_m, p_pool, p_mm, p_used = sem("p_in"), sem("p_m"), sem("p_pool"), sem("p_mm"), sem("p_used")
        b_gate, b_y = sem("b_gate"), sem("b_y")
        gates_out, gates_in = [sem("gates_out0"), sem("gates_out1")], [sem("gates_in0"), sem("gates_in1")]
        s_hi, s_lo, merged = sem("s_hi"), sem("s_lo"), sem("merged")
        x2_saved, x2_back = sem("x2_saved"), sem("x2_back")
        n_sum, n_mean, n_cent, n_sq, n_acc, n_ssq, n_var, n_r, n_y = (
            sem("n_" + k) for k in ("sum", "mean", "cent", "sq", "acc", "ssq", "var", "r", "y"))

        stood = {nc.scalar: sem("act_stood"), nc.vector: sem("dve_stood"), nc.gpsimd: sem("pool_stood")}

        def wait_apart(eng, semaphore, value):
            eng.wait_ge(semaphore, value)
            eng.sem_inc(stood[eng], 1)

        def scored(par, u, width):
            return G[:, par, 0:width] if u % 3 == 2 else AUX[:, u % 3, 0:width]

        block = ctx.enter_context(nc.Block())

        @block.sync
        def _(sp):
            for par in range(2):
                sp.dma_start(wraw[:, par], wjobs[par]).then_inc(w_loaded[par], 16)
            with sp.Fori(1, N_JOBS // 2) as i:
                for par in range(2):
                    sp.wait_ge(w_split, i * 2 + (par - 1))
                    sp.dma_start(wraw[:, par], wjobs[bass.ds(i * 2 + par, 1)].rearrange("a p n -> (a p) n"))\
                      .then_inc(w_loaded[par], 16)

        @block.gpsimd
        def _(pool):
            def split(n, i, par, started):
                pool.wait_ge(w_loaded[par], i * 16 + 16)
                if started:
                    wait_apart(pool, job_done, n - 1)
                pool.tensor_copy(whi[:, par], wraw[:, par]).then_inc(w_hi, 1)
                pool.wait_ge(w_hi, n + 1)
                pool.tensor_tensor(wlo[:, par], wraw[:, par], whi[:, par], ALU.subtract).then_inc(w_split, 1)

            def splits(first, last):
                with pool.Fori(first // 2, last // 2) as i:
                    for par in range(2):
                        split(i * 2 + par, i, par, True)

            for par in range(2):
                split(par, 0, par, False)
            splits(2, START["k"])
            pool.wait_ge(job_done, START["mem0"] + 8)
            pool.memset(keys[:, :, 0:P], 0.0)
            pool.memset(keys[:, :, S + P:S + 2 * P], 0.0)
            pool.memset(vals[:, 0, :], 0.0)
            pool.memset(vals[:, NBLK + 1, :], 0.0).then_inc(pads, 1)
            splits(START["k"], START["lru"] + 4)
            pool.memset(xb[:, 0:1], 0.0)
            pool.memset(xb[:, S + 1:S + 3], 0.0).then_inc(pads, 1)

            def lru_block(j, par, last=False):
                if not last:
                    split(j * 2 + (START["lru"] + 4), j + (START["lru"] // 2 + 2), 0, True)
                for dr in range(2):
                    pool.wait_ge(l_sig, j * 4 + (2 * dr + 2))
                    pool.tensor_tensor(ig[:, dr], ig[:, dr], xc[par][:], ALU.mult).then_inc(l_ix, 1)
                for dr in range(2):
                    pool.wait_ge(l_exp, j * 4 + (2 * dr + 2))
                    pool.tensor_tensor(T[:, dr], av[:, dr], av[:, dr], ALU.mult).then_inc(l_a2, 1)
                if not last:
                    split(j * 2 + (START["lru"] + 5), j + (START["lru"] // 2 + 2), 1, True)

            with pool.Fori(0, 3) as i:
                for par in range(2):
                    lru_block(i * 2 + par, par)
            lru_block(6, 0)
            lru_block(7, 1, last=True)
            splits(START["wo_mixed1"] + 2, START["gla"] + 4)
            with pool.Fori(0, KV) as h:
                def decayed(step, n):
                    pool.wait_ge(g_exp, h * 8 + step)
                    if n:
                        pool.wait_ge(g_w, h * 7 + (6 if step == 8 else step))
                    pool.tensor_tensor(dq[:], gq[:], dec[:], ALU.mult).then_inc(g_dq, 1)

                for n in (1, 2, -4, 3, -5, 4, 5, -6, 6, -7, 8, -8, -9):
                    if n > 0:
                        decayed(n, True)
                    else:
                        split(h * 6 + (START["gla"] - n), h * 3 + (START["gla"] // 2 + -n // 2), -n % 2, True)
            splits(START["gla"] + 28, N_JOBS)

        @block.tensor
        def _(pe):
            def psum_waits(name, l, par, own=None, other=None):
                e = EVAC[name]
                pe.wait_ge(evac[e], l + (1 + (BASE[name][e] if own is None else 0)) if own is None else own + l + 1)
                if PREV[name] not in (None, e):
                    o = PREV[name]
                    pe.wait_ge(evac[o], (2 + BASE[name][o] if other is None else other + 2) - (par == 0))

            def job_part(q, n, par, hi, lo, ready, kt=KT, width=S):
                half = min(width, 512)
                halves = width // half
                k, c = q // halves, q % halves
                if q == 0:
                    pe.wait_ge(w_split, n + 1)
                if c == 0 and ready is not None:
                    pe.wait_ge(ready[0], ready[1] + (k + 1))
                cols = slice(c * half, (c + 1) * half)
                for j, (w, x) in enumerate(((whi, hi), (whi, lo), (wlo, hi))):
                    mm = pe.matmul(G[:, par, cols], w[:, par, k, :], x[:, k, cols],
                                   start=(k == 0 and j == 0), stop=(k == kt - 1 and j == 2))
                if q == kt * halves - 1:
                    mm.then_inc(job_done, 1)

            def job(n, par, hi, lo, ready, kt=KT, width=S):
                for q in range(kt * (width // min(width, 512))):
                    job_part(q, n, par, hi, lo, ready, kt, width)

            def next_part(q, n, par, shift):
                if q == 0:
                    pe.wait_ge(evac["act"], n + shift)
                job_part(q, n, par, Hhi, Hlo, None)

            def jobs(name, count, hi, lo, ready, after=None, **kw):
                with pe.Fori(0, count // 2) as i:
                    for par in range(2):
                        psum_waits(name, i * 2 + par, par)
                        job(i * 2 + (START[name] + par), par, hi, lo, ready, **kw)
                        if after:
                            after(i, par)

            def sum_squares(name, width):
                r = NORMS.index(name)
                pe.wait_ge(norm_s["acc"], KT * r + KT)
                half = min(width, 512)
                for c in range(width // half):
                    mm = pe.matmul(AUX[:, c, 0:half], ones, acc[:, c * half:(c + 1) * half], start=True, stop=True)
                mm.then_inc(norm_s["ssq"], 1)

            def mem_phase(l):
                sum_squares(f"nmem{l}", MEM)
                ready = (norm_s["lo"], KT * NORMS.index(f"nmem{l}"))
                name = f"mem{l}"
                for half in range(2):
                    with pe.Fori(0, 2) as i:
                        for par in range(2):
                            psum_waits(name, i * 2 + (4 * half + par), par)
                            job(i * 2 + (START[name] + 4 * half + par), par, Mhi, Mlo, ready, width=MEM)
                            if half:
                                pe.wait_ge(evac["act"], i * 2 + (2 + BASE[name]["act"] + 5 + par))
                                if par:
                                    pe.wait_ge(mvc[l], i * 2 + 1)
                                for t in range(2):
                                    tr = pe.transpose(AUX[:, 2, t * P:(t + 1) * P], T[:, par, t * P:(t + 1) * P], ident)
                                tr.then_inc(mvt[l], 1)
                                pe.wait_ge(mvc[l], i * 2 + (1 + par))

            def attention(s, i, par, subs, nk, kop, vop, between):
                U = NBLK * subs
                dim = P // subs

                def scores(u):
                    b, h = u // subs, u % subs
                    if u >= 3:
                        pe.wait_ge(s["pr"], i * U + (u - 2))
                    pe.matmul(scored(par, u, nk * P), T[:, h, b * P:(b + 1) * P], kop(b),
                              start=True, stop=True).then_inc(s["sc"], 1)

                def turn(u):
                    pe.wait_ge(s["pr"], i * U + (u + 1))
                    if u:
                        pe.wait_ge(s["pc"], i * U + u)
                    for t in range(nk):
                        tr = pe.transpose(AUX[:, 2, t * P:(t + 1) * P], probs[:, u % 2, t * P:(t + 1) * P], ident)
                    tr.then_inc(s["pt"], 1)

                def weigh(u):
                    b, h = u // subs, u % subs
                    pe.wait_ge(s["pc"], i * U + (u + 1))
                    if u:
                        pe.wait_ge(s["os"], i * U + u)
                    for t in range(nk):
                        mm = pe.matmul(AUX[:, 3, 0:dim], probsT[:, u % 2, t * P:(t + 1) * P],
                                       vop(b, t), start=(t == 0), stop=(t == nk - 1))
                    mm.then_inc(s["pv"], 1)

                def turn_result(b):
                    pe.wait_ge(s["os"], i * U + (b + 1) * subs)
                    if b:
                        pe.wait_ge(s["oc"], i * NBLK + b)
                    pe.transpose(G[:, par, 512:512 + P], O_sb[:, b % 2, :], ident).then_inc(s["ot"], 1)

                scores(0)
                scores(1)
                for u in range(U):
                    if u + 2 < U:
                        scores(u + 2)
                    between(u)
                    turn(u)
                    if u >= 2 and (u - 1) % subs == 0:
                        turn_result((u - 2) // subs)
                    if u:
                        weigh(u - 1)
                if (U - 2) % subs == subs - 1:
                    turn_result((U - 2) // subs)
                weigh(U - 1)
                turn_result(NBLK - 1)

            def mem_attention(l):
                s, name = attns["am"], f"mq{l}"
                shift = 1 + BASE[name]["act"] - START[name]
                psum_waits(name, 0, 0)
                job(START[name], 0, Hhi, Hlo, (norm_s["lo"], KT * NORMS.index(f"nmix{l}")))
                with pe.Fori(0, 2) as i:
                    for par in range(2):
                        head = i * 2 + par
                        after = head + (START[name] + 1)
                        pe.wait_ge(evac["act"], i * 2 + (3 + BASE[name]["act"] + par))
                        next_part(0, after, 1 - par, shift)
                        next_part(1, after, 1 - par, shift)

                        def between(u):
                            for q in range(2 + 2 * u, min(4 + 2 * u, 16)):
                                next_part(q, after, 1 - par, shift)

                        attention(s, head + MEM_HEADS * l, par, 1, 2,
                                  lambda b: MK[:, bass.ds(head, 1), :].rearrange("p a n -> p (a n)"),
                                  lambda b, t: MV[:, t, bass.ds(head, 1), :].rearrange("p a n -> p (a n)"), between)

            def rotate(r, e, between):
                pe.wait_ge(evac["act"], e)
                for c in range(2):
                    mm = pe.matmul(AUX[:, c, :], perm, T[:, 0, c * 512:(c + 1) * 512], start=True, stop=True)
                mm.then_inc(rot_sw, 1)
                between()
                pe.wait_ge(rot_ok, r + 1)

            def window():
                shift = 1 + BASE["k"]["act"] - START["k"]
                for par in range(2):
                    after = START["k"] + par + 1

                    def between():
                        for q in range(16):
                            next_part(q, after, 1 - par, shift)

                    rotate(par, 3 + BASE["k"]["act"] + par, between)
                    for h in range(2):
                        if h:
                            pe.wait_ge(kcopied, 2 * par + h)
                        at = CCOLS["dup"] + h * P
                        for c in range(2):
                            mm = pe.matmul(AUX[:, c, :], cst[:, at:at + P], T[:, 0, c * 512:(c + 1) * 512],
                                           start=True, stop=True)
                        mm.then_inc(kdup, 1)
                    pe.wait_ge(kcopied, 2 * par + 2)
                for par in range(2):
                    for q in range(16):
                        next_part(q, START["v"] + par + 1, 1 - par, shift)
                    pe.wait_ge(evac["act"], 3 + BASE["v"]["act"] + par)
                    if par:
                        pe.wait_ge(vcopied, 1)
                    for b in range(NBLK):
                        at = (b % 4) * P
                        tr = pe.transpose(AUX[:, b // 4, at:at + P], T[:, 0, b * P:(b + 1) * P], ident)
                    tr.then_inc(vt, 1)
                pe.wait_ge(vcopied, 2)
                pe.wait_ge(pads, 1)

                def tile(g, par, last=False):
                    p = g * 2 + par
                    after = p + (START["q"] + 1)

                    def turning():
                        if not last:
                            for q in range(6):
                                next_part(q, after, 1 - par, shift)

                    def between(u):
                        if not last and 1 <= u <= 10:
                            next_part(5 + u, after, 1 - par, shift)

                    rotate(p + 2, p + (3 + BASE["q"]["act"]), turning)
                    attention(attns["aw"], p, par, 2, 3,
                              lambda b: keys[:, bass.ds(g, 1), b * P:(b + 3) * P].rearrange("p a n -> p (a n)"),
                              lambda b, t: vals[:, b + t, bass.ds(g * HD, HD)], between)

                with pe.Fori(0, KV - 1) as g:
                    for par in range(2):
                        tile(g, par)
                for par in range(2):
                    tile(KV - 1, par, last=(par == 1))

            def project_out(l):
                jobs(f"wo_mixed{l}", 8, Hhi, Hlo, (split_lo[l], 0))
                jobs(f"wo_mem{l}", 8, MOhi, MOlo, (split_lo[l], 8), kt=4)

            def mlp(l):
                sum_squares(f"nmlp{l}", S)
                n0, a0, d0 = START[f"up{l}0"], BASE[f"up{l}0"]["act"], BASE[f"up{l}0"]["dve"]
                with pe.Fori(0, 4) as c:
                    with pe.Fori(0, 4) as i:
                        for par in range(2):
                            pe.wait_ge(evac["act"], c * 8 + i * 2 + (a0 + par + 1))
                            pe.wait_ge(evac["dve"], c * 8 + (d0 + 2 - (par == 0)))
                            job(c * 16 + i * 2 + (n0 + par), par, Hhi, Hlo, (norm_s["lo"], KT * NORMS.index(f"nmlp{l}")))
                    with pe.Fori(0, 4) as i:
                        for par in range(2):
                            pe.wait_ge(evac["dve"], c * 8 + i * 2 + (d0 + par + 1))
                            pe.wait_ge(evac["act"], c * 8 + (a0 + 8 + 2 - (par == 0)))
                            job(c * 16 + i * 2 + (n0 + 8 + par), par, Uhi, Ulo, (up_lo[l], c * 8))

            def lru():
                pe.wait_ge(attns["am"]["oc"], 2 * MEM_HEADS * NBLK)
                shift = 1 + BASE["lru"]["act"] - START["lru"]

                def gates(par, dr):
                    for g in range(2):
                        for c in range(2):
                            mm = pe.matmul(AUX[:, 2 * g + c, :], lw[:, par, 2 * dr + g, :], xc[par][:, c * 512:(c + 1) * 512],
                                           start=True, stop=True)
                    mm.then_inc(l_mm, 1)

                def first_gates(j, lw_count, par):
                    pe.wait_ge(l_xc, j + 1)
                    pe.wait_ge(lw_in[par], lw_count * 16 + 16)
                    gates(par, 0)

                def block_of(j, i, par):
                    pe.wait_ge(l_sig, j * 4 + 2)
                    gates(par, 1)
                    for q in range(16):
                        next_part(q, j * 2 + (START["lru"] + 3), 1, shift)
                    if not (isinstance(j, int) and j == 6):
                        for q in range(16):
                            next_part(q, j * 2 + (START["lru"] + 4), 0, shift)
                    pe.wait_ge(l_sig, j * 4 + 4)
                    first_gates(j + 1, i + par, 1 - par)

                for n in (1, 2):
                    for q in range(16):
                        next_part(q, START["lru"] + n, n % 2, shift)
                first_gates(0, 0, 0)
                with pe.Fori(0, 3) as i:
                    for par in range(2):
                        block_of(i * 2 + par, i, par)
                block_of(6, 3, 0)
                pe.wait_ge(l_sig, 30)
                gates(1, 1)

            def gla():
                pe.wait_ge(g_in, 48)
                pe.wait_ge(norm_s["lo"], KT * NORMS.index("nfin") + KT)
                for c in range(2):
                    for k in range(KT):
                        mm = pe.matmul(AUX[0:RANK, c, :], alow_w[:, k, :], X[:, k, c * 512:(c + 1) * 512],
                                       start=(k == 0), stop=(k == KT - 1))
                mm.then_inc(g_low, 1)
                pe.wait_ge(g_lowc, 1)
                for h in range(KV):
                    for c in range(2):
                        if h >= 2 and c == 0:
                            pe.wait_ge(g_abs, h - 1)
                            pe.wait_ge(g_min, h - 1)
                        mm = pe.matmul(AUX[:, 2 * (h % 2) + c, :], aup_w[:, h * P:(h + 1) * P], alow[:, c * 512:(c + 1) * 512],
                                       start=True, stop=True)
                    mm.then_inc(g_z, 1)
                pe.wait_ge(g_abs, KV)
                pe.wait_ge(g_min, KV)
                a0 = BASE["gla"]["act"]
                shift = 1 + a0 - START["gla"]

                def head(h, last=False):

                    def weights(step):
                        if step:
                            pe.wait_ge(g_dq, h * 7 + step)
                            pe.wait_ge(g_dk, h * 7 + step)
                            pe.wait_ge(g_keep, h * 7 + step)
                            q, k = dq, dk
                        else:
                            pe.wait_ge(evac["act"], h * 6 + (a0 + 4))
                            q, k = gq, gk
                        for b in range(NBLK):
                            cols = slice(b * P, (b + 1) * P)
                            mm = pe.matmul(AUX[:, b // 4, (b % 4) * P:(b % 4 + 1) * P], k[:, cols], q[:, cols],
                                           start=True, stop=True)
                        mm.then_inc(g_w, 1)

                    def turn_values(n):
                        pe.wait_ge(evac["act"], h * 6 + (a0 + 5 + n))
                        if n:
                            pe.wait_ge(g_vc, h * 2 + 1)
                        for b in range(NBLK):
                            tr = pe.transpose(AUX[:, 2 + b // 4, (b % 4) * P:(b % 4 + 1) * P], T[:, n, b * P:(b + 1) * P], ident)
                        tr.then_inc(g_vt, 1)

                    weights(0)
                    for q in range(64):
                        next_part(q % 16, h * 6 + (START["gla"] + 2 + q // 16), q // 16 % 2, shift)
                        if q + 1 in (11, 22, 33, 44, 54):
                            weights((q + 1) // 11 if q + 1 < 54 else 5)
                        if q + 1 == 24:
                            turn_values(0)
                        if q + 1 == 40:
                            turn_values(1)
                    weights(6)
                    pe.wait_ge(g_dk, h * 7 + 7)
                    pe.wait_ge(g_vc, h * 2 + 2)
                    for b in range(NBLK):
                        tr = pe.transpose(AUX[:, 2 + b // 4, (b % 4) * P:(b % 4 + 1) * P], dk[:, b * P:(b + 1) * P], ident)
                    tr.then_inc(g_kt, 1)
                    pe.wait_ge(g_kc, h + 1)
                    pe.wait_ge(g_keep, h * 7 + 7)
                    pe.wait_ge(g_dq, h * 7 + 7)
                    for c in range(S // CHUNK):
                        b, rows = c // 2, slice((c % 2) * CHUNK, (c % 2 + 1) * CHUNK)
                        if not last:
                            for q in range(2 * c, 2 * c + 2):
                                next_part(q % 16, h * 6 + (START["gla"] + 6 + q // 16), q // 16, shift)
                        if c >= 2:
                            pe.wait_ge(g_st, h * 16 + (c - 1))
                        pe.matmul(AUX[:, c % 2, 0:2 * P], ktok[rows, b, :], vtok[rows, b, :], start=True, stop=True)\
                          .then_inc(g_up, 1)
                        if c == 8:
                            pe.wait_ge(g_oc, h * 4 + 2)
                        at = (b % 4) * P
                        for d in range(2):
                            if c % 2 == 0:
                                pe.matmul(AUX[:, 2 + d, at:at + P], vtok[:, b, d * P:(d + 1) * P], wts[:, b, :],
                                          start=True, stop=False)
                            if d == 0 and c == 0:
                                pe.wait_ge(g_s0, h + 1)
                            elif d == 0:
                                pe.wait_ge(g_st, h * 16 + c)
                            mm = pe.matmul(AUX[:, 2 + d, at + (c % 2) * CHUNK:at + (c % 2 + 1) * CHUNK],
                                           state[:, c % 2, d * P:(d + 1) * P], dq[:, c * CHUNK:(c + 1) * CHUNK],
                                           start=False, stop=(c % 2 == 1))
                        if c % 8 == 7:
                            mm.then_inc(g_o, 1)
                    pe.wait_ge(g_st, h * 16 + 16)
                    pe.wait_ge(g_ss, h + 1)
                    for c in range(2):
                        mm = pe.matmul(AUX[:, c, :], ones, T[:, 0, c * 512:(c + 1) * 512], start=True, stop=True)
                    mm.then_inc(g_ssq, 1)
                    pe.wait_ge(g_var, h + 1)

                for n in range(2):
                    psum_waits("gla", n, n)
                    job(START["gla"] + n, n, Hhi, Hlo, None)
                with pe.Fori(0, KV - 1) as h:
                    head(h)
                head(KV - 1, last=True)

            def pool_group(g, par):
                if par == 0:
                    return
                pe.wait_ge(p_pool, g * 2 + 2)
                pe.wait_ge(p_m, g * 16 + 16)
                for m in range(2):
                    for c in range(2):
                        for k in range(2):
                            mm = pe.matmul(AUX[:, 2 * m + c, :], pool_m[:, k, m * P:(m + 1) * P],
                                           pooled[:, k, c * 512:(c + 1) * 512], start=(k == 0), stop=(k == 1))
                mm.then_inc(p_mm, 1)
                pe.wait_ge(p_used, g * 2 + 2)

            pe.wait_ge(tables, 32)
            mem_phase(0)
            sum_squares("nmix0", S)
            mem_attention(0)
            window()
            project_out(0)
            mlp(0)
            mem_phase(1)
            sum_squares("nmix1", S)
            mem_attention(1)
            lru()
            project_out(1)
            mlp(1)
            sum_squares("nfin", S)
            gla()
            jobs("pool", 8, Hhi, Hlo, None, after=pool_group)
            jobs("gate_b", 8, Hhi, Hlo, None)
            jobs("merge", 16, Hhi, Hlo, None)
            jobs("proj_a", 8, Hhi, Hlo, (s_lo, 0))
            jobs("proj_b", 8, Hhi, Hlo, (s_lo, 8))
            jobs("out", 8, Uhi, Ulo, (s_lo, 16))
            for src, done, out_sem in ((acc, n_sum, n_mean), (acc, n_acc, n_ssq)):
                pe.wait_ge(done, KT)
                for c in range(2):
                    mm = pe.matmul(AUX[:, c, :], ones, src[:, c * 512:(c + 1) * 512], start=True, stop=True)
                mm.then_inc(out_sem, 1)

        @block.scalar
        def _(act):
            chain = Chain(act, act_chain)
            act.dma_start(vecs[:], vec).then_inc(tables, 16)
            act.dma_start(cst[:], const).then_inc(tables, 16)
            act.dma_start(mraw[:], memT).then_inc(mem_in[0], 16)
            act.dma_start(X[:], xT).then_inc(x_loaded, 16)
            act.nop().then_inc(evac["act"], 2)
            act.wait_ge(tables, 32)

            def norm(name, src, hi, width):
                s, r = norm_s, NORMS.index(name)
                for k in range(KT):
                    if k >= 2:
                        act.wait_ge(s["acc"], KT * r + k - 1)
                    act.activation(squares[:, k % 2, 0:width], src[:, k, :], ACT.Square).then_inc(s["sq"], 1)
                act.wait_ge(s["var"], r + 1)
                act.activation(rstd[:, 0:width], rstd[:, 0:width], ACT.Sqrt).then_inc(s["r"], 1)
                for k in range(KT):
                    act.wait_ge(s["t"], KT * r + k + 1)
                    act.copy(hi[:, k, :], T[:, k % 2, 0:width]).then_inc(s["hi"], 1)

            def empty(n, par, dst, width=S):
                wait_apart(act, job_done, n + 1)
                act.copy(dst, G[:, par, 0:width]).then_inc(evac["act"], 1)

            def mem_phase(l):
                act.wait_ge(mem_in[l], 16)
                norm(f"nmem{l}", mraw, Mhi, MEM)
                name = f"mem{l}"
                with act.Fori(0, 2) as i:
                    for par in range(2):
                        empty(i * 2 + (START[name] + par), par,
                              MK[:, bass.ds(i * 2 + par, 1), :].rearrange("p a n -> p (a n)"), MEM)
                with act.Fori(0, 2) as i:
                    for par in range(2):
                        empty(i * 2 + (START[name] + 4 + par), par, T[:, par, 0:MEM], MEM)

            def attention(s, i, par, subs, nk, dst, scale, sink=None):
                U = NBLK * subs

                def exp(u):
                    if u >= 2:
                        act.wait_ge(s["pt"], i * U + (u - 1))
                    if u >= 4:
                        act.wait_ge(s["os"], i * U + (u - 3))
                    wait_apart(act, s["mx"], i * U + (u + 1))
                    t = u % 4
                    negm = stat[:, 4 + t:5 + t]
                    if sink:
                        act.activation(stat[:, 12 + t:13 + t], sink(u % subs), ACT.Exp, bias=negm)
                        src = probs[:, u % 2, :]
                    else:
                        src = scored(par, u, nk * P)
                    act.activation(probs[:, u % 2, 0:nk * P], src, ACT.Exp, bias=negm, scale=scale,
                                   accum_out=stat[:, 8 + t:9 + t]).then_inc(s["pr"], 1)

                def copies(u):
                    act.wait_ge(s["pt"], i * U + (u + 1))
                    if u >= 2:
                        act.wait_ge(s["pv"], i * U + (u - 1))
                    act.copy(probsT[:, u % 2, 0:nk * P], AUX[:, 2, 0:nk * P]).then_inc(s["pc"], 1)

                def result(b):
                    wait_apart(act, s["ot"], i * NBLK + (b + 1))
                    act.copy(dst(b), G[:, par, 512:512 + P]).then_inc(s["oc"], 1)

                exp(0)
                for u in range(U):
                    if u + 1 < U:
                        exp(u + 1)
                    copies(u)
                    if u >= 2 and (u - 1) % subs == 0:
                        result((u - 2) // subs)
                if (U - 2) % subs == subs - 1:
                    result((U - 2) // subs)
                result(NBLK - 1)

            def mem_attention(l):
                name = f"mq{l}"
                with act.Fori(0, 2) as i:
                    for par in range(2):
                        head = i * 2 + par
                        empty(i * 2 + (START[name] + par), par, T[:, 0, :])
                        attention(attns["am"], head + MEM_HEADS * l, par, 1, 2,
                                  lambda b: mo[:, bass.ds(head, 1), b * P:(b + 1) * P].rearrange("p a n -> p (a n)"),
                                  MEM_SCALE)

            def window():
                for n, t in enumerate((sin, cos)):
                    act.wait_ge(trig, n + 1)
                    chain.link(act.activation(t[:], t[:], ACT.Sin))
                for par in range(2):
                    empty(START["k"] + par, par, T[:, 0, :])
                    for h in range(2):
                        act.wait_ge(kdup, 2 * par + h + 1)
                        act.copy(keys[:, 2 * par + h, P:P + S], AUX[:, 0:2, :].rearrange("p a n -> p (a n)"))\
                           .then_inc(kcopied, 1)
                for par in range(2):
                    if par:
                        act.wait_ge(vt, par)
                    empty(START["v"] + par, par, T[:, 0, :])
                act.wait_ge(vt, 2)
                with act.Fori(0, KV) as g:
                    for par in range(2):
                        empty(g * 2 + (START["q"] + par), par, T[:, 0, :])
                        attention(attns["aw"], g * 2 + par, par, 2, 3,
                                  lambda b: mixed[:, bass.ds(g * 2 + par, 1), b * P:(b + 1) * P].rearrange("p a n -> p (a n)"),
                                  SINK_SCALE, lambda h: dcol("sinks", g * 4 + (2 * par + h)))

            def project_out(l):
                if l == 0:
                    act.wait_ge(attns["aw"]["oc"], KT * NBLK)
                act.wait_ge(attns["am"]["oc"], (l + 1) * MEM_HEADS * NBLK)
                for k in range(KT):
                    act.copy(Hhi[:, k, :], mixed[:, k, :]).then_inc(split_hi[l], 1)
                for k in range(MEM_HEADS):
                    act.copy(MOhi[:, k, :], mo[:, k, :]).then_inc(split_hi[l], 1)
                act.wait_ge(split_lo[l], KT + MEM_HEADS)
                act.dma_start(X[:], xT if l == 0 else scratch[0]).then_inc(x_back[l], 16)

            def mlp(l):
                act.wait_ge(evac["dve"], 2 + BASE[f"up{l}0"]["dve"])
                norm(f"nmlp{l}", X, Hhi, S)
                n0 = START[f"up{l}0"]
                with act.Fori(0, 4) as c:
                    with act.Fori(0, 4) as i:
                        for par in range(2):
                            n = c * 8 + i * 2 + par
                            act.wait_ge(job_done, c * 16 + i * 2 + (n0 + par + 1))
                            if par == 0:
                                act.wait_ge(up_lo[l], n)
                            act.activation(T[:, par, :], G[:, par, :], ACT.Relu).then_inc(evac["act"], 1)
                            wait_apart(act, evac["act"], c * 8 + i * 2 + (3 + BASE[f"up{l}0"]["act"] + par))
                            act.activation(Uhi[:, bass.ds(i * 2 + par, 1), :].rearrange("p a n -> p (a n)"), T[:, par, :],
                                           ACT.Square).then_inc(up_hi[l], 1)

            def lru():
                act.wait_ge(l_dec, 1)
                act.activation(decay_c[:, 16:32], decay_c[:, 0:16], ACT.Exp, scale=-1.0).then_inc(l_de, 1)
                def input_of(j, par):
                    wait_apart(act, job_done, j * 2 + (START["lru"] + 1))
                    act.copy(xb[:, 1:S + 1], G[:, 0, :]).then_inc(evac["act"], 1)
                    block = lru_w[j] if isinstance(j, int) else lru_w[bass.ds(j, 1)].rearrange("a p g n -> (a p) g n")
                    act.dma_start(lw[:, par], block).then_inc(lw_in[par], 16)

                def block_of(j, par, last=False):
                    wait_apart(act, job_done, j * 2 + (START["lru"] + 2))
                    act.activation(gl[:], G[:, 1, :], ACT.Gelu_apprx_tanh).then_inc(evac["act"], 1)
                    for dr in range(2):
                        wait_apart(act, l_mm, j * 2 + (dr + 1))
                        for g, (dst, b) in enumerate(((rg, "lru_ba"), (ig, "lru_bx"))):
                            act.activation(dst[:, dr], AUX[:, 2 * g:2 * g + 2, :].rearrange("p a n -> p (a n)"),
                                           ACT.Sigmoid, bias=dcol(b, j + 8 * dr)).then_inc(l_sig, 1)
                    if not last:
                        input_of(j + 1, 1 - par)
                    wait_apart(act, l_sig, j * 4 + 4)
                    for dr in range(2):
                        c = decay_c[:, bass.ds(j + (80 + 8 * dr), 1)]
                        act.activation(av[:, dr], rg[:, dr], ACT.Exp, scale=c).then_inc(l_exp, 1)
                        act.activation(rg[:, dr], rg[:, dr], ACT.Tanh, scale=c).then_inc(l_exp, 1)
                    for dr in range(2):
                        act.wait_ge(l_e, j * 2 + (dr + 1))
                        act.activation(T[:, dr], T[:, dr], ACT.Sqrt, scale=-1.0).then_inc(l_sq, 1)
                    act.wait_ge(l_y, j + 1)

                input_of(0, 0)
                with act.Fori(0, 3) as i:
                    for par in range(2):
                        block_of(i * 2 + par, par)
                block_of(6, 0)
                block_of(7, 1, last=True)

            def gla():
                act.wait_ge(job_done, START["gla"])
                act.dma_start(pmask[:], pair_masks).then_inc(g_in, 16)
                act.dma_start(alow_w[:], alpha_w).then_inc(g_in, 16)
                act.dma_start(aup_w[:], alpha_up).then_inc(g_in, 16)
                act.wait_ge(g_low, 1)
                act.copy(alow[:], AUX[0:RANK, 0:2, :].rearrange("p a n -> p (a n)")).then_inc(g_lowc, 1)
                for h in range(KV):
                    act.wait_ge(g_z, h + 1)
                    if h:
                        act.wait_ge(g_zero, h)
                    act.activation(T[:, 1, :], AUX[:, 2 * (h % 2):2 * (h % 2) + 2, :].rearrange("p a n -> p (a n)"),
                                   ACT.Abs, bias=vcol("b_alpha", h)).then_inc(g_abs, 1)
                    act.wait_ge(g_abs, h + 1)
                    chain.link(act.activation(T[:, 1, :], T[:, 1, :], ACT.Exp, scale=-1.0))
                    chain.link(act.activation(T[:, 1, :], T[:, 1, :], ACT.Ln, bias=1.0))
                act.wait_ge(g_zero, KV)
                act.wait_ge(x2_saved, 16)
                def queries(n0):
                    act.wait_ge(job_done, n0 + 1)
                    act.activation(gq[:], G[:, 0, :], ACT.Copy, scale=P ** -0.5).then_inc(evac["act"], 1)
                    empty(n0 + 1, 1, gk[:])

                def head(h, last=False):
                    n0 = h * 6 + START["gla"]
                    head = gsum[:, bass.ds(h, 1), :].rearrange("p a n -> p (a n)")

                    def decay(step):
                        act.wait_ge(g_diff, h * 7 + step)
                        if step < 7:
                            chain.link(act.activation(dec[:], dec[:], ACT.Abs))
                        act.activation(dec[:], dec[:], ACT.Exp, scale=-1.0 / TAU).then_inc(g_exp, 1)

                    def values(n):
                        act.wait_ge(g_vt, h * 2 + (n + 1))
                        act.copy(vtok[:, :, n * P:(n + 1) * P], AUX[:, 2:4, :].rearrange("p a (b n) -> p (a b) n", n=P))\
                           .then_inc(g_vc, 1)

                    def gate(n):
                        wait_apart(act, job_done, n0 + (5 + n))
                        act.activation(ya[:, bass.ds(h * 2 + n, 1), :].rearrange("p a n -> p (a n)"), G[:, n, :], ACT.Silu)\
                           .then_inc(evac["act"], 1)

                    decay(1)
                    decay(2)
                    empty(n0 + 2, 0, T[:, 0, :])
                    decay(3)
                    act.wait_ge(g_y, h)
                    values(0)
                    empty(n0 + 3, 1, T[:, 1, :])
                    decay(4)
                    values(1)
                    decay(5)
                    gate(0)
                    decay(6)
                    gate(1)
                    decay(7)
                    act.wait_ge(g_kt, h + 1)
                    act.copy(ktok[:], AUX[:, 2:4, :].rearrange("p a (b n) -> p (a b) n", n=P)).then_inc(g_kc, 1)
                    wait_apart(act, g_dk, h * 7 + 7)
                    act.activation(chunk_decay[:], gsum[:, bass.ds(h, 1), CHUNK - 1::CHUNK].rearrange("p a n -> p (a n)"),
                                   ACT.Exp, scale=1.0 / TAU).then_inc(g_cd, 1)
                    act.activation(dec[:], head, ACT.Exp, scale=1.0 / TAU).then_inc(g_exp, 1)
                    act.wait_ge(g_dq, h * 7 + 7)
                    for half in range(2):
                        act.wait_ge(g_o, h * 2 + (half + 1))
                        for d in range(2):
                            act.copy(results[:, half, d, :], AUX[:, 2 + d, :]).then_inc(g_oc, 1)
                    if not last:
                        queries(n0 + 6)
                    act.wait_ge(g_oc, h * 4 + 4)
                    for d in range(2):
                        act.activation(T[:, d, :].rearrange("p (a n) -> p a n", a=2), results[:, :, d, :], ACT.Square)\
                           .then_inc(g_sq, 1)
                    act.wait_ge(g_var, h + 1)
                    act.activation(dec[:], dec[:], ACT.Sqrt).then_inc(g_r, 1)

                queries(START["gla"])
                with chain.loop(KV - 1, 6) as h:
                    head(h)
                chain.turn = None
                head(KV - 1, last=True)
                act.wait_ge(g_y, KV)

            def pooling():
                act.dma_start(inv_cnt[:], inv_count).then_inc(p_in, 16)
                with act.Fori(0, KV) as g:
                    act.dma_start(pool_m[:], pool_w[bass.ds(g, 1)].rearrange("a p k n -> (a p) k n")).then_inc(p_m, 16)
                    for par in range(2):
                        empty(g * 2 + (START["pool"] + par), par, T[:, par, :])
                    for m in range(2):
                        wait_apart(act, p_mm, g + 1)
                        act.activation(yb[:, bass.ds(g * 2 + m, 1), :].rearrange("p a n -> p (a n)"),
                                       AUX[:, 2 * m:2 * m + 2, :].rearrange("p a n -> p (a n)"),
                                       ACT.Copy, scale=dcol("pool_scale", g * 2 + m)).then_inc(p_used, 1)
                    act.wait_ge(p_used, g * 2 + 2)

            def gates():
                with act.Fori(0, 4) as i:
                    for par in range(2):
                        act.wait_ge(b_y, i * 2)
                        act.wait_ge(job_done, i * 2 + (START["gate_b"] + par + 1))
                        act.activation(T[:, par, :], G[:, par, :], ACT.Silu).then_inc(evac["act"], 1)
                act.wait_ge(b_y, 8)
                with act.Fori(0, 8) as i:
                    for par in range(2):
                        act.wait_ge(gates_out[par], i * 16)
                        wait_apart(act, job_done, i * 2 + (START["merge"] + par + 1))
                        act.activation(T[:, par, :], G[:, par, :], ACT.Sigmoid, bias=dcol("b_merge", i * 2 + par))\
                           .then_inc(evac["act"], 1)
                        act.wait_ge(evac["act"], i * 2 + (BASE["merge"]["act"] + par + 3))
                        act.dma_start(gate_tiles[bass.ds(i * 2 + par, 1)].rearrange("a p n -> (a p) n"),
                                      T[:, par, :]).then_inc(gates_out[par], 16)
                for par in range(2):
                    act.wait_ge(gates_out[par], 128)

            def projections():
                act.wait_ge(job_done, START["proj_a"])
                for n, src in enumerate((ya, yb)):
                    if n:
                        act.wait_ge(job_done, START["proj_b"])
                    for par in range(2):
                        if n:
                            act.wait_ge(merged, 8)
                        act.dma_start(T[:, par, :], gate_tiles[8 * n + par]).then_inc(gates_in[par], 16)
                    for k in range(KT):
                        act.copy(Hhi[:, k, :], src[:, k, :]).then_inc(s_hi, 1)
                    with act.Fori(0, 3) as i:
                        for par in range(2):
                            act.wait_ge(merged, i * 2 + (8 * n + par + 1))
                            act.dma_start(T[:, par, :], gate_tiles[bass.ds(i * 2 + (8 * n + 2 + par), 1)]
                                          .rearrange("a p n -> (a p) n")).then_inc(gates_in[par], 16)
                for k in range(KT):
                    act.wait_ge(merged, 8 + k + 1)
                    act.copy(Uhi[:, k, :], ya[:, k, :]).then_inc(s_hi, 1)
                act.wait_ge(job_done, START["out"])
                act.dma_start(X2[:], scratch[0]).then_inc(x2_back, 16)

            def layer_norm():
                for k in range(KT):
                    act.wait_ge(n_cent, k + 1)
                    if k >= 2:
                        act.wait_ge(n_acc, k - 1)
                    act.activation(T[:, k % 2, :], X2[:, k, :], ACT.Square).then_inc(n_sq, 1)
                act.wait_ge(n_var, 1)
                act.activation(rstd[:], rstd[:], ACT.Sqrt).then_inc(n_r, 1)
                for k in range(KT):
                    act.wait_ge(n_y, k + 1)
                    act.dma_start(out[:, k, :], X2[:, k, :]).then_inc(out_done, 16)

            mem_phase(0)
            act.wait_ge(x_loaded, 16)
            norm("nmix0", X, Hhi, S)
            act.wait_ge(norm_s["lo"], KT * NORMS.index("nmix0") + KT)
            act.dma_start(wmask[:], masks).then_inc(masks_in, 16)
            act.dma_start(sin[:].bitcast(I32), pos).then_inc(pos_in, 16)
            mem_attention(0)
            window()
            project_out(0)
            mlp(0)
            act.wait_ge(evac["dve"], 2 + BASE["mem1"]["dve"])
            act.dma_start(mraw[:], memT).then_inc(mem_in[1], 16)
            act.dma_start(scratch[0], X[:]).then_inc(x_saved, 16)
            mem_phase(1)
            norm("nmix1", X, Hhi, S)
            act.wait_ge(norm_s["lo"], KT * NORMS.index("nmix1") + KT)
            act.wait_ge(x_saved, 16)
            mem_attention(1)
            lru()
            project_out(1)
            mlp(1)
            act.wait_ge(evac["dve"], 2 + BASE["gla"]["dve"])
            norm("nfin", X, Hhi, S)
            act.wait_ge(norm_s["lo"], KT * NORMS.index("nfin") + KT)
            act.dma_start(scratch[0], X[:]).then_inc(x2_saved, 16)
            gla()
            pooling()
            gates()
            projections()
            layer_norm()
            act.wait_ge(out_done, 16 * KT)

        @block.vector
        def _(dve):
            chain = Chain(dve, dve_chain)
            dve.nop().then_inc(evac["dve"], 2)
            dve.wait_ge(tables, 32)

            def norm(name, src, hi, lo, width, gain, inplace=False):
                s, r = norm_s, NORMS.index(name)
                for k in range(KT):
                    dve.wait_ge(s["sq"], KT * r + k + 1)
                    if k == 0:
                        dve.tensor_copy(acc[:, 0:width], squares[:, 0, 0:width]).then_inc(s["acc"], 1)
                    else:
                        dve.tensor_tensor(acc[:, 0:width], acc[:, 0:width], squares[:, k % 2, 0:width], ALU.add)\
                           .then_inc(s["acc"], 1)
                    dve.wait_ge(s["acc"], KT * r + k + 1)
                dve.wait_ge(s["ssq"], r + 1)
                total = AUX[:, 0, 0:width] if width <= 512 else AUX[:, 0:2, :].rearrange("p a n -> p (a n)")
                chain.link(dve.tensor_scalar(rstd[:, 0:width], total, 1.0 / D, EPS, ALU.mult, ALU.add))
                dve.reciprocal(rstd[:, 0:width], rstd[:, 0:width]).then_inc(s["var"], 1)
                dve.wait_ge(s["r"], r + 1)

                def scaled(k):
                    if k >= 2:
                        dve.wait_ge(s["lo"], KT * r + k - 1)
                    if inplace:
                        chain.link(dve.scalar_tensor_tensor(src[:, k, :], src[:, k, :], gain(k), rstd[:, 0:width],
                                                            ALU.mult, ALU.mult))
                        dve.tensor_copy(T[:, k % 2, 0:width], src[:, k, :]).then_inc(s["t"], 1)
                    else:
                        dve.scalar_tensor_tensor(T[:, k % 2, 0:width], src[:, k, :], gain(k), rstd[:, 0:width],
                                                 ALU.mult, ALU.mult).then_inc(s["t"], 1)

                scaled(0)
                for k in range(KT):
                    if k + 1 < KT:
                        scaled(k + 1)
                    dve.wait_ge(s["hi"], KT * r + k + 1)
                    dve.tensor_tensor(lo[:, k, :], T[:, k % 2, 0:width], hi[:, k, :], ALU.subtract).then_inc(s["lo"], 1)

            def mem_phase(l):
                norm(f"nmem{l}", mraw, Mhi, Mlo, MEM, lambda k: vcol("mem_norm", k))
                with dve.Fori(0, 2) as i:
                    for par in range(2):
                        dve.wait_ge(mvt[l], i * 2 + (par + 1))
                        dve.tensor_copy(MV[:, :, bass.ds(i * 2 + par, 1), :].rearrange("p t a n -> p t (a n)"),
                                        AUX[:, 2, 0:MEM].rearrange("p (t n) -> p t n", t=2)).then_inc(mvc[l], 1)

            def attention(s, i, par, subs, nk, scale, sink, turns):
                U = NBLK * subs
                dim = P // subs

                def peak(u):
                    t = u % 4
                    mx, negm = stat[:, t:t + 1], stat[:, 4 + t:5 + t]
                    if sink and u >= 2:
                        dve.wait_ge(s["pt"], i * U + (u - 1))
                    wait_apart(dve, s["sc"], i * U + (u + 1))
                    if sink:
                        m = {0: 0, NBLK - 1: 2}.get(u // subs, 1)
                        chain.link(dve.tensor_tensor_reduce(probs[:, u % 2, :], scored(par, u, nk * P), wmask[:, m, :],
                                                            1.0, -3e38, ALU.add, ALU.max, mx))
                        dve.tensor_scalar(negm, mx, -scale, stat[:, 20 + u % subs:21 + u % subs], ALU.mult, ALU.min)\
                           .then_inc(s["mx"], 1)
                    else:
                        chain.link(dve.reduce_max(mx, scored(par, u, nk * P), AX_X))
                        dve.tensor_scalar(negm, mx, -scale, None, ALU.mult).then_inc(s["mx"], 1)

                def scale_out(u):
                    b, h = u // subs, u % subs
                    dve.wait_ge(s["pr"], i * U + (u + 1))
                    t = u % 4
                    total = stat[:, 8 + t:9 + t]
                    if sink:
                        chain.link(dve.tensor_tensor(total, total, stat[:, 12 + t:13 + t], ALU.add))
                    inv = stat[:, 16 + t:17 + t]
                    chain.link(dve.reciprocal(inv, total))
                    dve.wait_ge(s["pv"], i * U + (u + 1))
                    if b >= 2:
                        dve.wait_ge(s["ot"], i * NBLK + (b - 1))
                    dve.tensor_scalar(O_sb[:, b % 2, h * dim:(h + 1) * dim], AUX[:, 3, 0:dim],
                                      inv, None, ALU.mult).then_inc(s["os"], 1)

                if sink:
                    for h in range(subs):
                        chain.link(dve.tensor_scalar(stat[:, 20 + h:21 + h], sink(h), -1.0, None, ALU.mult))
                peak(0)
                peak(1)
                for u in range(U):
                    if u:
                        scale_out(u - 1)
                    if u + 2 < U:
                        peak(u + 2)
                scale_out(U - 1)

            def mem_attention(l):
                with chain.loop(2, 2 * NBLK * 2) as i:
                    for par in range(2):
                        attention(attns["am"], i * 2 + (par + MEM_HEADS * l), par, 1, 2, MEM_SCALE, None, None)

            def angles():
                dve.wait_ge(pos_in, 16)
                dve.wait_ge(masks_in, 16)
                turn = 2 * np.pi
                c1 = 6.28125
                c2 = float((np.array(turn - c1, np.float32).view(np.uint32) & np.uint32(0xFFFFF000)).view(np.float32))
                c3 = float(np.float32(turn - c1 - c2))
                big = 1.5 * 2.0 ** 23
                a, k = T[:, 0, :], T[:, 1, :]
                chain.link(dve.tensor_copy(k, sin[:].bitcast(I32)))
                chain.link(dve.tensor_scalar(a, k, freq, None, ALU.mult))
                for n, (t, quarter) in enumerate(((sin, 0.0), (cos, 0.25))):
                    chain.link(dve.tensor_scalar(k, a, float(1.0 / turn), quarter, ALU.mult, ALU.add))
                    chain.link(dve.tensor_scalar(k, k, big, None, ALU.add))
                    chain.link(dve.tensor_scalar(k, k, -big, None, ALU.add))
                    chain.link(dve.scalar_tensor_tensor(t[:], k, -c1, a, ALU.mult, ALU.add))
                    chain.link(dve.scalar_tensor_tensor(t[:], k, -c2, t[:], ALU.mult, ALU.add))
                    chain.link(dve.scalar_tensor_tensor(t[:], k, -c3, t[:], ALU.mult, ALU.add))
                    chain.link(dve.tensor_scalar(t[:], t[:], float(quarter * turn), float(np.float32(3.1415925)), ALU.add, ALU.min))
                    dve.tensor_scalar(t[:], t[:], -float(np.float32(3.1415925)), None, ALU.max).then_inc(trig, 1)
                    dve.wait_ge(trig, n + 1)

            def rotate(r, heads=False):
                dve.wait_ge(rot_sw, r + 1)
                chain.link(dve.tensor_tensor(T[:, 1, :], AUX[:, 0:2, :].rearrange("p a n -> p (a n)"), sin[:], ALU.mult))
                chain.link(dve.tensor_tensor(T[:, 0, :], T[:, 0, :], cos[:], ALU.mult))
                if not heads:
                    dve.tensor_tensor(T[:, 0, :], T[:, 0, :], T[:, 1, :], ALU.add).then_inc(rot_ok, 1)
                    return
                chain.link(dve.tensor_tensor(T[:, 0, :], T[:, 0, :], T[:, 1, :], ALU.add))
                at = CCOLS["half"]
                chain.link(dve.tensor_scalar(T[:, 1, :], T[:, 0, :], cst[:, at + 1:at + 2], None, ALU.mult))
                dve.tensor_scalar(T[:, 0, :], T[:, 0, :], cst[:, at:at + 1], None, ALU.mult).then_inc(rot_ok, 1)

            def window():
                dve.wait_ge(act_chain, 2)
                for r in range(2):
                    rotate(r)
                dve.wait_ge(rot_ok, 2)
                for par in range(2):
                    dve.wait_ge(vt, par + 1)
                    dve.tensor_copy(vals[:, 1:NBLK + 1, par * P:(par + 1) * P],
                                    AUX[:, 0:2, :].rearrange("p a (b n) -> p (a b) n", n=P)).then_inc(vcopied, 1)
                with chain.loop(KV, 2 * (4 + 2 + 16 * 3)) as g:
                    for par in range(2):
                        rotate(g * 2 + (2 + par), True)
                        attention(attns["aw"], g * 2 + par, par, 2, 3, SINK_SCALE,
                                  lambda h: dcol("sinks", g * 4 + (2 * par + h)), None)

            def add_to_x(name, l=None):
                with dve.Fori(0, 4) as i:
                    for par in range(2):
                        m = i * 2 + par
                        dve.wait_ge(job_done, i * 2 + (START[name] + par + 1))
                        xm = X[:, bass.ds(m, 1), :].rearrange("p a n -> p (a n)")
                        dve.tensor_tensor(xm, G[:, par, :], xm, ALU.add).then_inc(evac["dve"], 1)

            def project_out(l):
                for k in range(KT):
                    dve.wait_ge(split_hi[l], k + 1)
                    dve.tensor_tensor(Hlo[:, k, :], mixed[:, k, :], Hhi[:, k, :], ALU.subtract).then_inc(split_lo[l], 1)
                for k in range(MEM_HEADS):
                    dve.wait_ge(split_hi[l], KT + k + 1)
                    dve.tensor_tensor(MOlo[:, k, :], mo[:, k, :], MOhi[:, k, :], ALU.subtract).then_inc(split_lo[l], 1)
                dve.wait_ge(x_back[l], 16)
                add_to_x(f"wo_mixed{l}")
                dve.wait_ge(evac["dve"], 2 + BASE[f"wo_mem{l}"]["dve"])
                add_to_x(f"wo_mem{l}")
                dve.wait_ge(evac["dve"], 2 + BASE[f"up{l}0"]["dve"])

            def mlp(l):
                norm(f"nmlp{l}", X, Hhi, Hlo, S, lambda k: vcol("mlp_norm", 8 * l + k))
                n0 = START[f"up{l}0"]
                a0, d0 = BASE[f"up{l}0"]["act"], BASE[f"up{l}0"]["dve"]
                with dve.Fori(0, 4) as c:
                    with dve.Fori(0, 4) as i:
                        for par in range(2):
                            dve.wait_ge(evac["act"], c * 8 + i * 2 + (a0 + par + 3))
                            dve.wait_ge(up_hi[l], c * 8 + i * 2 + (par + 1))
                            dve.tensor_tensor(T[:, par, :], T[:, par, :], T[:, par, :], ALU.mult).then_inc(up_sq[l], 1)
                            dve.wait_ge(up_sq[l], c * 8 + i * 2 + (par + 1))
                            m = bass.ds(i * 2 + par, 1)
                            dve.tensor_tensor(Ulo[:, m, :].rearrange("p a n -> p (a n)"), T[:, par, :],
                                              Uhi[:, m, :].rearrange("p a n -> p (a n)"), ALU.subtract).then_inc(up_lo[l], 1)
                    with dve.Fori(0, 4) as i:
                        for par in range(2):
                            dve.wait_ge(job_done, c * 16 + i * 2 + (n0 + 8 + par + 1))
                            xm = X[:, bass.ds(i * 2 + par, 1), :].rearrange("p a n -> p (a n)")
                            dve.tensor_tensor(xm, G[:, par, :], xm, ALU.add).then_inc(evac["dve"], 1)
                    dve.wait_ge(evac["dve"], c * 8 + (d0 + 8 + 2))

            def lru():
                lam = vecs[:, VCOLS["lam"]:VCOLS["lam"] + 16]
                e, z, z2, s = (decay_c[:, 16 * n:16 * n + 16] for n in (1, 2, 3, 4))
                c = decay_c[:, 80:96]
                dve.tensor_scalar(s, lam, -1.0, None, ALU.mult).then_inc(l_dx, 1)
                dve.wait_ge(l_dx, 1)
                dve.tensor_tensor(decay_c[:, 0:16], lam, s, ALU.max).then_inc(l_dec, 1)
                chain.link(dve.tensor_scalar(c, s, 0.0, None, ALU.max))
                dve.wait_ge(l_de, 1)
                chain.link(dve.tensor_scalar(z, e, 2.0, None, ALU.add))
                chain.link(dve.reciprocal(z, z))
                chain.link(dve.tensor_tensor(z, z, e, ALU.mult))
                chain.link(dve.tensor_tensor(z2, z, z, ALU.mult))
                chain.link(dve.memset(s, 1.0 / 19))
                for n in range(8, -1, -1):
                    chain.link(dve.tensor_tensor(s, s, z2, ALU.mult))
                    chain.link(dve.tensor_scalar(s, s, 1.0 / (2 * n + 1), None, ALU.add))
                chain.link(dve.tensor_tensor(s, s, z, ALU.mult))
                chain.link(dve.scalar_tensor_tensor(c, s, 2.0, c, ALU.mult, ALU.add))
                dve.tensor_scalar(c, c, -8.0, None, ALU.mult).then_inc(l_dx, 1)
                dve.wait_ge(l_dx, 2)
                dve.wait_ge(pads, 2)

                def convolve(j, par):
                    dve.wait_ge(evac["act"], j * 2 + (BASE["lru"]["act"] + 3))
                    x = xc[par][:]
                    chain.link(dve.tensor_scalar(x, xb[:, 0:S], dcol("conv_w", j), dcol("conv_b", j), ALU.mult, ALU.add))
                    for tap in range(1, 4):
                        ins = dve.scalar_tensor_tensor(x, xb[:, tap:tap + S], dcol("conv_w", j + 8 * tap), x, ALU.mult, ALU.add)
                        if tap < 3:
                            chain.link(ins)
                        else:
                            ins.then_inc(l_xc, 1)

                def block_of(j, par, last=False):
                    if not last:
                        convolve(j + 1, 1 - par)
                    for dr in range(2):
                        dve.wait_ge(l_exp, j * 4 + (2 * dr + 2))
                        dve.wait_ge(l_a2, j * 2 + (dr + 1))
                        dve.scalar_tensor_tensor(T[:, dr], T[:, dr], 1.0, rg[:, dr], ALU.add, ALU.mult).then_inc(l_e, 1)
                    for dr in range(2):
                        dve.wait_ge(l_sq, j * 2 + (dr + 1))
                        dve.wait_ge(l_ix, j * 2 + (dr + 1))
                        chain.link(dve.tensor_tensor(ig[:, dr], ig[:, dr], T[:, dr], ALU.mult))
                        if dr == 0:
                            chain.link(dve.tensor_tensor_scan(rg[:, 0], av[:, 0], ig[:, 0], 0.0, ALU.mult, ALU.add))
                        else:
                            chain.link(dve.tensor_tensor_scan(rg[:, 1, ::-1], av[:, 1, ::-1], ig[:, 1, ::-1], 0.0,
                                                              ALU.mult, ALU.add))
                    dve.tensor_tensor(rg[:, 0], rg[:, 0], rg[:, 1], ALU.add).then_inc(l_h, 1)
                    dve.wait_ge(l_h, j + 1)
                    dve.wait_ge(evac["act"], j * 2 + (BASE["lru"]["act"] + 4))
                    dve.tensor_tensor(mixed[:, bass.ds(j, 1), :].rearrange("p a n -> p (a n)"), rg[:, 0], gl[:], ALU.mult)\
                       .then_inc(l_y, 1)

                convolve(0, 0)
                with chain.loop(3, 14) as i:
                    for par in range(2):
                        block_of(i * 2 + par, par)
                block_of(6, 0)
                block_of(7, 1, last=True)
                dve.wait_ge(l_y, 8)

            def gla():
                dve.wait_ge(job_done, START["gla"])
                chain.link(dve.memset(starts[:], 1.0))
                chain.link(dve.memset(starts[:, ::CHUNK], 0.0))
                for h in range(KV):
                    dve.wait_ge(g_abs, h + 1)
                    dve.tensor_scalar(T[:, 0, :], AUX[:, 2 * (h % 2):2 * (h % 2) + 2, :].rearrange("p a n -> p (a n)"),
                                      vcol("b_alpha", h), 0.0, ALU.add, ALU.min).then_inc(g_min, 1)
                    dve.wait_ge(g_min, h + 1)
                    dve.wait_ge(act_chain, 2 + 2 * (h + 1))
                    chain.link(dve.tensor_tensor(T[:, 0, :], T[:, 0, :], T[:, 1, :], ALU.subtract))
                    dve.tensor_tensor_scan(gsum[:, h, :], starts[:], T[:, 0, :], 0.0, ALU.mult, ALU.add).then_inc(g_zero, 1)
                    dve.wait_ge(g_zero, h + 1)
                chain.link(dve.memset(wts[:], 0.0))
                dve.wait_ge(g_in, 48)
                with chain.loop(KV, 4) as h:
                    def difference(step):
                        size = CHUNK >> (step - 1) if step < 7 else CHUNK
                        ref = size // 2 - 1 if step < 7 else size - 1
                        if step > 1:
                            dve.wait_ge(g_dq, h * 7 + (min(step - 1, 6)))
                        else:
                            dve.wait_ge(g_dq, h * 7)
                        g3 = gsum[:, bass.ds(h, 1), :].rearrange("p a (b n) -> p (a b) n", n=size)
                        dve.tensor_tensor(dec[:].rearrange("p (b n) -> p b n", n=size), g3,
                                          g3[:, :, ref:ref + 1].broadcast_to([P, S // size, size]), ALU.subtract)\
                           .then_inc(g_diff, 1)

                    def keep(step):
                        wait_apart(dve, g_w, h * 7 + (step + 1))
                        mask = pmask[:, step:step + 1, :].broadcast_to([P, NBLK, P])
                        dve.copy_predicated(wts[:], mask, AUX[:, 0:2, :].rearrange("p a (b n) -> p (a b) n", n=P))\
                           .then_inc(g_keep, 1)

                    for step in range(1, 8):
                        difference(step)
                        keep(step - 1)
                        dve.wait_ge(g_exp, h * 8 + step)
                        dve.tensor_tensor(dk[:], gk[:], dec[:], ALU.mult).then_inc(g_dk, 1)
                        dve.wait_ge(g_dk, h * 7 + step)
                    dve.memset(state[:, 0, :], 0.0).then_inc(g_s0, 1)
                    dve.wait_ge(g_s0, h + 1)
                    dve.wait_ge(g_cd, h + 1)
                    for c in range(S // CHUNK):
                        dve.wait_ge(g_up, h * 16 + (c + 1))
                        dve.scalar_tensor_tensor(state[:, (c + 1) % 2, :], state[:, c % 2, :], chunk_decay[:, c:c + 1],
                                                 AUX[:, c % 2, 0:2 * P], ALU.mult, ALU.add).then_inc(g_st, 1)
                        dve.wait_ge(g_st, h * 16 + (c + 1))
                    dve.wait_ge(g_sq, h * 2 + 2)
                    dve.tensor_tensor(T[:, 0, :], T[:, 0, :], T[:, 1, :], ALU.add).then_inc(g_ss, 1)
                    dve.wait_ge(g_ssq, h + 1)
                    chain.link(dve.tensor_scalar(dec[:], AUX[:, 0:2, :].rearrange("p a n -> p (a n)"), 1.0 / (2 * P), EPS_2,
                                                 ALU.mult, ALU.add))
                    dve.reciprocal(dec[:], dec[:]).then_inc(g_var, 1)
                    dve.wait_ge(g_r, h + 1)
                    for d in range(2):
                        o = results[:, :, d, :]
                        halves = dec[:].rearrange("p (a n) -> p a n", a=2)
                        chain.link(dve.scalar_tensor_tensor(o, o, dcol("gla_norm", h * 2 + d), halves, ALU.mult, ALU.mult))
                        m = ya[:, bass.ds(h * 2 + d, 1), :].rearrange("p b (a n) -> p (b a) n", a=2)
                        ins = dve.tensor_tensor(m, m, o, ALU.mult)
                        if d:
                            ins.then_inc(g_y, 1)
                        else:
                            chain.link(ins)
                dve.wait_ge(g_y, KV)

            def pooling():
                chain.link(dve.memset(unit[:], 1.0))
                chain.link(dve.memset(csum[:, 0:16], 0.0))
                dve.wait_ge(p_in, 16)
                for g, w in enumerate(WINDOWS):
                    for par in range(2):
                        u = T[:, par, :]
                        dve.wait_ge(evac["act"], 2 * g + par + 3 + BASE["pool"]["act"])
                        if g:
                            dve.wait_ge(p_mm, g)
                        chain.link(dve.tensor_tensor_scan(csum[:, 16:16 + S], unit[:], u, 0.0, ALU.mult, ALU.add))
                        chain.link(dve.tensor_tensor(pooled[:, par, :], csum[:, 16:16 + S], csum[:, 16 - w:16 - w + S],
                                                     ALU.subtract))
                        chain.link(dve.tensor_tensor(pooled[:, par, 0:16], pooled[:, par, 0:16], inv_cnt[:, g, :], ALU.mult))
                        chain.link(dve.tensor_tensor(pooled[:, par, 0:16], pooled[:, par, 0:16], u[:, 0:16], ALU.subtract))
                        dve.scalar_tensor_tensor(pooled[:, par, 16:S], pooled[:, par, 16:S], 1.0 / w, u[:, 16:S],
                                                 ALU.mult, ALU.subtract).then_inc(p_pool, 1)
                        dve.wait_ge(p_pool, 2 * g + par + 1)

            def gates():
                dve.wait_ge(p_used, 8)
                with dve.Fori(0, 4) as i:
                    for par in range(2):
                        dve.wait_ge(evac["act"], i * 2 + (BASE["gate_b"]["act"] + par + 3))
                        m = yb[:, bass.ds(i * 2 + par, 1), :].rearrange("p a n -> p (a n)")
                        dve.tensor_tensor(m, m, T[:, par, :], ALU.mult).then_inc(b_y, 1)
                dve.wait_ge(b_y, 8)

            def projections():
                for n, (name, src) in enumerate((("proj_a", ya), ("proj_b", yb))):
                    for k in range(KT):
                        dve.wait_ge(s_hi, 8 * n + k + 1)
                        dve.tensor_tensor(Hlo[:, k, :], src[:, k, :], Hhi[:, k, :], ALU.subtract).then_inc(s_lo, 1)
                    with chain.loop(4, 2 * n) as i:
                        for par in range(2):
                            dve.wait_ge(gates_in[par], i * 16 + (64 * n + 16))
                            dve.wait_ge(job_done, i * 2 + (START[name] + par + 1))
                            m = ya[:, bass.ds(i * 2 + par, 1), :].rearrange("p a n -> p (a n)")
                            if n == 0:
                                dve.tensor_tensor(m, G[:, par, :], T[:, par, :], ALU.mult).then_inc(evac["dve"], 1)
                                dve.wait_ge(evac["dve"], i * 2 + (BASE[name]["dve"] + par + 3))
                                dve.memset(stat[:, 24:25], 0.0).then_inc(merged, 1)
                            else:
                                dve.tensor_tensor(T[:, par, :], G[:, par, :], T[:, par, :], ALU.mult).then_inc(evac["dve"], 1)
                                dve.wait_ge(evac["dve"], i * 2 + (BASE[name]["dve"] + par + 3))
                                dve.tensor_tensor(m, m, T[:, par, :], ALU.add).then_inc(merged, 1)
                                chain.link(dve.memset(stat[:, 25:26], 0.0))
                for k in range(KT):
                    dve.wait_ge(s_hi, 16 + k + 1)
                    dve.tensor_tensor(Ulo[:, k, :], ya[:, k, :], Uhi[:, k, :], ALU.subtract).then_inc(s_lo, 1)

            def layer_norm():
                dve.wait_ge(x2_back, 16)
                for m in range(KT):
                    dve.wait_ge(job_done, START["out"] + m + 1)
                    dve.scalar_tensor_tensor(X2[:, m, :], X2[:, m, :], ALPHA, G[:, m % 2, :], ALU.mult, ALU.add)\
                       .then_inc(evac["dve"], 1)
                    dve.wait_ge(evac["dve"], 2 + BASE["out"]["dve"] + m + 1)
                dve.wait_ge(job_done, N_JOBS)
                for m in range(KT):
                    if m == 0:
                        dve.tensor_copy(acc[:], X2[:, 0, :]).then_inc(n_sum, 1)
                    else:
                        dve.tensor_tensor(acc[:], acc[:], X2[:, m, :], ALU.add).then_inc(n_sum, 1)
                    dve.wait_ge(n_sum, m + 1)
                dve.wait_ge(n_mean, 1)
                chain.link(dve.tensor_scalar(rstd[:], AUX[:, 0:2, :].rearrange("p a n -> p (a n)"), 1.0 / D, None, ALU.mult))
                for k in range(KT):
                    dve.tensor_tensor(X2[:, k, :], X2[:, k, :], rstd[:], ALU.subtract).then_inc(n_cent, 1)
                for k in range(KT):
                    dve.wait_ge(n_sq, k + 1)
                    if k == 0:
                        dve.tensor_copy(acc[:], T[:, 0, :]).then_inc(n_acc, 1)
                    else:
                        dve.tensor_tensor(acc[:], acc[:], T[:, k % 2, :], ALU.add).then_inc(n_acc, 1)
                    dve.wait_ge(n_acc, k + 1)
                dve.wait_ge(n_ssq, 1)
                chain.link(dve.tensor_scalar(rstd[:], AUX[:, 0:2, :].rearrange("p a n -> p (a n)"), 1.0 / D, EPS_2,
                                             ALU.mult, ALU.add))
                dve.reciprocal(rstd[:], rstd[:]).then_inc(n_var, 1)
                dve.wait_ge(n_r, 1)
                for k in range(KT):
                    chain.link(dve.scalar_tensor_tensor(X2[:, k, :], X2[:, k, :], vcol("ln_g", k), rstd[:], ALU.mult, ALU.mult))
                    dve.tensor_scalar(X2[:, k, :], X2[:, k, :], vcol("ln_b", k), None, ALU.add).then_inc(n_y, 1)

            mem_phase(0)
            dve.wait_ge(x_loaded, 16)
            norm("nmix0", X, Hhi, Hlo, S, lambda k: vcol("mix_norm", k))
            mem_attention(0)
            angles()
            window()
            project_out(0)
            mlp(0)
            mem_phase(1)
            norm("nmix1", X, Hhi, Hlo, S, lambda k: vcol("mix_norm", 8 + k))
            mem_attention(1)
            lru()
            project_out(1)
            mlp(1)
            norm("nfin", X, Hhi, Hlo, S, lambda k: vcol("final_norm", k), inplace=True)
            gla()
            pooling()
            gates()
            projections()
            layer_norm()



def feature_major(a):
    return np.ascontiguousarray(a.T.reshape(-1, P, a.shape[0]).transpose(1, 0, 2))


def vector_cols(a):
    return a.reshape(-1, P).T


def weight_jobs(w, rows=None):
    k, m = w.shape
    j = w.reshape(k // P, P, m // P, P).transpose(2, 1, 0, 3)
    if k < D:
        full = np.zeros((m // P, P, KT, P), w.dtype)
        full[:, :, :k // P] = j
        j = full
    return list(j.reshape(m // P, P, KT * P))


def constants():
    c = np.zeros((P, N_CONST), np.float32)
    c[:, CCOLS["ident"]:CCOLS["ident"] + P] = np.eye(P)
    c[:, CCOLS["ones"]:CCOLS["ones"] + P] = 1
    perm = np.zeros((P, P), np.float32)
    dup = np.zeros((P, 2, P), np.float32)
    for h in range(2):
        for f in range(8):
            perm[64 * h + 8 + f, 64 * h + f] = -1
            perm[64 * h + f, 64 * h + 8 + f] = 1
            c[64 * h + f, CCOLS["freq"]] = c[64 * h + 8 + f, CCOLS["freq"]] = np.float32(500000.0 ** (-2.0 * f / 16))
        c[64 * h:64 * h + 64, CCOLS["half"] + h] = 1
        for f in range(64):
            dup[64 * h + f, h, f] = dup[64 * h + f, h, 64 + f] = 1
    c[:, CCOLS["perm"]:CCOLS["perm"] + P] = perm
    c[:, CCOLS["dup"]:CCOLS["dup"] + 2 * P] = dup.reshape(P, 2 * P)
    q, k = np.arange(P)[:, None], np.arange(3 * P)[None, :]
    band = np.abs(k - P - q) <= 128
    masks = np.stack([np.where(band & ok, 0.0, NEG) for ok in (k >= P, k >= 0, k < 2 * P)], 1).astype(np.float32)
    t = np.arange(P)
    pairs = [np.eye(P, dtype=bool)]
    for level in range(LEVELS):
        size = CHUNK >> level
        pairs.append((t[:, None] // size == t // size) & (t[:, None] // (size // 2) != t // (size // 2)))
    counts = [1.0 / np.minimum(np.arange(1, 17), w) for w in WINDOWS]
    return (c, masks, np.ascontiguousarray(np.stack(pairs, 1).astype(np.int32)),
            np.ascontiguousarray(np.broadcast_to(np.array(counts, np.float32), (P, KV, 16))))


def kernel(**inputs):
    import concourse.bacc as bacc
    from concourse.bass_utils import run_bass_kernel_spmd as run

    a = {k: np.asarray(v) for k, v in inputs.items()}
    jobs = []
    for l in range(2):
        jobs += weight_jobs(a["w_mem_kv"][l])
        w = a["attn_w_in"][0] if l == 0 else a["lru_w_in"][0]
        if l == 0:
            q, k, v, mq = np.split(w, [1024, 1280, 1536], axis=1)
            jobs += weight_jobs(mq) + weight_jobs(k) + weight_jobs(v) + weight_jobs(q)
        else:
            xb, gate, mq = np.split(w, [1024, 2048], axis=1)
            jobs += weight_jobs(mq)
            for x, g in zip(weight_jobs(xb), weight_jobs(gate)):
                jobs += [x, g]
        jobs += weight_jobs(a["w_out"][l][:D]) + weight_jobs(a["w_out"][l][D:])
        for c in range(4):
            jobs += weight_jobs(a["w_up"][l][:, c * D:(c + 1) * D]) + weight_jobs(a["w_down"][l][c * D:(c + 1) * D])
    q, k, v, gate_a, low, pool_in, gate_b, merge = np.split(
        a["w_in_2"][0], [512, 1024, 2048, 3072, 3088, 4112, 5136], axis=1)
    for h in range(KV):
        for w in (q[:, h * P:(h + 1) * P], k[:, h * P:(h + 1) * P], v[:, h * 2 * P:(h + 1) * 2 * P],
                  gate_a[:, h * 2 * P:(h + 1) * 2 * P]):
            jobs += weight_jobs(w)
    for w in (pool_in, gate_b, merge, a["w_proj_a_2"][0], a["w_proj_b_2"][0], a["w_out_2"][0]):
        jobs += weight_jobs(w)
    wj = np.stack(jobs)
    vec = np.concatenate([
        vector_cols(a["mix_norm"]), vector_cols(a["mlp_norm"]), vector_cols(a["mem_norm"]), vector_cols(a["final_norm"]),
        np.broadcast_to(a["attn_sinks"], (P, HEADS)), vector_cols(a["lru_conv_w"]), vector_cols(a["lru_conv_b"]),
        vector_cols(a["lru_ba"]), vector_cols(a["lru_bx"]), vector_cols(a["lru_lambda"]),
        vector_cols(a["b_alpha_2"]), vector_cols(a["gla_norm_g_2"]), vector_cols(a["pool_scale_2"]),
        vector_cols(a["b_merge_2"]), vector_cols(a["ln_g_2"]), vector_cols(a["ln_b_2"])], axis=1)
    lw = np.stack([a["lru_wa"][0, 0], a["lru_wx"][0, 0], a["lru_wa"][0, 1], a["lru_wx"][0, 1]], 2)
    const, masks, pair_masks, inv_count = constants()
    arrays = {
        "xT": feature_major(a["x"][0]), "memT": feature_major(a["mem"][0]),
        "pos": np.ascontiguousarray(np.broadcast_to(a["positions"], (P, S))),
        "wjobs": wj, "lru_w": np.ascontiguousarray(lw), "vec": np.ascontiguousarray(vec), "const": const, "masks": masks,
        "pair_masks": pair_masks, "inv_count": inv_count,
        "alpha_w": np.ascontiguousarray(low.reshape(KT, P, RANK).transpose(1, 0, 2)),
        "alpha_up": a["w_alpha_up_2"][0],
        "pool_w": np.ascontiguousarray(a["w_pool_grp_2"][0].reshape(KV, 2, P, 2 * P).transpose(0, 2, 1, 3)),
    }
    nc = bacc.Bacc("TRN2", target_bir_lowering=False, num_devices=1)
    t = {k: nc.dram_tensor(k, v.shape, mybir.dt.from_np(v.dtype), kind="ExternalInput").ap() for k, v in arrays.items()}
    scratch = nc.dram_tensor("scratch", (1, P, KT, S), F32, kind="Internal").ap()
    out = nc.dram_tensor("out", (P, KT, S), F32, kind="ExternalOutput").ap()
    gate_tiles = nc.dram_tensor("gate_tiles", (16, P, S), F32, kind="Internal").ap()
    build(nc, t["xT"], t["memT"], t["pos"], t["wjobs"], t["lru_w"], t["alpha_w"], t["alpha_up"], t["pool_w"], t["vec"],
          t["const"], t["masks"], t["pair_masks"], t["inv_count"], scratch, gate_tiles, out)
    r = run(nc, [arrays], core_ids=[0])
    y = r.results[0]["out"]
    return y.transpose(1, 0, 2).reshape(D, S).T[None]
```

```python
from contextlib import ExitStack, contextmanager

import numpy as np
import concourse.bass as bass
from concourse import mybir

F32 = mybir.dt.float32
F32R = mybir.dt.float32r
I32 = mybir.dt.int32
ALU = mybir.AluOpType
ACT = mybir.ActivationFunctionType
AX_X = mybir.AxisListType.X

P = 128
D = 1024
S = 1024
KT = D // P
NBLK = S // P
MEM = 256
MEM_HEADS = 4
HEADS = 16
KV = 4
HD = 64
SINK_SCALE = HD ** -0.5
MEM_SCALE = 128 ** -0.5
NEG = -1e30
EPS = 1e-6
EPS_2 = 1e-5
ALPHA = 2.0 ** 0.25
CHUNK = 64
TAU = 16.0
RANK = 16
LEVELS = 6
WINDOWS = (2, 4, 8, 16)

PHASES = [("mem0", 8, "act"), ("mem1", 8, "act")]
for _l in range(2):
    PHASES += [(f"mq{_l}", 4, "act")]
    PHASES += [("k", 2, "act"), ("v", 2, "act"), ("q", 8, "act")] if _l == 0 else [("lru", 16, "act")]
    PHASES += [(f"wo_mixed{_l}", 8, "dve"), (f"wo_mem{_l}", 8, "dve")]
    for _c in range(4):
        PHASES += [(f"up{_l}{_c}", 8, "act"), (f"down{_l}{_c}", 8, "dve")]
PHASES += [("gla", 24, "act"), ("pool", 8, "act"), ("gate_b", 8, "act"), ("merge", 16, "act"),
           ("proj_a", 8, "dve"), ("proj_b", 8, "dve"), ("out", 8, "dve")]
START, BASE, PREV = {}, {}, {}
_n, _done, _before = 0, {"act": 0, "dve": 0}, None
for _name, _count, _eng in PHASES:
    START[_name], BASE[_name], PREV[_name] = _n, dict(_done), _before
    _n += _count
    _done[_eng] += _count
    _before = _eng
N_JOBS = _n
MEM_JOBS = START["mq0"]
EVAC = {name: eng for name, _, eng in PHASES}

NORMS = ["nmem", "nmix0", "nmlp0", "nmix1", "nmlp1", "nfin"]


def tiles_before(name):
    return KT * (NORMS.index(name) - 1)


VCOLS, _at = {}, 0
for _name, _n in (("mix_norm", 16), ("mlp_norm", 16), ("mem_norm", 8), ("final_norm", 8), ("sinks", 16),
                  ("conv_w", 32), ("conv_b", 8), ("lru_ba", 16), ("lru_bx", 16), ("lam", 16),
                  ("b_alpha", 4), ("gla_norm", 8), ("pool_scale", 8), ("b_merge", 16), ("ln_g", 8),
                  ("ln_b", 8)):
    VCOLS[_name] = _at
    _at += _n
N_VEC = _at

CCOLS, _at = {}, 0
for _name, _n in (("ident", 128), ("ones", 128), ("perm", 128), ("dup", 256), ("freq", 1), ("half", 2)):
    CCOLS[_name] = _at
    _at += _n
N_CONST = _at


class Chain:

    def __init__(self, eng, sem):
        self.eng, self.sem, self.turn, self.per, self.n = eng, sem, None, 0, 0

    def link(self, ins):
        ins.then_inc(self.sem, 1)
        self.n += 1
        self.eng.wait_ge(self.sem, self.n if self.turn is None else self.turn * self.per + self.n)

    @contextmanager
    def loop(self, count, per):
        first = self.n
        with self.eng.Fori(0, count) as i:
            self.turn, self.per = i, per
            yield i
            assert self.n == first + per, (self.n - first, per)
        self.turn, self.n = None, first + per * count


def build(nc, xT, memT, pos, wjobs, lru_w, alpha_w, alpha_up, pool_w, vec, const, masks, pair_masks, inv_count,
          scratch, gate_tiles, kv_tiles, out):
    with ExitStack() as ctx:
        base = (nc.sbuf_base + 31) // 32 * 32

        def sb(name, shape, dt, at):
            return nc.alloc_sbuf_tensor_at(name, shape, dt, offset=base + at)

        def sem(name):
            return ctx.enter_context(nc.semaphore(name))

        KB = 1024
        X_AT, H_AT, U_AT, W_AT, R_AT = 0, 32 * KB, 96 * KB, 160 * KB, 184 * KB
        X = sb("X", [P, KT, S], F32, X_AT)
        Hhi = sb("Hhi", [P, KT, S], F32R, H_AT)
        Hlo = sb("Hlo", [P, KT, S], F32R, H_AT + 32 * KB)
        Uhi = sb("Uhi", [P, KT, S], F32R, U_AT)
        Ulo = sb("Ulo", [P, KT, S], F32R, U_AT + 32 * KB)
        wraw = sb("wraw", [P, 2, KT, P], F32, W_AT)
        whi = sb("whi", [P, 2, KT, P], F32R, W_AT + 8 * KB)
        wlo = sb("wlo", [P, 2, KT, P], F32R, W_AT + 16 * KB)
        T = sb("T", [P, 2, S], F32, R_AT)
        MK = sb("MK", [P, MEM_HEADS, MEM], F32, R_AT + 8 * KB)
        MV = sb("MV", [P, 2, MEM_HEADS, P], F32, R_AT + 12 * KB)
        vecs = sb("vecs", [P, N_VEC], F32, R_AT + 16 * KB)
        cst = sb("cst", [P, N_CONST], F32, R_AT + 17 * KB)
        stat = sb("stat", [P, 48], F32, R_AT + 19 * KB + 640)
        O_sb = sb("O_sb", [P, 2, P], F32, R_AT + 19 * KB + 832)
        probsT = sb("probsT", [P, 2, 3 * P], F32, R_AT + 20 * KB + 832)
        squares = sb("squares", [P, 2, S], F32, H_AT + 48 * KB)
        acc = sb("acc", [P, S], F32, H_AT + 56 * KB)
        rstd = sb("rstd", [P, S], F32, H_AT + 60 * KB)
        eps_col = stat[:, 30:31]
        mraw = sb("mraw", [P, KT, MEM], F32, U_AT)
        MT = sb("MT", [P, 2, MEM], F32, U_AT + 8 * KB)
        MK1 = sb("MK1", [P, MEM_HEADS, MEM], F32, U_AT + 12 * KB)
        MV1 = sb("MV1", [P, 2, MEM_HEADS, P], F32, U_AT + 16 * KB)
        mixed = sb("mixed", [P, KT, S], F32, U_AT + 32 * KB)
        mo = sb("mo", [P, MEM_HEADS, S], F32, X_AT)
        MOhi = sb("MOhi", [P, MEM_HEADS, S], F32R, U_AT)
        MOlo = sb("MOlo", [P, MEM_HEADS, S], F32R, U_AT + 16 * KB)
        keys = sb("keys", [P, KV, S + 2 * P], F32, U_AT)
        vals = sb("vals", [P, NBLK + 2, KV * HD], F32, U_AT + 20 * KB)
        cos = sb("cos", [P, S], F32, X_AT + 16 * KB)
        sin = sb("sin", [P, S], F32, X_AT + 20 * KB)
        wmask = sb("wmask", [P, 3, 3 * P], F32, X_AT + 24 * KB)
        probs = sb("probs", [P, 2, 3 * P], F32, X_AT + 29 * KB)
        lw = sb("lw", [P, 2, 4, P], F32, U_AT)
        xb = sb("xb", [P, S + 8], F32, U_AT + 4 * KB)
        xc = [sb("xc0", [P, S], F32, U_AT + 9 * KB), sb("xc1", [P, S], F32, X_AT + 28 * KB)]
        rg = sb("rg", [P, 2, S], F32, U_AT + 13 * KB)
        ig = sb("ig", [P, 2, S], F32, U_AT + 21 * KB)
        decay_c = sb("decay_c", [P, 96], F32, U_AT + 29 * KB)
        av = sb("av", [P, 2, S], F32, X_AT + 16 * KB)
        gl = sb("gl", [P, S], F32, X_AT + 24 * KB)

        gsum = sb("gsum", [P, KV, S], F32, U_AT)
        gq = sb("gq", [P, S], F32, U_AT + 16 * KB)
        gk = sb("gk", [P, S], F32, U_AT + 20 * KB)
        dec = sb("dec", [P, S], F32, U_AT + 24 * KB)
        dq = sb("dq", [P, S], F32, U_AT + 28 * KB)
        dk = sb("dk", [P, S], F32, U_AT + 32 * KB)
        vtok = sb("vtok", [P, NBLK, 2 * P], F32, U_AT + 36 * KB)
        results = sb("results", [P, 2, 2, S // 2], F32, U_AT + 36 * KB)
        ktok = sb("ktok", [P, NBLK, P], F32, U_AT + 44 * KB)
        wts = sb("wts", [P, NBLK, P], F32, U_AT + 48 * KB)
        state = sb("state", [P, 2, 2 * P], F32, U_AT + 52 * KB)
        pmask = sb("pmask", [P, LEVELS + 1, P], I32, U_AT + 54 * KB)
        chunk_decay = sb("chunk_decay", [P, S // CHUNK], F32, U_AT + 57 * KB + 512)
        alow_w = sb("alow_w", [P, KT, RANK], F32, U_AT + 58 * KB)
        aup_w = sb("aup_w", [RANK, KV * P], F32, U_AT + 59 * KB)
        alow = sb("alow", [RANK, S], F32, U_AT + 28 * KB)
        starts = sb("starts", [P, S], F32, U_AT + 24 * KB)
        ya = sb("ya", [P, KT, S], F32, X_AT)
        yb = sb("yb", [P, KT, S], F32, U_AT + 32 * KB)
        unit = sb("unit", [P, S], F32, U_AT)
        csum = sb("csum", [P, 16 + S], F32, U_AT + 4 * KB)
        pooled = sb("pooled", [P, 2, S], F32, U_AT + 9 * KB)
        pool_m = sb("pool_m", [P, 2, 2 * P], F32, U_AT + 17 * KB)
        inv_cnt = sb("inv_cnt", [P, KV, 16], F32, U_AT + 19 * KB)
        X2 = sb("X2", [P, KT, S], F32, H_AT)
        ln_acc = sb("ln_acc", [P, S], F32, X_AT)
        ln_stat = sb("ln_stat", [P, S], F32, X_AT + 4 * KB)

        G = ctx.enter_context(nc.psum_tensor("G", [P, 2, S], F32))
        AUX = ctx.enter_context(nc.psum_tensor("AUX", [P, 4, 512], F32))
        ident = cst[:, CCOLS["ident"]:CCOLS["ident"] + P]
        ones = cst[:, CCOLS["ones"]:CCOLS["ones"] + P]
        perm = cst[:, CCOLS["perm"]:CCOLS["perm"] + P]
        freq = cst[:, CCOLS["freq"]:CCOLS["freq"] + 1]

        def vcol(name, i):
            return vecs[:, VCOLS[name] + i:VCOLS[name] + i + 1]

        def dcol(name, i, width=1):
            return vecs[:, bass.ds(VCOLS[name] + i, width)]

        w_loaded = [sem("w_loaded0"), sem("w_loaded1")]
        w_hi = sem("w_hi")
        w_split = sem("w_split")
        job_done = sem("job_done")
        evac = {"act": sem("evac_act"), "dve": sem("evac_dve")}
        act_chain, dve_chain, pool_chain = sem("act_chain"), sem("dve_chain"), sem("pool_chain")
        tables = sem("tables")
        x_loaded = sem("x_loaded")
        x_back = [sem("x_back0"), sem("x_back1")]
        x_saved = sem("x_saved")
        mem_in, mem_ready = sem("mem_in"), sem("mem_ready")
        kv_saved, kv_in = sem("kv_saved"), sem("kv_in")
        pos_in, masks_in, pads = sem("pos_in"), sem("masks_in"), sem("pads")
        out_done = sem("out_done")

        norm_s = {k: sem(f"norm_{k}") for k in ("sq", "acc", "ssq", "var", "r", "t", "hi", "lo")}

        def attn_sems(name):
            return {k: sem(f"{name}_{k}") for k in ("sc", "mx", "pr", "pt", "pc", "pv", "os", "ot", "oc")}

        attns = {n: attn_sems(n) for n in ("am", "aw")}
        mvt, mvc = sem("mvt"), sem("mvc")
        trig, rot_sw, rot_ok = sem("trig"), sem("rot_sw"), sem("rot_ok")
        kdup, kcopied, vt, vcopied = sem("kdup"), sem("kcopied"), sem("vt"), sem("vcopied")
        split_hi, split_lo = [sem("split_hi0"), sem("split_hi1")], [sem("split_lo0"), sem("split_lo1")]
        up_hi, up_lo, up_sq = [sem("up_hi0"), sem("up_hi1")], [sem("up_lo0"), sem("up_lo1")], [sem("up_sq0"), sem("up_sq1")]
        lw_in = [sem("lw_in0"), sem("lw_in1")]
        l_dec, l_xc, l_mm, l_sig, l_exp, l_a2, l_e, l_sq, l_ix, l_h, l_sum, l_y = (
            sem("l_" + k) for k in ("dec", "xc", "mm", "sig", "exp", "a2", "e", "sq", "ix", "h", "sum", "y"))
        l_dx, l_de = sem("l_dx"), sem("l_de")
        g_in, g_low, g_lowc, g_z, g_abs, g_min, g_zero = (sem("g_" + k) for k in ("in", "low", "lowc", "z", "abs", "min", "zero"))
        g_diff, g_exp, g_dq, g_dk, g_w, g_keep = (sem("g_" + k) for k in ("diff", "exp", "dq", "dk", "w", "keep"))
        g_vt, g_vc, g_kt, g_kc, g_up, g_st, g_o, g_oc = (sem("g_" + k) for k in ("vt", "vc", "kt", "kc", "up", "st", "o", "oc"))
        g_s0 = sem("g_s0")
        g_cd, g_sq, g_ss, g_ssq, g_var, g_r, g_y = (sem("g_" + k) for k in ("cd", "sq", "ss", "ssq", "var", "r", "y"))
        p_in, p_m, p_pool, p_mm, p_used = sem("p_in"), sem("p_m"), sem("p_pool"), sem("p_mm"), sem("p_used")
        b_gate, b_y = sem("b_gate"), sem("b_y")
        gates_out, gates_in = [sem("gates_out0"), sem("gates_out1")], [sem("gates_in0"), sem("gates_in1")]
        s_hi, s_lo, merged = sem("s_hi"), sem("s_lo"), sem("merged")
        x2_saved, x2_back = sem("x2_saved"), sem("x2_back")
        n_sum, n_mean, n_cent, n_sq, n_acc, n_ssq, n_r, n_y = (
            sem("n_" + k) for k in ("sum", "mean", "cent", "sq", "acc", "ssq", "r", "y"))

        def sums(width):
            return AUX[:, 0, 0:width] if width <= 512 else AUX[:, 0:2, :].rearrange("p a n -> p (a n)")

        stood = {nc.scalar: sem("act_stood"), nc.vector: sem("dve_stood"), nc.gpsimd: sem("pool_stood")}

        def wait_apart(eng, semaphore, value):
            eng.wait_ge(semaphore, value)
            eng.sem_inc(stood[eng], 1)

        def scored(par, u, width):
            return G[:, par, 0:width] if u % 3 == 2 else AUX[:, u % 3, 0:width]

        block = ctx.enter_context(nc.Block())

        @block.sync
        def _(sp):
            for par in range(2):
                sp.dma_start(wraw[:, par], wjobs[par]).then_inc(w_loaded[par], 16)
            for first, last, free in ((1, MEM_JOBS // 2 + 1, job_done), (MEM_JOBS // 2 + 1, N_JOBS // 2, w_split)):
                with sp.Fori(first, last) as i:
                    for par in range(2):
                        sp.wait_ge(free, i * 2 + (par - 1))
                        sp.dma_start(wraw[:, par], wjobs[bass.ds(i * 2 + par, 1)].rearrange("a p n -> (a p) n"))\
                          .then_inc(w_loaded[par], 16)

        @block.gpsimd
        def _(pool):
            def split(n, i, par, started):
                pool.wait_ge(w_loaded[par], i * 16 + 16)
                if started:
                    wait_apart(pool, job_done, n - 1)
                pool.tensor_copy(whi[:, par], wraw[:, par]).then_inc(w_hi, 1)
                pool.wait_ge(w_hi, n + 1)
                pool.tensor_tensor(wlo[:, par], wraw[:, par], whi[:, par], ALU.subtract).then_inc(w_split, 1)

            def splits(first, last):
                with pool.Fori(first // 2, last // 2) as i:
                    for par in range(2):
                        split(i * 2 + par, i, par, True)

            pool.nop().then_inc(w_hi, MEM_JOBS)
            pool.nop().then_inc(w_split, MEM_JOBS)
            for par in range(2):
                split(MEM_JOBS + par, MEM_JOBS // 2, par, False)
            splits(MEM_JOBS + 2, START["k"])
            pool.wait_ge(kv_saved, 32)
            pool.memset(keys[:, :, 0:P], 0.0)
            pool.memset(keys[:, :, S + P:S + 2 * P], 0.0)
            pool.memset(vals[:, 0, :], 0.0)
            pool.memset(vals[:, NBLK + 1, :], 0.0).then_inc(pads, 1)
            splits(START["k"], START["lru"] + 4)
            pool.memset(xb[:, 0:1], 0.0)
            pool.memset(xb[:, S + 1:S + 3], 0.0).then_inc(pads, 1)

            def lru_block(j, par, last=False):
                if not last:
                    split(j * 2 + (START["lru"] + 4), j + (START["lru"] // 2 + 2), 0, True)
                for dr in range(2):
                    pool.wait_ge(l_sig, j * 4 + (2 * dr + 2))
                    pool.tensor_tensor(ig[:, dr], ig[:, dr], xc[par][:], ALU.mult).then_inc(l_ix, 1)
                for dr in range(2):
                    pool.wait_ge(l_exp, j * 4 + (2 * dr + 2))
                    pool.tensor_tensor(T[:, dr], av[:, dr], av[:, dr], ALU.mult).then_inc(l_a2, 1)
                if not last:
                    split(j * 2 + (START["lru"] + 5), j + (START["lru"] // 2 + 2), 1, True)

            with pool.Fori(0, 3) as i:
                for par in range(2):
                    lru_block(i * 2 + par, par)
            lru_block(6, 0)
            lru_block(7, 1, last=True)
            splits(START["wo_mixed1"] + 2, START["gla"] + 4)
            with pool.Fori(0, KV) as h:
                def decayed(step, n):
                    pool.wait_ge(g_exp, h * 8 + step)
                    if n:
                        pool.wait_ge(g_w, h * 7 + (6 if step == 8 else step))
                    pool.tensor_tensor(dq[:], gq[:], dec[:], ALU.mult).then_inc(g_dq, 1)

                for n in (1, 2, -4, 3, -5, 4, 5, -6, 6, -7, 8, -8, -9):
                    if n > 0:
                        decayed(n, True)
                    else:
                        split(h * 6 + (START["gla"] - n), h * 3 + (START["gla"] // 2 + -n // 2), -n % 2, True)
            splits(START["gla"] + 28, N_JOBS)

        @block.tensor
        def _(pe):
            def psum_waits(name, l, par, own=None, other=None):
                e = EVAC[name]
                pe.wait_ge(evac[e], l + (1 + (BASE[name][e] if own is None else 0)) if own is None else own + l + 1)
                if PREV[name] not in (None, e):
                    o = PREV[name]
                    pe.wait_ge(evac[o], (2 + BASE[name][o] if other is None else other + 2) - (par == 0))

            def job_part(q, n, par, hi, lo, ready, kt=KT, width=S):
                half = min(width, 512)
                halves = width // half
                k, c = q // halves, q % halves
                if q == 0:
                    pe.wait_ge(w_split, n + 1)
                if c == 0 and ready is not None:
                    pe.wait_ge(ready[0], ready[1] + (k + 1))
                cols = slice(c * half, (c + 1) * half)
                for j, (w, x) in enumerate(((whi, hi), (whi, lo), (wlo, hi))):
                    mm = pe.matmul(G[:, par, cols], w[:, par, k, :], x[:, k, cols],
                                   start=(k == 0 and j == 0), stop=(k == kt - 1 and j == 2))
                if q == kt * halves - 1:
                    mm.then_inc(job_done, 1)

            def job(n, par, hi, lo, ready, kt=KT, width=S):
                for q in range(kt * (width // min(width, 512))):
                    job_part(q, n, par, hi, lo, ready, kt, width)

            def next_part(q, n, par, shift):
                if q == 0:
                    pe.wait_ge(evac["act"], n + shift)
                job_part(q, n, par, Hhi, Hlo, None)

            def jobs(name, count, hi, lo, ready, after=None, **kw):
                with pe.Fori(0, count // 2) as i:
                    for par in range(2):
                        psum_waits(name, i * 2 + par, par)
                        job(i * 2 + (START[name] + par), par, hi, lo, ready, **kw)
                        if after:
                            after(i, par)

            def sum_squares(name, width):
                r = NORMS.index(name)
                pe.wait_ge(norm_s["acc"], KT * r + KT)
                half = min(width, 512)
                for c in range(width // half):
                    mm = pe.matmul(AUX[:, c, 0:half], ones, acc[:, c * half:(c + 1) * half], start=True, stop=True)
                mm.then_inc(norm_s["ssq"], 1)

            def mem_phase(l):
                name = f"mem{l}"
                for half in range(2):
                    with pe.Fori(0, 2) as i:
                        for par in range(2):
                            m = 4 * half + par
                            pe.wait_ge(evac["act"], i * 2 + (START[name] + m + 1))
                            pe.wait_ge(w_loaded[par], i * 16 + (START[name] + 4 * half + 2) * 8)
                            for k in range(KT):
                                mm = pe.matmul(G[:, par, 0:MEM], wraw[:, par, k, :], mraw[:, k, :], start=(k == 0),
                                               stop=(k == KT - 1))
                            mm.then_inc(job_done, 1)
                            if half:
                                pe.wait_ge(evac["act"], i * 2 + (START[name] + m + 3))
                                if l or par:
                                    pe.wait_ge(mvc, i * 2 + (4 * l + par))
                                for t in range(2):
                                    tr = pe.transpose(AUX[:, 2, t * P:(t + 1) * P], MT[:, par, t * P:(t + 1) * P], ident)
                                tr.then_inc(mvt, 1)
                                pe.wait_ge(mvc, i * 2 + (4 * l + 1 + par))

            def attention(s, i, par, subs, nk, kop, vop, between):
                U = NBLK * subs
                dim = P // subs

                def scores(u):
                    b, h = u // subs, u % subs
                    if u >= 3:
                        pe.wait_ge(s["pr"], i * U + (u - 2))
                    pe.matmul(scored(par, u, nk * P), T[:, h, b * P:(b + 1) * P], kop(b),
                              start=True, stop=True).then_inc(s["sc"], 1)

                def turn(u):
                    pe.wait_ge(s["pr"], i * U + (u + 1))
                    if u:
                        pe.wait_ge(s["pc"], i * U + u)
                    for t in range(nk):
                        tr = pe.transpose(AUX[:, 2, t * P:(t + 1) * P], probs[:, u % 2, t * P:(t + 1) * P], ident)
                    tr.then_inc(s["pt"], 1)

                def weigh(u):
                    b, h = u // subs, u % subs
                    pe.wait_ge(s["pc"], i * U + (u + 1))
                    if u:
                        pe.wait_ge(s["os"], i * U + u)
                    for t in range(nk):
                        mm = pe.matmul(AUX[:, 3, 0:dim], probsT[:, u % 2, t * P:(t + 1) * P],
                                       vop(b, t), start=(t == 0), stop=(t == nk - 1))
                    mm.then_inc(s["pv"], 1)

                def turn_result(b):
                    pe.wait_ge(s["os"], i * U + (b + 1) * subs)
                    if b:
                        pe.wait_ge(s["oc"], i * NBLK + b)
                    pe.transpose(G[:, par, 512:512 + P], O_sb[:, b % 2, :], ident).then_inc(s["ot"], 1)

                scores(0)
                scores(1)
                for u in range(U):
                    if u + 2 < U:
                        scores(u + 2)
                    between(u)
                    turn(u)
                    if u >= 2 and (u - 1) % subs == 0:
                        turn_result((u - 2) // subs)
                    if u:
                        weigh(u - 1)
                if (U - 2) % subs == subs - 1:
                    turn_result((U - 2) // subs)
                weigh(U - 1)
                turn_result(NBLK - 1)

            def mem_attention(l):
                s, name = attns["am"], f"mq{l}"
                shift = 1 + BASE[name]["act"] - START[name]
                if l:
                    pe.wait_ge(kv_in, 32)
                psum_waits(name, 0, 0)
                job(START[name], 0, Hhi, Hlo, (norm_s["lo"], tiles_before(f"nmix{l}")))
                with pe.Fori(0, 2) as i:
                    for par in range(2):
                        head = i * 2 + par
                        after = head + (START[name] + 1)
                        pe.wait_ge(evac["act"], i * 2 + (3 + BASE[name]["act"] + par))
                        next_part(0, after, 1 - par, shift)
                        next_part(1, after, 1 - par, shift)

                        def between(u):
                            for q in range(2 + 2 * u, min(4 + 2 * u, 16)):
                                next_part(q, after, 1 - par, shift)

                        attention(s, head + MEM_HEADS * l, par, 1, 2,
                                  lambda b: MK[:, bass.ds(head, 1), :].rearrange("p a n -> p (a n)"),
                                  lambda b, t: MV[:, t, bass.ds(head, 1), :].rearrange("p a n -> p (a n)"), between)

            def rotate(r, e, between):
                pe.wait_ge(evac["act"], e)
                for c in range(2):
                    mm = pe.matmul(AUX[:, c, :], perm, T[:, 0, c * 512:(c + 1) * 512], start=True, stop=True)
                mm.then_inc(rot_sw, 1)
                between()
                pe.wait_ge(rot_ok, r + 1)

            def window():
                shift = 1 + BASE["k"]["act"] - START["k"]
                for par in range(2):
                    after = START["k"] + par + 1

                    def between():
                        for q in range(16):
                            next_part(q, after, 1 - par, shift)

                    rotate(par, 3 + BASE["k"]["act"] + par, between)
                    for h in range(2):
                        if h:
                            pe.wait_ge(kcopied, 2 * par + h)
                        at = CCOLS["dup"] + h * P
                        for c in range(2):
                            mm = pe.matmul(AUX[:, c, :], cst[:, at:at + P], T[:, 0, c * 512:(c + 1) * 512],
                                           start=True, stop=True)
                        mm.then_inc(kdup, 1)
                    pe.wait_ge(kcopied, 2 * par + 2)
                for par in range(2):
                    for q in range(16):
                        next_part(q, START["v"] + par + 1, 1 - par, shift)
                    pe.wait_ge(evac["act"], 3 + BASE["v"]["act"] + par)
                    if par:
                        pe.wait_ge(vcopied, 1)
                    for b in range(NBLK):
                        at = (b % 4) * P
                        tr = pe.transpose(AUX[:, b // 4, at:at + P], T[:, 0, b * P:(b + 1) * P], ident)
                    tr.then_inc(vt, 1)
                pe.wait_ge(vcopied, 2)
                pe.wait_ge(pads, 1)

                def tile(g, par, last=False):
                    p = g * 2 + par
                    after = p + (START["q"] + 1)

                    def turning():
                        if not last:
                            for q in range(6):
                                next_part(q, after, 1 - par, shift)

                    def between(u):
                        if not last and 1 <= u <= 10:
                            next_part(5 + u, after, 1 - par, shift)

                    rotate(p + 2, p + (3 + BASE["q"]["act"]), turning)
                    attention(attns["aw"], p, par, 2, 3,
                              lambda b: keys[:, bass.ds(g, 1), b * P:(b + 3) * P].rearrange("p a n -> p (a n)"),
                              lambda b, t: vals[:, b + t, bass.ds(g * HD, HD)], between)

                with pe.Fori(0, KV - 1) as g:
                    for par in range(2):
                        tile(g, par)
                for par in range(2):
                    tile(KV - 1, par, last=(par == 1))

            def project_out(l):
                jobs(f"wo_mixed{l}", 8, Hhi, Hlo, (split_lo[l], 0))
                jobs(f"wo_mem{l}", 8, MOhi, MOlo, (split_lo[l], 8), kt=4)

            def mlp(l):
                sum_squares(f"nmlp{l}", S)
                n0, a0, d0 = START[f"up{l}0"], BASE[f"up{l}0"]["act"], BASE[f"up{l}0"]["dve"]
                with pe.Fori(0, 4) as c:
                    with pe.Fori(0, 4) as i:
                        for par in range(2):
                            pe.wait_ge(evac["act"], c * 8 + i * 2 + (a0 + par + 1))
                            pe.wait_ge(evac["dve"], c * 8 + (d0 + 2 - (par == 0)))
                            job(c * 16 + i * 2 + (n0 + par), par, Hhi, Hlo, (norm_s["lo"], tiles_before(f"nmlp{l}")))
                    with pe.Fori(0, 4) as i:
                        for par in range(2):
                            pe.wait_ge(evac["dve"], c * 8 + i * 2 + (d0 + par + 1))
                            pe.wait_ge(evac["act"], c * 8 + (a0 + 8 + 2 - (par == 0)))
                            job(c * 16 + i * 2 + (n0 + 8 + par), par, Uhi, Ulo, (up_lo[l], c * 8))

            def lru():
                pe.wait_ge(attns["am"]["oc"], 2 * MEM_HEADS * NBLK)
                shift = 1 + BASE["lru"]["act"] - START["lru"]

                def gates(par, dr):
                    for g in range(2):
                        for c in range(2):
                            mm = pe.matmul(AUX[:, 2 * g + c, :], lw[:, par, 2 * dr + g, :], xc[par][:, c * 512:(c + 1) * 512],
                                           start=True, stop=True)
                    mm.then_inc(l_mm, 1)

                def first_gates(j, lw_count, par):
                    pe.wait_ge(l_xc, j + 1)
                    pe.wait_ge(lw_in[par], lw_count * 16 + 16)
                    gates(par, 0)

                def block_of(j, i, par):
                    pe.wait_ge(l_sig, j * 4 + 2)
                    gates(par, 1)
                    for q in range(16):
                        next_part(q, j * 2 + (START["lru"] + 3), 1, shift)
                    if not (isinstance(j, int) and j == 6):
                        for q in range(16):
                            next_part(q, j * 2 + (START["lru"] + 4), 0, shift)
                    pe.wait_ge(l_sig, j * 4 + 4)
                    first_gates(j + 1, i + par, 1 - par)

                for n in (1, 2):
                    for q in range(16):
                        next_part(q, START["lru"] + n, n % 2, shift)
                first_gates(0, 0, 0)
                with pe.Fori(0, 3) as i:
                    for par in range(2):
                        block_of(i * 2 + par, i, par)
                block_of(6, 3, 0)
                pe.wait_ge(l_sig, 30)
                gates(1, 1)

            def gla():
                pe.wait_ge(g_in, 48)
                pe.wait_ge(norm_s["lo"], tiles_before("nfin") + KT)
                for c in range(2):
                    for k in range(KT):
                        mm = pe.matmul(AUX[0:RANK, c, :], alow_w[:, k, :], X[:, k, c * 512:(c + 1) * 512],
                                       start=(k == 0), stop=(k == KT - 1))
                mm.then_inc(g_low, 1)
                pe.wait_ge(g_lowc, 1)
                for h in range(KV):
                    for c in range(2):
                        if h >= 2 and c == 0:
                            pe.wait_ge(g_abs, h - 1)
                            pe.wait_ge(g_min, h - 1)
                        mm = pe.matmul(AUX[:, 2 * (h % 2) + c, :], aup_w[:, h * P:(h + 1) * P], alow[:, c * 512:(c + 1) * 512],
                                       start=True, stop=True)
                    mm.then_inc(g_z, 1)
                pe.wait_ge(g_abs, KV)
                pe.wait_ge(g_min, KV)
                a0 = BASE["gla"]["act"]
                shift = 1 + a0 - START["gla"]

                def head(h, last=False):

                    def weights(step):
                        if step:
                            pe.wait_ge(g_dq, h * 7 + step)
                            pe.wait_ge(g_dk, h * 7 + step)
                            pe.wait_ge(g_keep, h * 7 + step)
                            q, k = dq, dk
                        else:
                            pe.wait_ge(evac["act"], h * 6 + (a0 + 4))
                            q, k = gq, gk
                        for b in range(NBLK):
                            cols = slice(b * P, (b + 1) * P)
                            mm = pe.matmul(AUX[:, b // 4, (b % 4) * P:(b % 4 + 1) * P], k[:, cols], q[:, cols],
                                           start=True, stop=True)
                        mm.then_inc(g_w, 1)

                    def turn_values(n):
                        pe.wait_ge(evac["act"], h * 6 + (a0 + 5 + n))
                        if n:
                            pe.wait_ge(g_vc, h * 2 + 1)
                        for b in range(NBLK):
                            tr = pe.transpose(AUX[:, 2 + b // 4, (b % 4) * P:(b % 4 + 1) * P], T[:, n, b * P:(b + 1) * P], ident)
                        tr.then_inc(g_vt, 1)

                    weights(0)
                    for q in range(64):
                        next_part(q % 16, h * 6 + (START["gla"] + 2 + q // 16), q // 16 % 2, shift)
                        if q + 1 in (11, 22, 33, 44, 54):
                            weights((q + 1) // 11 if q + 1 < 54 else 5)
                        if q + 1 == 24:
                            turn_values(0)
                        if q + 1 == 40:
                            turn_values(1)
                    weights(6)
                    pe.wait_ge(g_dk, h * 7 + 7)
                    pe.wait_ge(g_vc, h * 2 + 2)
                    for b in range(NBLK):
                        tr = pe.transpose(AUX[:, 2 + b // 4, (b % 4) * P:(b % 4 + 1) * P], dk[:, b * P:(b + 1) * P], ident)
                    tr.then_inc(g_kt, 1)
                    pe.wait_ge(g_kc, h + 1)
                    pe.wait_ge(g_keep, h * 7 + 7)
                    pe.wait_ge(g_dq, h * 7 + 7)
                    for c in range(S // CHUNK):
                        b, rows = c // 2, slice((c % 2) * CHUNK, (c % 2 + 1) * CHUNK)
                        if not last:
                            for q in range(2 * c, 2 * c + 2):
                                next_part(q % 16, h * 6 + (START["gla"] + 6 + q // 16), q // 16, shift)
                        if c >= 2:
                            pe.wait_ge(g_st, h * 16 + (c - 1))
                        pe.matmul(AUX[:, c % 2, 0:2 * P], ktok[rows, b, :], vtok[rows, b, :], start=True, stop=True)\
                          .then_inc(g_up, 1)
                        if c == 8:
                            pe.wait_ge(g_oc, h * 4 + 2)
                        at = (b % 4) * P
                        for d in range(2):
                            if c % 2 == 0:
                                pe.matmul(AUX[:, 2 + d, at:at + P], vtok[:, b, d * P:(d + 1) * P], wts[:, b, :],
                                          start=True, stop=False)
                            if d == 0 and c == 0:
                                pe.wait_ge(g_s0, h + 1)
                            elif d == 0:
                                pe.wait_ge(g_st, h * 16 + c)
                            mm = pe.matmul(AUX[:, 2 + d, at + (c % 2) * CHUNK:at + (c % 2 + 1) * CHUNK],
                                           state[:, c % 2, d * P:(d + 1) * P], dq[:, c * CHUNK:(c + 1) * CHUNK],
                                           start=False, stop=(c % 2 == 1))
                        if c % 8 == 7:
                            mm.then_inc(g_o, 1)
                    pe.wait_ge(g_st, h * 16 + 16)
                    pe.wait_ge(g_ss, h + 1)
                    for c in range(2):
                        mm = pe.matmul(AUX[:, c, :], ones, T[:, 0, c * 512:(c + 1) * 512], start=True, stop=True)
                    mm.then_inc(g_ssq, 1)
                    pe.wait_ge(g_var, h + 1)

                for n in range(2):
                    psum_waits("gla", n, n)
                    job(START["gla"] + n, n, Hhi, Hlo, None)
                with pe.Fori(0, KV - 1) as h:
                    head(h)
                head(KV - 1, last=True)

            def pool_group(g, par):
                if par == 0:
                    return
                pe.wait_ge(p_pool, g * 2 + 2)
                pe.wait_ge(p_m, g * 16 + 16)
                for m in range(2):
                    for c in range(2):
                        for k in range(2):
                            mm = pe.matmul(AUX[:, 2 * m + c, :], pool_m[:, k, m * P:(m + 1) * P],
                                           pooled[:, k, c * 512:(c + 1) * 512], start=(k == 0), stop=(k == 1))
                mm.then_inc(p_mm, 1)
                pe.wait_ge(p_used, g * 2 + 2)

            pe.wait_ge(tables, 32)
            sum_squares("nmem", MEM)
            pe.wait_ge(mem_ready, KT)
            mem_phase(0)
            sum_squares("nmix0", S)
            mem_phase(1)
            mem_attention(0)
            window()
            project_out(0)
            mlp(0)
            sum_squares("nmix1", S)
            mem_attention(1)
            lru()
            project_out(1)
            mlp(1)
            sum_squares("nfin", S)
            gla()
            jobs("pool", 8, Hhi, Hlo, None, after=pool_group)
            jobs("gate_b", 8, Hhi, Hlo, None)
            jobs("merge", 16, Hhi, Hlo, None)
            jobs("proj_a", 8, Hhi, Hlo, (s_lo, 0))
            jobs("proj_b", 8, Hhi, Hlo, (s_lo, 8))
            jobs("out", 8, Uhi, Ulo, (s_lo, 16))
            for done, out_sem in ((n_sum, n_mean), (n_acc, n_ssq)):
                pe.wait_ge(done, KT)
                for c in range(2):
                    mm = pe.matmul(AUX[:, c, :], ones, ln_acc[:, c * 512:(c + 1) * 512], start=True, stop=True)
                mm.then_inc(out_sem, 1)

        @block.scalar
        def _(act):
            chain = Chain(act, act_chain)
            act.dma_start(vecs[:], vec).then_inc(tables, 16)
            act.dma_start(cst[:], const).then_inc(tables, 16)
            act.dma_start(mraw[:], memT).then_inc(mem_in, 16)
            act.dma_start(X[:], xT).then_inc(x_loaded, 16)
            act.nop().then_inc(evac["act"], 2)
            act.wait_ge(tables, 32)

            def square(name, k, src, width=S):
                if k >= 2:
                    act.wait_ge(norm_s["acc"], KT * NORMS.index(name) + k - 1)
                act.activation(squares[:, k % 2, 0:width], src[:, k, :], ACT.Square).then_inc(norm_s["sq"], 1)

            def root(name, width=S):
                act.wait_ge(norm_s["ssq"], NORMS.index(name) + 1)
                act.activation(rstd[:, 0:width], sums(width), ACT.Sqrt, bias=eps_col, scale=1.0 / D).then_inc(norm_s["r"], 1)

            def high(name, k):
                act.wait_ge(norm_s["t"], tiles_before(name) + k + 1)
                act.copy(Hhi[:, k, :], T[:, k % 2, :]).then_inc(norm_s["hi"], 1)

            def norm(name, phase):
                for k in range(KT):
                    act.wait_ge(evac["dve"], 3 + BASE[phase]["dve"] + k)
                    square(name, k, X)
                root(name)
                for k in range(KT):
                    high(name, k)

            def empty(n, par, dst, width=S):
                wait_apart(act, job_done, n + 1)
                act.copy(dst, G[:, par, 0:width]).then_inc(evac["act"], 1)

            def start():
                act.wait_ge(mem_in, 16)
                for k in range(KT):
                    square("nmem", k, mraw, MEM)
                root("nmem", MEM)
                for m in range(4):
                    empty(START["mem0"] + m, m % 2, MK[:, m, :], MEM)
                act.wait_ge(x_loaded, 16)
                for m in range(4):
                    empty(START["mem0"] + 4 + m, m % 2, MT[:, m % 2, :], MEM)
                    square("nmix0", 2 * m, X)
                    square("nmix0", 2 * m + 1, X)
                root("nmix0")
                for k in range(KT):
                    empty(START["mem1"] + k, k % 2, MK1[:, k, :] if k < 4 else MT[:, k % 2, :], MEM)
                    high("nmix0", k)
                act.wait_ge(mvc, 8)
                act.wait_ge(evac["act"], 2 + MEM_JOBS)
                act.dma_start(kv_tiles[0], MK1[:].rearrange("p a n -> p (a n)")).then_inc(kv_saved, 16)
                act.dma_start(kv_tiles[1], MV1[:].rearrange("p t a n -> p (t a n)")).then_inc(kv_saved, 16)

            def attention(s, i, par, subs, nk, dst, scale, sink=None):
                U = NBLK * subs

                def exp(u):
                    if u >= 2:
                        act.wait_ge(s["pt"], i * U + (u - 1))
                    if u >= 4:
                        act.wait_ge(s["os"], i * U + (u - 3))
                    wait_apart(act, s["mx"], i * U + (u + 1))
                    t = u % 4
                    negm = stat[:, 4 + t:5 + t]
                    if sink:
                        act.activation(stat[:, 12 + t:13 + t], sink(u % subs), ACT.Exp, bias=negm)
                        src = probs[:, u % 2, :]
                    else:
                        src = scored(par, u, nk * P)
                    act.activation(probs[:, u % 2, 0:nk * P], src, ACT.Exp, bias=negm, scale=scale,
                                   accum_out=stat[:, 8 + t:9 + t]).then_inc(s["pr"], 1)

                def copies(u):
                    act.wait_ge(s["pt"], i * U + (u + 1))
                    if u >= 2:
                        act.wait_ge(s["pv"], i * U + (u - 1))
                    act.copy(probsT[:, u % 2, 0:nk * P], AUX[:, 2, 0:nk * P]).then_inc(s["pc"], 1)

                def result(b):
                    wait_apart(act, s["ot"], i * NBLK + (b + 1))
                    act.copy(dst(b), G[:, par, 512:512 + P]).then_inc(s["oc"], 1)

                exp(0)
                for u in range(U):
                    if u + 1 < U:
                        exp(u + 1)
                    copies(u)
                    if u >= 2 and (u - 1) % subs == 0:
                        result((u - 2) // subs)
                if (U - 2) % subs == subs - 1:
                    result((U - 2) // subs)
                result(NBLK - 1)

            def mem_attention(l):
                name = f"mq{l}"
                with act.Fori(0, 2) as i:
                    for par in range(2):
                        head = i * 2 + par
                        empty(i * 2 + (START[name] + par), par, T[:, 0, :])
                        attention(attns["am"], head + MEM_HEADS * l, par, 1, 2,
                                  lambda b: mo[:, bass.ds(head, 1), b * P:(b + 1) * P].rearrange("p a n -> p (a n)"),
                                  MEM_SCALE)

            def window():
                act.wait_ge(kv_saved, 32)
                for n, t in enumerate((sin, cos)):
                    act.wait_ge(trig, n + 1)
                    chain.link(act.activation(t[:], t[:], ACT.Sin))
                for par in range(2):
                    empty(START["k"] + par, par, T[:, 0, :])
                    for h in range(2):
                        act.wait_ge(kdup, 2 * par + h + 1)
                        act.copy(keys[:, 2 * par + h, P:P + S], AUX[:, 0:2, :].rearrange("p a n -> p (a n)"))\
                           .then_inc(kcopied, 1)
                for par in range(2):
                    if par:
                        act.wait_ge(vt, par)
                    empty(START["v"] + par, par, T[:, 0, :])
                act.wait_ge(vt, 2)
                with act.Fori(0, KV) as g:
                    for par in range(2):
                        empty(g * 2 + (START["q"] + par), par, T[:, 0, :])
                        attention(attns["aw"], g * 2 + par, par, 2, 3,
                                  lambda b: mixed[:, bass.ds(g * 2 + par, 1), b * P:(b + 1) * P].rearrange("p a n -> p (a n)"),
                                  SINK_SCALE, lambda h: dcol("sinks", g * 4 + (2 * par + h)))

            def project_out(l):
                if l == 0:
                    act.wait_ge(attns["aw"]["oc"], KT * NBLK)
                act.wait_ge(attns["am"]["oc"], (l + 1) * MEM_HEADS * NBLK)
                if l == 0:
                    act.dma_start(MK[:].rearrange("p a n -> p (a n)"), kv_tiles[0]).then_inc(kv_in, 16)
                    act.dma_start(MV[:].rearrange("p t a n -> p (t a n)"), kv_tiles[1]).then_inc(kv_in, 16)
                for k in range(KT):
                    act.copy(Hhi[:, k, :], mixed[:, k, :]).then_inc(split_hi[l], 1)
                for k in range(MEM_HEADS):
                    act.copy(MOhi[:, k, :], mo[:, k, :]).then_inc(split_hi[l], 1)
                act.wait_ge(split_lo[l], KT + MEM_HEADS)
                act.dma_start(X[:], xT if l == 0 else scratch[0]).then_inc(x_back[l], 16)

            def mlp(l):
                norm(f"nmlp{l}", f"wo_mem{l}")
                n0 = START[f"up{l}0"]
                with act.Fori(0, 4) as c:
                    with act.Fori(0, 4) as i:
                        for par in range(2):
                            n = c * 8 + i * 2 + par
                            act.wait_ge(job_done, c * 16 + i * 2 + (n0 + par + 1))
                            if par == 0:
                                act.wait_ge(up_lo[l], n)
                            act.activation(T[:, par, :], G[:, par, :], ACT.Relu).then_inc(evac["act"], 1)
                            wait_apart(act, evac["act"], c * 8 + i * 2 + (3 + BASE[f"up{l}0"]["act"] + par))
                            act.activation(Uhi[:, bass.ds(i * 2 + par, 1), :].rearrange("p a n -> p (a n)"), T[:, par, :],
                                           ACT.Square).then_inc(up_hi[l], 1)

            def lru():
                act.wait_ge(l_dec, 1)
                act.activation(decay_c[:, 16:32], decay_c[:, 0:16], ACT.Exp, scale=-1.0).then_inc(l_de, 1)
                def input_of(j, par):
                    wait_apart(act, job_done, j * 2 + (START["lru"] + 1))
                    act.copy(xb[:, 1:S + 1], G[:, 0, :]).then_inc(evac["act"], 1)
                    block = lru_w[j] if isinstance(j, int) else lru_w[bass.ds(j, 1)].rearrange("a p g n -> (a p) g n")
                    act.dma_start(lw[:, par], block).then_inc(lw_in[par], 16)

                def block_of(j, par, last=False):
                    wait_apart(act, job_done, j * 2 + (START["lru"] + 2))
                    act.activation(gl[:], G[:, 1, :], ACT.Gelu_apprx_tanh).then_inc(evac["act"], 1)
                    for dr in range(2):
                        wait_apart(act, l_mm, j * 2 + (dr + 1))
                        for g, (dst, b) in enumerate(((rg, "lru_ba"), (ig, "lru_bx"))):
                            act.activation(dst[:, dr], AUX[:, 2 * g:2 * g + 2, :].rearrange("p a n -> p (a n)"),
                                           ACT.Sigmoid, bias=dcol(b, j + 8 * dr)).then_inc(l_sig, 1)
                    if not last:
                        input_of(j + 1, 1 - par)
                    wait_apart(act, l_sig, j * 4 + 4)
                    for dr in range(2):
                        c = decay_c[:, bass.ds(j + (80 + 8 * dr), 1)]
                        act.activation(av[:, dr], rg[:, dr], ACT.Exp, scale=c).then_inc(l_exp, 1)
                        act.activation(rg[:, dr], rg[:, dr], ACT.Tanh, scale=c).then_inc(l_exp, 1)
                    for dr in range(2):
                        act.wait_ge(l_e, j * 2 + (dr + 1))
                        act.activation(T[:, dr], T[:, dr], ACT.Sqrt, scale=-1.0).then_inc(l_sq, 1)
                    act.wait_ge(l_y, j + 1)

                input_of(0, 0)
                with act.Fori(0, 3) as i:
                    for par in range(2):
                        block_of(i * 2 + par, par)
                block_of(6, 0)
                block_of(7, 1, last=True)

            def gla():
                act.wait_ge(job_done, START["gla"])
                act.dma_start(pmask[:], pair_masks).then_inc(g_in, 16)
                act.dma_start(alow_w[:], alpha_w).then_inc(g_in, 16)
                act.dma_start(aup_w[:], alpha_up).then_inc(g_in, 16)
                act.wait_ge(g_low, 1)
                act.copy(alow[:], AUX[0:RANK, 0:2, :].rearrange("p a n -> p (a n)")).then_inc(g_lowc, 1)
                for h in range(KV):
                    act.wait_ge(g_z, h + 1)
                    if h:
                        act.wait_ge(g_zero, h)
                    act.activation(T[:, 1, :], AUX[:, 2 * (h % 2):2 * (h % 2) + 2, :].rearrange("p a n -> p (a n)"),
                                   ACT.Abs, bias=vcol("b_alpha", h)).then_inc(g_abs, 1)
                    act.wait_ge(g_abs, h + 1)
                    chain.link(act.activation(T[:, 1, :], T[:, 1, :], ACT.Exp, scale=-1.0))
                    chain.link(act.activation(T[:, 1, :], T[:, 1, :], ACT.Ln, bias=1.0))
                act.wait_ge(g_zero, KV)
                act.wait_ge(x2_saved, 16)
                def queries(n0):
                    act.wait_ge(job_done, n0 + 1)
                    act.activation(gq[:], G[:, 0, :], ACT.Copy, scale=P ** -0.5).then_inc(evac["act"], 1)
                    empty(n0 + 1, 1, gk[:])

                def head(h, last=False):
                    n0 = h * 6 + START["gla"]
                    head = gsum[:, bass.ds(h, 1), :].rearrange("p a n -> p (a n)")

                    def decay(step):
                        act.wait_ge(g_diff, h * 7 + step)
                        if step < 7:
                            chain.link(act.activation(dec[:], dec[:], ACT.Abs))
                        act.activation(dec[:], dec[:], ACT.Exp, scale=-1.0 / TAU).then_inc(g_exp, 1)

                    def values(n):
                        act.wait_ge(g_vt, h * 2 + (n + 1))
                        act.copy(vtok[:, :, n * P:(n + 1) * P], AUX[:, 2:4, :].rearrange("p a (b n) -> p (a b) n", n=P))\
                           .then_inc(g_vc, 1)

                    def gate(n):
                        wait_apart(act, job_done, n0 + (5 + n))
                        act.activation(ya[:, bass.ds(h * 2 + n, 1), :].rearrange("p a n -> p (a n)"), G[:, n, :], ACT.Silu)\
                           .then_inc(evac["act"], 1)

                    decay(1)
                    decay(2)
                    empty(n0 + 2, 0, T[:, 0, :])
                    decay(3)
                    act.wait_ge(g_y, h)
                    values(0)
                    empty(n0 + 3, 1, T[:, 1, :])
                    decay(4)
                    values(1)
                    decay(5)
                    gate(0)
                    decay(6)
                    gate(1)
                    decay(7)
                    act.wait_ge(g_kt, h + 1)
                    act.copy(ktok[:], AUX[:, 2:4, :].rearrange("p a (b n) -> p (a b) n", n=P)).then_inc(g_kc, 1)
                    wait_apart(act, g_dk, h * 7 + 7)
                    act.activation(chunk_decay[:], gsum[:, bass.ds(h, 1), CHUNK - 1::CHUNK].rearrange("p a n -> p (a n)"),
                                   ACT.Exp, scale=1.0 / TAU).then_inc(g_cd, 1)
                    act.activation(dec[:], head, ACT.Exp, scale=1.0 / TAU).then_inc(g_exp, 1)
                    act.wait_ge(g_dq, h * 7 + 7)
                    for half in range(2):
                        act.wait_ge(g_o, h * 2 + (half + 1))
                        for d in range(2):
                            act.copy(results[:, half, d, :], AUX[:, 2 + d, :]).then_inc(g_oc, 1)
                    if not last:
                        queries(n0 + 6)
                    act.wait_ge(g_oc, h * 4 + 4)
                    for d in range(2):
                        act.activation(T[:, d, :].rearrange("p (a n) -> p a n", a=2), results[:, :, d, :], ACT.Square)\
                           .then_inc(g_sq, 1)
                    act.wait_ge(g_var, h + 1)
                    act.activation(dec[:], dec[:], ACT.Sqrt).then_inc(g_r, 1)

                queries(START["gla"])
                with chain.loop(KV - 1, 6) as h:
                    head(h)
                chain.turn = None
                head(KV - 1, last=True)
                act.wait_ge(g_y, KV)

            def pooling():
                act.dma_start(inv_cnt[:], inv_count).then_inc(p_in, 16)
                with act.Fori(0, KV) as g:
                    act.dma_start(pool_m[:], pool_w[bass.ds(g, 1)].rearrange("a p k n -> (a p) k n")).then_inc(p_m, 16)
                    for par in range(2):
                        empty(g * 2 + (START["pool"] + par), par, T[:, par, :])
                    for m in range(2):
                        wait_apart(act, p_mm, g + 1)
                        act.activation(yb[:, bass.ds(g * 2 + m, 1), :].rearrange("p a n -> p (a n)"),
                                       AUX[:, 2 * m:2 * m + 2, :].rearrange("p a n -> p (a n)"),
                                       ACT.Copy, scale=dcol("pool_scale", g * 2 + m)).then_inc(p_used, 1)
                    act.wait_ge(p_used, g * 2 + 2)

            def gates():
                with act.Fori(0, 4) as i:
                    for par in range(2):
                        act.wait_ge(b_y, i * 2)
                        act.wait_ge(job_done, i * 2 + (START["gate_b"] + par + 1))
                        act.activation(T[:, par, :], G[:, par, :], ACT.Silu).then_inc(evac["act"], 1)
                act.wait_ge(b_y, 8)
                with act.Fori(0, 8) as i:
                    for par in range(2):
                        act.wait_ge(gates_out[par], i * 16)
                        wait_apart(act, job_done, i * 2 + (START["merge"] + par + 1))
                        act.activation(T[:, par, :], G[:, par, :], ACT.Sigmoid, bias=dcol("b_merge", i * 2 + par))\
                           .then_inc(evac["act"], 1)
                        act.wait_ge(evac["act"], i * 2 + (BASE["merge"]["act"] + par + 3))
                        act.dma_start(gate_tiles[bass.ds(i * 2 + par, 1)].rearrange("a p n -> (a p) n"),
                                      T[:, par, :]).then_inc(gates_out[par], 16)
                for par in range(2):
                    act.wait_ge(gates_out[par], 128)

            def projections():
                act.wait_ge(job_done, START["proj_a"])
                for n, src in enumerate((ya, yb)):
                    if n:
                        act.wait_ge(job_done, START["proj_b"])
                    for par in range(2):
                        if n:
                            act.wait_ge(merged, 8)
                        act.dma_start(T[:, par, :], gate_tiles[8 * n + par]).then_inc(gates_in[par], 16)
                    for k in range(KT):
                        act.copy(Hhi[:, k, :], src[:, k, :]).then_inc(s_hi, 1)
                    with act.Fori(0, 3) as i:
                        for par in range(2):
                            act.wait_ge(merged, i * 2 + (8 * n + par + 1))
                            act.dma_start(T[:, par, :], gate_tiles[bass.ds(i * 2 + (8 * n + 2 + par), 1)]
                                          .rearrange("a p n -> (a p) n")).then_inc(gates_in[par], 16)
                for k in range(KT):
                    act.wait_ge(merged, 8 + k + 1)
                    act.copy(Uhi[:, k, :], ya[:, k, :]).then_inc(s_hi, 1)
                act.wait_ge(job_done, START["out"])
                act.dma_start(X2[:], scratch[0]).then_inc(x2_back, 16)

            def layer_norm():
                for k in range(KT):
                    act.wait_ge(n_cent, k + 1)
                    if k >= 2:
                        act.wait_ge(n_acc, k - 1)
                    act.activation(T[:, k % 2, :], X2[:, k, :], ACT.Square).then_inc(n_sq, 1)
                act.wait_ge(n_ssq, 1)
                act.activation(ln_stat[:], sums(S), ACT.Sqrt, bias=stat[:, 31:32], scale=1.0 / D).then_inc(n_r, 1)
                for k in range(KT):
                    act.wait_ge(n_y, k + 1)
                    act.dma_start(out[:, k, :], X2[:, k, :]).then_inc(out_done, 16)

            start()
            act.wait_ge(norm_s["lo"], tiles_before("nmix0") + KT)
            act.dma_start(wmask[:], masks).then_inc(masks_in, 16)
            act.dma_start(sin[:].bitcast(I32), pos).then_inc(pos_in, 16)
            mem_attention(0)
            window()
            project_out(0)
            mlp(0)
            norm("nmix1", "down03")
            act.dma_start(scratch[0], X[:]).then_inc(x_saved, 16)
            act.wait_ge(norm_s["lo"], tiles_before("nmix1") + KT)
            act.wait_ge(x_saved, 16)
            mem_attention(1)
            lru()
            project_out(1)
            mlp(1)
            norm("nfin", "down13")
            act.wait_ge(norm_s["lo"], tiles_before("nfin") + KT)
            act.dma_start(scratch[0], X[:]).then_inc(x2_saved, 16)
            gla()
            pooling()
            gates()
            projections()
            layer_norm()
            act.wait_ge(out_done, 16 * KT)

        @block.vector
        def _(dve):
            chain = Chain(dve, dve_chain)
            dve.nop().then_inc(evac["dve"], 2)
            dve.memset(eps_col, EPS)
            dve.memset(stat[:, 31:32], EPS_2)
            dve.wait_ge(tables, 32)

            def add_square(name, k, width=S):
                r = KT * NORMS.index(name)
                dve.wait_ge(norm_s["sq"], r + k + 1)
                if k == 0:
                    dve.tensor_copy(acc[:, 0:width], squares[:, 0, 0:width]).then_inc(norm_s["acc"], 1)
                else:
                    dve.tensor_tensor(acc[:, 0:width], acc[:, 0:width], squares[:, k % 2, 0:width], ALU.add)\
                       .then_inc(norm_s["acc"], 1)
                dve.wait_ge(norm_s["acc"], r + k + 1)

            def invert(name, width=S):
                r = NORMS.index(name)
                dve.wait_ge(norm_s["r"], r + 1)
                dve.reciprocal(rstd[:, 0:width], rstd[:, 0:width]).then_inc(norm_s["var"], 1)
                dve.wait_ge(norm_s["var"], r + 1)

            def split_norm(name, gain, inplace=False, also=None):
                s, r = norm_s, tiles_before(name)

                def scaled(k):
                    if k >= 2:
                        dve.wait_ge(s["lo"], r + k - 1)
                    if inplace:
                        chain.link(dve.scalar_tensor_tensor(X[:, k, :], X[:, k, :], gain(k), rstd[:], ALU.mult, ALU.mult))
                        dve.tensor_copy(T[:, k % 2, :], X[:, k, :]).then_inc(s["t"], 1)
                    else:
                        dve.scalar_tensor_tensor(T[:, k % 2, :], X[:, k, :], gain(k), rstd[:], ALU.mult, ALU.mult)\
                           .then_inc(s["t"], 1)

                scaled(0)
                for k in range(KT):
                    if k + 1 < KT:
                        scaled(k + 1)
                    if also:
                        also(k)
                    dve.wait_ge(s["hi"], r + k + 1)
                    dve.tensor_tensor(Hlo[:, k, :], T[:, k % 2, :], Hhi[:, k, :], ALU.subtract).then_inc(s["lo"], 1)

            def norm(name, gain, inplace=False):
                invert(name)
                split_norm(name, gain, inplace)

            def start():
                for k in range(KT):
                    add_square("nmem", k, MEM)
                invert("nmem", MEM)
                for k in range(KT):
                    dve.scalar_tensor_tensor(mraw[:, k, :], mraw[:, k, :], vcol("mem_norm", k), rstd[:, 0:MEM],
                                             ALU.mult, ALU.mult).then_inc(mem_ready, 1)

                def values(dst, m, turn):
                    dve.wait_ge(mvt, turn + 1)
                    dve.tensor_copy(dst[:, :, m, :], AUX[:, 2, 0:MEM].rearrange("p (t n) -> p t n", t=2)).then_inc(mvc, 1)

                for m in range(4):
                    add_square("nmix0", 2 * m)
                    add_square("nmix0", 2 * m + 1)
                    values(MV, m, m)
                invert("nmix0")
                split_norm("nmix0", lambda k: vcol("mix_norm", k), also=lambda k: values(MV1, k - 4, k) if k >= 4 else None)

            def attention(s, i, par, subs, nk, scale, sink, turns):
                U = NBLK * subs
                dim = P // subs

                def peak(u):
                    t = u % 4
                    mx, negm = stat[:, t:t + 1], stat[:, 4 + t:5 + t]
                    if sink and u >= 2:
                        dve.wait_ge(s["pt"], i * U + (u - 1))
                    wait_apart(dve, s["sc"], i * U + (u + 1))
                    if sink:
                        m = {0: 0, NBLK - 1: 2}.get(u // subs, 1)
                        chain.link(dve.tensor_tensor_reduce(probs[:, u % 2, :], scored(par, u, nk * P), wmask[:, m, :],
                                                            1.0, -3e38, ALU.add, ALU.max, mx))
                        dve.tensor_scalar(negm, mx, -scale, stat[:, 20 + u % subs:21 + u % subs], ALU.mult, ALU.min)\
                           .then_inc(s["mx"], 1)
                    else:
                        chain.link(dve.reduce_max(mx, scored(par, u, nk * P), AX_X))
                        dve.tensor_scalar(negm, mx, -scale, None, ALU.mult).then_inc(s["mx"], 1)

                def scale_out(u):
                    b, h = u // subs, u % subs
                    dve.wait_ge(s["pr"], i * U + (u + 1))
                    t = u % 4
                    total = stat[:, 8 + t:9 + t]
                    if sink:
                        chain.link(dve.tensor_tensor(total, total, stat[:, 12 + t:13 + t], ALU.add))
                    inv = stat[:, 16 + t:17 + t]
                    chain.link(dve.reciprocal(inv, total))
                    dve.wait_ge(s["pv"], i * U + (u + 1))
                    if b >= 2:
                        dve.wait_ge(s["ot"], i * NBLK + (b - 1))
                    dve.tensor_scalar(O_sb[:, b % 2, h * dim:(h + 1) * dim], AUX[:, 3, 0:dim],
                                      inv, None, ALU.mult).then_inc(s["os"], 1)

                if sink:
                    for h in range(subs):
                        chain.link(dve.tensor_scalar(stat[:, 20 + h:21 + h], sink(h), -1.0, None, ALU.mult))
                peak(0)
                peak(1)
                for u in range(U):
                    if u:
                        scale_out(u - 1)
                    if u + 2 < U:
                        peak(u + 2)
                scale_out(U - 1)

            def mem_attention(l):
                with chain.loop(2, 2 * NBLK * 2) as i:
                    for par in range(2):
                        attention(attns["am"], i * 2 + (par + MEM_HEADS * l), par, 1, 2, MEM_SCALE, None, None)

            def angles():
                dve.wait_ge(pos_in, 16)
                dve.wait_ge(masks_in, 16)
                turn = 2 * np.pi
                c1 = 6.28125
                c2 = float((np.array(turn - c1, np.float32).view(np.uint32) & np.uint32(0xFFFFF000)).view(np.float32))
                c3 = float(np.float32(turn - c1 - c2))
                big = 1.5 * 2.0 ** 23
                a, k = T[:, 0, :], T[:, 1, :]
                chain.link(dve.tensor_copy(k, sin[:].bitcast(I32)))
                chain.link(dve.tensor_scalar(a, k, freq, None, ALU.mult))
                for n, (t, quarter) in enumerate(((sin, 0.0), (cos, 0.25))):
                    chain.link(dve.tensor_scalar(k, a, float(1.0 / turn), quarter, ALU.mult, ALU.add))
                    chain.link(dve.tensor_scalar(k, k, big, None, ALU.add))
                    chain.link(dve.tensor_scalar(k, k, -big, None, ALU.add))
                    chain.link(dve.scalar_tensor_tensor(t[:], k, -c1, a, ALU.mult, ALU.add))
                    chain.link(dve.scalar_tensor_tensor(t[:], k, -c2, t[:], ALU.mult, ALU.add))
                    chain.link(dve.scalar_tensor_tensor(t[:], k, -c3, t[:], ALU.mult, ALU.add))
                    chain.link(dve.tensor_scalar(t[:], t[:], float(quarter * turn), float(np.float32(3.1415925)), ALU.add, ALU.min))
                    dve.tensor_scalar(t[:], t[:], -float(np.float32(3.1415925)), None, ALU.max).then_inc(trig, 1)
                    dve.wait_ge(trig, n + 1)

            def rotate(r, heads=False):
                dve.wait_ge(rot_sw, r + 1)
                chain.link(dve.tensor_tensor(T[:, 1, :], AUX[:, 0:2, :].rearrange("p a n -> p (a n)"), sin[:], ALU.mult))
                chain.link(dve.tensor_tensor(T[:, 0, :], T[:, 0, :], cos[:], ALU.mult))
                if not heads:
                    dve.tensor_tensor(T[:, 0, :], T[:, 0, :], T[:, 1, :], ALU.add).then_inc(rot_ok, 1)
                    return
                chain.link(dve.tensor_tensor(T[:, 0, :], T[:, 0, :], T[:, 1, :], ALU.add))
                at = CCOLS["half"]
                chain.link(dve.tensor_scalar(T[:, 1, :], T[:, 0, :], cst[:, at + 1:at + 2], None, ALU.mult))
                dve.tensor_scalar(T[:, 0, :], T[:, 0, :], cst[:, at:at + 1], None, ALU.mult).then_inc(rot_ok, 1)

            def window():
                dve.wait_ge(act_chain, 2)
                for r in range(2):
                    rotate(r)
                dve.wait_ge(rot_ok, 2)
                for par in range(2):
                    dve.wait_ge(vt, par + 1)
                    dve.tensor_copy(vals[:, 1:NBLK + 1, par * P:(par + 1) * P],
                                    AUX[:, 0:2, :].rearrange("p a (b n) -> p (a b) n", n=P)).then_inc(vcopied, 1)
                with chain.loop(KV, 2 * (4 + 2 + 16 * 3)) as g:
                    for par in range(2):
                        rotate(g * 2 + (2 + par), True)
                        attention(attns["aw"], g * 2 + par, par, 2, 3, SINK_SCALE,
                                  lambda h: dcol("sinks", g * 4 + (2 * par + h)), None)

            def add_last_to_x(phase, name):
                for m in range(KT):
                    dve.wait_ge(job_done, START[phase] + m + 1)
                    dve.tensor_tensor(X[:, m, :], G[:, m % 2, :], X[:, m, :], ALU.add).then_inc(evac["dve"], 1)
                    if m:
                        add_square(name, m - 1)
                add_square(name, KT - 1)
                dve.wait_ge(evac["dve"], 2 + BASE[phase]["dve"] + KT)

            def add_to_x(name):
                with dve.Fori(0, 4) as i:
                    for par in range(2):
                        m = i * 2 + par
                        dve.wait_ge(job_done, i * 2 + (START[name] + par + 1))
                        xm = X[:, bass.ds(m, 1), :].rearrange("p a n -> p (a n)")
                        dve.tensor_tensor(xm, G[:, par, :], xm, ALU.add).then_inc(evac["dve"], 1)

            def project_out(l):
                for k in range(KT):
                    dve.wait_ge(split_hi[l], k + 1)
                    dve.tensor_tensor(Hlo[:, k, :], mixed[:, k, :], Hhi[:, k, :], ALU.subtract).then_inc(split_lo[l], 1)
                for k in range(MEM_HEADS):
                    dve.wait_ge(split_hi[l], KT + k + 1)
                    dve.tensor_tensor(MOlo[:, k, :], mo[:, k, :], MOhi[:, k, :], ALU.subtract).then_inc(split_lo[l], 1)
                dve.wait_ge(x_back[l], 16)
                add_to_x(f"wo_mixed{l}")
                dve.wait_ge(evac["dve"], 2 + BASE[f"wo_mem{l}"]["dve"])
                add_last_to_x(f"wo_mem{l}", f"nmlp{l}")

            def mlp(l):
                norm(f"nmlp{l}", lambda k: vcol("mlp_norm", 8 * l + k))
                n0 = START[f"up{l}0"]
                a0, d0 = BASE[f"up{l}0"]["act"], BASE[f"up{l}0"]["dve"]

                def chunk(c):
                    with dve.Fori(0, 4) as i:
                        for par in range(2):
                            dve.wait_ge(evac["act"], i * 2 + c * 8 + (a0 + par + 3))
                            dve.wait_ge(up_hi[l], i * 2 + c * 8 + (par + 1))
                            dve.tensor_tensor(T[:, par, :], T[:, par, :], T[:, par, :], ALU.mult).then_inc(up_sq[l], 1)
                            dve.wait_ge(up_sq[l], i * 2 + c * 8 + (par + 1))
                            m = bass.ds(i * 2 + par, 1)
                            dve.tensor_tensor(Ulo[:, m, :].rearrange("p a n -> p (a n)"), T[:, par, :],
                                              Uhi[:, m, :].rearrange("p a n -> p (a n)"), ALU.subtract).then_inc(up_lo[l], 1)

                with dve.Fori(0, 3) as c:
                    chunk(c)
                    with dve.Fori(0, 4) as i:
                        for par in range(2):
                            dve.wait_ge(job_done, c * 16 + i * 2 + (n0 + 8 + par + 1))
                            xm = X[:, bass.ds(i * 2 + par, 1), :].rearrange("p a n -> p (a n)")
                            dve.tensor_tensor(xm, G[:, par, :], xm, ALU.add).then_inc(evac["dve"], 1)
                    dve.wait_ge(evac["dve"], c * 8 + (d0 + 8 + 2))
                chunk(3)
                add_last_to_x(f"down{l}3", "nmix1" if l == 0 else "nfin")

            def lru():
                lam = vecs[:, VCOLS["lam"]:VCOLS["lam"] + 16]
                e, z, z2, s = (decay_c[:, 16 * n:16 * n + 16] for n in (1, 2, 3, 4))
                c = decay_c[:, 80:96]
                dve.tensor_scalar(s, lam, -1.0, None, ALU.mult).then_inc(l_dx, 1)
                dve.wait_ge(l_dx, 1)
                dve.tensor_tensor(decay_c[:, 0:16], lam, s, ALU.max).then_inc(l_dec, 1)
                chain.link(dve.tensor_scalar(c, s, 0.0, None, ALU.max))
                dve.wait_ge(l_de, 1)
                chain.link(dve.tensor_scalar(z, e, 2.0, None, ALU.add))
                chain.link(dve.reciprocal(z, z))
                chain.link(dve.tensor_tensor(z, z, e, ALU.mult))
                chain.link(dve.tensor_tensor(z2, z, z, ALU.mult))
                chain.link(dve.memset(s, 1.0 / 19))
                for n in range(8, -1, -1):
                    chain.link(dve.tensor_tensor(s, s, z2, ALU.mult))
                    chain.link(dve.tensor_scalar(s, s, 1.0 / (2 * n + 1), None, ALU.add))
                chain.link(dve.tensor_tensor(s, s, z, ALU.mult))
                chain.link(dve.scalar_tensor_tensor(c, s, 2.0, c, ALU.mult, ALU.add))
                dve.tensor_scalar(c, c, -8.0, None, ALU.mult).then_inc(l_dx, 1)
                dve.wait_ge(l_dx, 2)
                dve.wait_ge(pads, 2)

                def convolve(j, par):
                    dve.wait_ge(evac["act"], j * 2 + (BASE["lru"]["act"] + 3))
                    x = xc[par][:]
                    chain.link(dve.tensor_scalar(x, xb[:, 0:S], dcol("conv_w", j), dcol("conv_b", j), ALU.mult, ALU.add))
                    for tap in range(1, 4):
                        ins = dve.scalar_tensor_tensor(x, xb[:, tap:tap + S], dcol("conv_w", j + 8 * tap), x, ALU.mult, ALU.add)
                        if tap < 3:
                            chain.link(ins)
                        else:
                            ins.then_inc(l_xc, 1)

                def block_of(j, par, last=False):
                    if not last:
                        convolve(j + 1, 1 - par)
                    for dr in range(2):
                        dve.wait_ge(l_exp, j * 4 + (2 * dr + 2))
                        dve.wait_ge(l_a2, j * 2 + (dr + 1))
                        dve.scalar_tensor_tensor(T[:, dr], T[:, dr], 1.0, rg[:, dr], ALU.add, ALU.mult).then_inc(l_e, 1)
                    for dr in range(2):
                        dve.wait_ge(l_sq, j * 2 + (dr + 1))
                        dve.wait_ge(l_ix, j * 2 + (dr + 1))
                        chain.link(dve.tensor_tensor(ig[:, dr], ig[:, dr], T[:, dr], ALU.mult))
                        if dr == 0:
                            chain.link(dve.tensor_tensor_scan(rg[:, 0], av[:, 0], ig[:, 0], 0.0, ALU.mult, ALU.add))
                        else:
                            chain.link(dve.tensor_tensor_scan(rg[:, 1, ::-1], av[:, 1, ::-1], ig[:, 1, ::-1], 0.0,
                                                              ALU.mult, ALU.add))
                    dve.tensor_tensor(rg[:, 0], rg[:, 0], rg[:, 1], ALU.add).then_inc(l_h, 1)
                    dve.wait_ge(l_h, j + 1)
                    dve.wait_ge(evac["act"], j * 2 + (BASE["lru"]["act"] + 4))
                    dve.tensor_tensor(mixed[:, bass.ds(j, 1), :].rearrange("p a n -> p (a n)"), rg[:, 0], gl[:], ALU.mult)\
                       .then_inc(l_y, 1)

                convolve(0, 0)
                with chain.loop(3, 14) as i:
                    for par in range(2):
                        block_of(i * 2 + par, par)
                block_of(6, 0)
                block_of(7, 1, last=True)
                dve.wait_ge(l_y, 8)

            def gla():
                dve.wait_ge(job_done, START["gla"])
                chain.link(dve.memset(starts[:], 1.0))
                chain.link(dve.memset(starts[:, ::CHUNK], 0.0))
                for h in range(KV):
                    dve.wait_ge(g_abs, h + 1)
                    dve.tensor_scalar(T[:, 0, :], AUX[:, 2 * (h % 2):2 * (h % 2) + 2, :].rearrange("p a n -> p (a n)"),
                                      vcol("b_alpha", h), 0.0, ALU.add, ALU.min).then_inc(g_min, 1)
                    dve.wait_ge(g_min, h + 1)
                    dve.wait_ge(act_chain, 2 + 2 * (h + 1))
                    chain.link(dve.tensor_tensor(T[:, 0, :], T[:, 0, :], T[:, 1, :], ALU.subtract))
                    dve.tensor_tensor_scan(gsum[:, h, :], starts[:], T[:, 0, :], 0.0, ALU.mult, ALU.add).then_inc(g_zero, 1)
                    dve.wait_ge(g_zero, h + 1)
                chain.link(dve.memset(wts[:], 0.0))
                dve.wait_ge(g_in, 48)
                with chain.loop(KV, 4) as h:
                    def difference(step):
                        size = CHUNK >> (step - 1) if step < 7 else CHUNK
                        ref = size // 2 - 1 if step < 7 else size - 1
                        if step > 1:
                            dve.wait_ge(g_dq, h * 7 + (min(step - 1, 6)))
                        else:
                            dve.wait_ge(g_dq, h * 7)
                        g3 = gsum[:, bass.ds(h, 1), :].rearrange("p a (b n) -> p (a b) n", n=size)
                        dve.tensor_tensor(dec[:].rearrange("p (b n) -> p b n", n=size), g3,
                                          g3[:, :, ref:ref + 1].broadcast_to([P, S // size, size]), ALU.subtract)\
                           .then_inc(g_diff, 1)

                    def keep(step):
                        wait_apart(dve, g_w, h * 7 + (step + 1))
                        mask = pmask[:, step:step + 1, :].broadcast_to([P, NBLK, P])
                        dve.copy_predicated(wts[:], mask, AUX[:, 0:2, :].rearrange("p a (b n) -> p (a b) n", n=P))\
                           .then_inc(g_keep, 1)

                    for step in range(1, 8):
                        difference(step)
                        keep(step - 1)
                        dve.wait_ge(g_exp, h * 8 + step)
                        dve.tensor_tensor(dk[:], gk[:], dec[:], ALU.mult).then_inc(g_dk, 1)
                        dve.wait_ge(g_dk, h * 7 + step)
                    dve.memset(state[:, 0, :], 0.0).then_inc(g_s0, 1)
                    dve.wait_ge(g_s0, h + 1)
                    dve.wait_ge(g_cd, h + 1)
                    for c in range(S // CHUNK):
                        dve.wait_ge(g_up, h * 16 + (c + 1))
                        dve.scalar_tensor_tensor(state[:, (c + 1) % 2, :], state[:, c % 2, :], chunk_decay[:, c:c + 1],
                                                 AUX[:, c % 2, 0:2 * P], ALU.mult, ALU.add).then_inc(g_st, 1)
                        dve.wait_ge(g_st, h * 16 + (c + 1))
                    dve.wait_ge(g_sq, h * 2 + 2)
                    dve.tensor_tensor(T[:, 0, :], T[:, 0, :], T[:, 1, :], ALU.add).then_inc(g_ss, 1)
                    dve.wait_ge(g_ssq, h + 1)
                    chain.link(dve.tensor_scalar(dec[:], AUX[:, 0:2, :].rearrange("p a n -> p (a n)"), 1.0 / (2 * P), EPS_2,
                                                 ALU.mult, ALU.add))
                    dve.reciprocal(dec[:], dec[:]).then_inc(g_var, 1)
                    dve.wait_ge(g_r, h + 1)
                    for d in range(2):
                        o = results[:, :, d, :]
                        halves = dec[:].rearrange("p (a n) -> p a n", a=2)
                        chain.link(dve.scalar_tensor_tensor(o, o, dcol("gla_norm", h * 2 + d), halves, ALU.mult, ALU.mult))
                        m = ya[:, bass.ds(h * 2 + d, 1), :].rearrange("p b (a n) -> p (b a) n", a=2)
                        ins = dve.tensor_tensor(m, m, o, ALU.mult)
                        if d:
                            ins.then_inc(g_y, 1)
                        else:
                            chain.link(ins)
                dve.wait_ge(g_y, KV)

            def pooling():
                chain.link(dve.memset(unit[:], 1.0))
                chain.link(dve.memset(csum[:, 0:16], 0.0))
                dve.wait_ge(p_in, 16)
                for g, w in enumerate(WINDOWS):
                    for par in range(2):
                        u = T[:, par, :]
                        dve.wait_ge(evac["act"], 2 * g + par + 3 + BASE["pool"]["act"])
                        if g:
                            dve.wait_ge(p_mm, g)
                        chain.link(dve.tensor_tensor_scan(csum[:, 16:16 + S], unit[:], u, 0.0, ALU.mult, ALU.add))
                        chain.link(dve.tensor_tensor(pooled[:, par, :], csum[:, 16:16 + S], csum[:, 16 - w:16 - w + S],
                                                     ALU.subtract))
                        chain.link(dve.tensor_tensor(pooled[:, par, 0:16], pooled[:, par, 0:16], inv_cnt[:, g, :], ALU.mult))
                        chain.link(dve.tensor_tensor(pooled[:, par, 0:16], pooled[:, par, 0:16], u[:, 0:16], ALU.subtract))
                        dve.scalar_tensor_tensor(pooled[:, par, 16:S], pooled[:, par, 16:S], 1.0 / w, u[:, 16:S],
                                                 ALU.mult, ALU.subtract).then_inc(p_pool, 1)
                        dve.wait_ge(p_pool, 2 * g + par + 1)

            def gates():
                dve.wait_ge(p_used, 8)
                with dve.Fori(0, 4) as i:
                    for par in range(2):
                        dve.wait_ge(evac["act"], i * 2 + (BASE["gate_b"]["act"] + par + 3))
                        m = yb[:, bass.ds(i * 2 + par, 1), :].rearrange("p a n -> p (a n)")
                        dve.tensor_tensor(m, m, T[:, par, :], ALU.mult).then_inc(b_y, 1)
                dve.wait_ge(b_y, 8)

            def projections():
                for n, (name, src) in enumerate((("proj_a", ya), ("proj_b", yb))):
                    for k in range(KT):
                        dve.wait_ge(s_hi, 8 * n + k + 1)
                        dve.tensor_tensor(Hlo[:, k, :], src[:, k, :], Hhi[:, k, :], ALU.subtract).then_inc(s_lo, 1)
                    with chain.loop(4, 2 * n) as i:
                        for par in range(2):
                            dve.wait_ge(gates_in[par], i * 16 + (64 * n + 16))
                            dve.wait_ge(job_done, i * 2 + (START[name] + par + 1))
                            m = ya[:, bass.ds(i * 2 + par, 1), :].rearrange("p a n -> p (a n)")
                            if n == 0:
                                dve.tensor_tensor(m, G[:, par, :], T[:, par, :], ALU.mult).then_inc(evac["dve"], 1)
                                dve.wait_ge(evac["dve"], i * 2 + (BASE[name]["dve"] + par + 3))
                                dve.memset(stat[:, 24:25], 0.0).then_inc(merged, 1)
                            else:
                                dve.tensor_tensor(T[:, par, :], G[:, par, :], T[:, par, :], ALU.mult).then_inc(evac["dve"], 1)
                                dve.wait_ge(evac["dve"], i * 2 + (BASE[name]["dve"] + par + 3))
                                dve.tensor_tensor(m, m, T[:, par, :], ALU.add).then_inc(merged, 1)
                                chain.link(dve.memset(stat[:, 25:26], 0.0))
                for k in range(KT):
                    dve.wait_ge(s_hi, 16 + k + 1)
                    dve.tensor_tensor(Ulo[:, k, :], ya[:, k, :], Uhi[:, k, :], ALU.subtract).then_inc(s_lo, 1)

            def layer_norm():
                dve.wait_ge(x2_back, 16)
                for m in range(KT):
                    dve.wait_ge(job_done, START["out"] + m + 1)
                    dve.scalar_tensor_tensor(X2[:, m, :], X2[:, m, :], ALPHA, G[:, m % 2, :], ALU.mult, ALU.add)\
                       .then_inc(evac["dve"], 1)
                    dve.wait_ge(evac["dve"], 2 + BASE["out"]["dve"] + m + 1)
                    if m == 0:
                        dve.tensor_copy(ln_acc[:], X2[:, 0, :]).then_inc(n_sum, 1)
                    else:
                        dve.tensor_tensor(ln_acc[:], ln_acc[:], X2[:, m, :], ALU.add).then_inc(n_sum, 1)
                    dve.wait_ge(n_sum, m + 1)
                dve.wait_ge(n_mean, 1)
                chain.link(dve.tensor_scalar(ln_stat[:], AUX[:, 0:2, :].rearrange("p a n -> p (a n)"), 1.0 / D, None, ALU.mult))
                for k in range(KT):
                    dve.tensor_tensor(X2[:, k, :], X2[:, k, :], ln_stat[:], ALU.subtract).then_inc(n_cent, 1)
                for k in range(KT):
                    dve.wait_ge(n_sq, k + 1)
                    if k == 0:
                        dve.tensor_copy(ln_acc[:], T[:, 0, :]).then_inc(n_acc, 1)
                    else:
                        dve.tensor_tensor(ln_acc[:], ln_acc[:], T[:, k % 2, :], ALU.add).then_inc(n_acc, 1)
                    dve.wait_ge(n_acc, k + 1)
                dve.wait_ge(n_r, 1)
                chain.link(dve.reciprocal(ln_stat[:], ln_stat[:]))
                for k in range(KT):
                    chain.link(dve.scalar_tensor_tensor(X2[:, k, :], X2[:, k, :], vcol("ln_g", k), ln_stat[:], ALU.mult, ALU.mult))
                    dve.tensor_scalar(X2[:, k, :], X2[:, k, :], vcol("ln_b", k), None, ALU.add).then_inc(n_y, 1)

            start()
            mem_attention(0)
            angles()
            window()
            project_out(0)
            mlp(0)
            norm("nmix1", lambda k: vcol("mix_norm", 8 + k))
            mem_attention(1)
            lru()
            project_out(1)
            mlp(1)
            norm("nfin", lambda k: vcol("final_norm", k), inplace=True)
            gla()
            pooling()
            gates()
            projections()
            layer_norm()



def feature_major(a):
    return np.ascontiguousarray(a.T.reshape(-1, P, a.shape[0]).transpose(1, 0, 2))


def vector_cols(a):
    return a.reshape(-1, P).T


def weight_jobs(w, rows=None):
    k, m = w.shape
    j = w.reshape(k // P, P, m // P, P).transpose(2, 1, 0, 3)
    if k < D:
        full = np.zeros((m // P, P, KT, P), w.dtype)
        full[:, :, :k // P] = j
        j = full
    return list(j.reshape(m // P, P, KT * P))


def constants():
    c = np.zeros((P, N_CONST), np.float32)
    c[:, CCOLS["ident"]:CCOLS["ident"] + P] = np.eye(P)
    c[:, CCOLS["ones"]:CCOLS["ones"] + P] = 1
    perm = np.zeros((P, P), np.float32)
    dup = np.zeros((P, 2, P), np.float32)
    for h in range(2):
        for f in range(8):
            perm[64 * h + 8 + f, 64 * h + f] = -1
            perm[64 * h + f, 64 * h + 8 + f] = 1
            c[64 * h + f, CCOLS["freq"]] = c[64 * h + 8 + f, CCOLS["freq"]] = np.float32(500000.0 ** (-2.0 * f / 16))
        c[64 * h:64 * h + 64, CCOLS["half"] + h] = 1
        for f in range(64):
            dup[64 * h + f, h, f] = dup[64 * h + f, h, 64 + f] = 1
    c[:, CCOLS["perm"]:CCOLS["perm"] + P] = perm
    c[:, CCOLS["dup"]:CCOLS["dup"] + 2 * P] = dup.reshape(P, 2 * P)
    q, k = np.arange(P)[:, None], np.arange(3 * P)[None, :]
    band = np.abs(k - P - q) <= 128
    masks = np.stack([np.where(band & ok, 0.0, NEG) for ok in (k >= P, k >= 0, k < 2 * P)], 1).astype(np.float32)
    t = np.arange(P)
    pairs = [np.eye(P, dtype=bool)]
    for level in range(LEVELS):
        size = CHUNK >> level
        pairs.append((t[:, None] // size == t // size) & (t[:, None] // (size // 2) != t // (size // 2)))
    counts = [1.0 / np.minimum(np.arange(1, 17), w) for w in WINDOWS]
    return (c, masks, np.ascontiguousarray(np.stack(pairs, 1).astype(np.int32)),
            np.ascontiguousarray(np.broadcast_to(np.array(counts, np.float32), (P, KV, 16))))


def kernel(**inputs):
    import concourse.bacc as bacc
    from concourse.bass_utils import run_bass_kernel_spmd as run

    a = {k: np.asarray(v) for k, v in inputs.items()}
    jobs = weight_jobs(a["w_mem_kv"][0]) + weight_jobs(a["w_mem_kv"][1])
    for l in range(2):
        w = a["attn_w_in"][0] if l == 0 else a["lru_w_in"][0]
        if l == 0:
            q, k, v, mq = np.split(w, [1024, 1280, 1536], axis=1)
            jobs += weight_jobs(mq) + weight_jobs(k) + weight_jobs(v) + weight_jobs(q)
        else:
            xb, gate, mq = np.split(w, [1024, 2048], axis=1)
            jobs += weight_jobs(mq)
            for x, g in zip(weight_jobs(xb), weight_jobs(gate)):
                jobs += [x, g]
        jobs += weight_jobs(a["w_out"][l][:D]) + weight_jobs(a["w_out"][l][D:])
        for c in range(4):
            jobs += weight_jobs(a["w_up"][l][:, c * D:(c + 1) * D]) + weight_jobs(a["w_down"][l][c * D:(c + 1) * D])
    q, k, v, gate_a, low, pool_in, gate_b, merge = np.split(
        a["w_in_2"][0], [512, 1024, 2048, 3072, 3088, 4112, 5136], axis=1)
    for h in range(KV):
        for w in (q[:, h * P:(h + 1) * P], k[:, h * P:(h + 1) * P], v[:, h * 2 * P:(h + 1) * 2 * P],
                  gate_a[:, h * 2 * P:(h + 1) * 2 * P]):
            jobs += weight_jobs(w)
    for w in (pool_in, gate_b, merge, a["w_proj_a_2"][0], a["w_proj_b_2"][0], a["w_out_2"][0]):
        jobs += weight_jobs(w)
    wj = np.stack(jobs)
    vec = np.concatenate([
        vector_cols(a["mix_norm"]), vector_cols(a["mlp_norm"]), vector_cols(a["mem_norm"]), vector_cols(a["final_norm"]),
        np.broadcast_to(a["attn_sinks"], (P, HEADS)), vector_cols(a["lru_conv_w"]), vector_cols(a["lru_conv_b"]),
        vector_cols(a["lru_ba"]), vector_cols(a["lru_bx"]), vector_cols(a["lru_lambda"]),
        vector_cols(a["b_alpha_2"]), vector_cols(a["gla_norm_g_2"]), vector_cols(a["pool_scale_2"]),
        vector_cols(a["b_merge_2"]), vector_cols(a["ln_g_2"]), vector_cols(a["ln_b_2"])], axis=1)
    lw = np.stack([a["lru_wa"][0, 0], a["lru_wx"][0, 0], a["lru_wa"][0, 1], a["lru_wx"][0, 1]], 2)
    const, masks, pair_masks, inv_count = constants()
    arrays = {
        "xT": feature_major(a["x"][0]), "memT": feature_major(a["mem"][0]),
        "pos": np.ascontiguousarray(np.broadcast_to(a["positions"], (P, S))),
        "wjobs": wj, "lru_w": np.ascontiguousarray(lw), "vec": np.ascontiguousarray(vec), "const": const, "masks": masks,
        "pair_masks": pair_masks, "inv_count": inv_count,
        "alpha_w": np.ascontiguousarray(low.reshape(KT, P, RANK).transpose(1, 0, 2)),
        "alpha_up": a["w_alpha_up_2"][0],
        "pool_w": np.ascontiguousarray(a["w_pool_grp_2"][0].reshape(KV, 2, P, 2 * P).transpose(0, 2, 1, 3)),
    }
    nc = bacc.Bacc("TRN2", target_bir_lowering=False, num_devices=1)
    t = {k: nc.dram_tensor(k, v.shape, mybir.dt.from_np(v.dtype), kind="ExternalInput").ap() for k, v in arrays.items()}
    scratch = nc.dram_tensor("scratch", (1, P, KT, S), F32, kind="Internal").ap()
    out = nc.dram_tensor("out", (P, KT, S), F32, kind="ExternalOutput").ap()
    gate_tiles = nc.dram_tensor("gate_tiles", (16, P, S), F32, kind="Internal").ap()
    kv_tiles = nc.dram_tensor("kv_tiles", (2, P, MEM_HEADS * MEM), F32, kind="Internal").ap()
    build(nc, t["xT"], t["memT"], t["pos"], t["wjobs"], t["lru_w"], t["alpha_w"], t["alpha_up"], t["pool_w"], t["vec"],
          t["const"], t["masks"], t["pair_masks"], t["inv_count"], scratch, gate_tiles, kv_tiles, out)
    r = run(nc, [arrays], core_ids=[0])
    y = r.results[0]["out"]
    return y.transpose(1, 0, 2).reshape(D, S).T[None]
```

```python
from contextlib import ExitStack, contextmanager

import numpy as np
import concourse.bass as bass
from concourse import mybir

F32 = mybir.dt.float32
F32R = mybir.dt.float32r
I32 = mybir.dt.int32
ALU = mybir.AluOpType
ACT = mybir.ActivationFunctionType
AX_X = mybir.AxisListType.X

P = 128
D = 1024
S = 1024
KT = D // P
NBLK = S // P
MEM = 256
MEM_HEADS = 4
HEADS = 16
EARLY = 6
KV = 4
HD = 64
SINK_SCALE = HD ** -0.5
MEM_SCALE = 128 ** -0.5
NEG = -1e30
EPS = 1e-6
EPS_2 = 1e-5
ALPHA = 2.0 ** 0.25
CHUNK = 64
TAU = 16.0
RANK = 16
LEVELS = 6
WINDOWS = (2, 4, 8, 16)

PHASES = [("mem0", 8, "act"), ("mem1", 8, "act")]
for _l in range(2):
    PHASES += [(f"mq{_l}", 4, "act")]
    PHASES += [("k", 2, "act"), ("v", 2, "act"), ("q", 8, "act")] if _l == 0 else [("lru", 16, "act")]
    PHASES += [(f"wo_mixed{_l}", 8, "dve"), (f"wo_mem{_l}", 8, "dve")]
    for _c in range(4):
        PHASES += [(f"up{_l}{_c}", 8, "act"), (f"down{_l}{_c}", 8, "dve")]
PHASES += [("gla", 24, "act"), ("pool", 8, "act"), ("gate_b", 8, "act"), ("merge", 16, "act"),
           ("proj_a", 8, "dve"), ("proj_b", 8, "dve"), ("out", 8, "dve")]
START, BASE, PREV = {}, {}, {}
_n, _done, _before = 0, {"act": 0, "dve": 0}, None
for _name, _count, _eng in PHASES:
    START[_name], BASE[_name], PREV[_name] = _n, dict(_done), _before
    _n += _count
    _done[_eng] += _count
    _before = _eng
N_JOBS = _n
MEM_JOBS = START["mq0"]
EVAC = {name: eng for name, _, eng in PHASES}

NORMS = ["nmem", "nmix0", "nmlp0", "nmix1", "nmlp1", "nfin"]


def tiles_before(name):
    return KT * (NORMS.index(name) - 1)


VCOLS, _at = {}, 0
for _name, _n in (("mix_norm", 16), ("mlp_norm", 16), ("mem_norm", 8), ("final_norm", 8), ("sinks", 16),
                  ("conv_w", 32), ("conv_b", 8), ("lru_ba", 16), ("lru_bx", 16), ("lam", 16),
                  ("b_alpha", 4), ("gla_norm", 8), ("pool_scale", 8), ("b_merge", 16), ("ln_g", 8),
                  ("ln_b", 8)):
    VCOLS[_name] = _at
    _at += _n
N_VEC = _at

CCOLS, _at = {}, 0
for _name, _n in (("ident", 128), ("ones", 128), ("perm", 128), ("dup", 256), ("freq", 1), ("half", 2)):
    CCOLS[_name] = _at
    _at += _n
N_CONST = _at


class Chain:

    def __init__(self, eng, sem):
        self.eng, self.sem, self.turn, self.per, self.n = eng, sem, None, 0, 0

    def link(self, ins):
        ins.then_inc(self.sem, 1)
        self.n += 1
        self.eng.wait_ge(self.sem, self.n if self.turn is None else self.turn * self.per + self.n)

    @contextmanager
    def loop(self, count, per):
        first = self.n
        with self.eng.Fori(0, count) as i:
            self.turn, self.per = i, per
            yield i
            assert self.n == first + per, (self.n - first, per)
        self.turn, self.n = None, first + per * count


def build(nc, xT, memT, pos, wjobs, lru_w, alpha_w, alpha_up, pool_w, vec, const, masks, pair_masks, inv_count,
          scratch, gate_tiles, kv_tiles, out):
    with ExitStack() as ctx:
        base = (nc.sbuf_base + 31) // 32 * 32

        def sb(name, shape, dt, at):
            return nc.alloc_sbuf_tensor_at(name, shape, dt, offset=base + at)

        def sem(name):
            return ctx.enter_context(nc.semaphore(name))

        KB = 1024
        X_AT, H_AT, U_AT, W_AT, R_AT = 0, 32 * KB, 96 * KB, 160 * KB, 184 * KB
        X = sb("X", [P, KT, S], F32, X_AT)
        Hhi = sb("Hhi", [P, KT, S], F32R, H_AT)
        Hlo = sb("Hlo", [P, KT, S], F32R, H_AT + 32 * KB)
        Uhi = sb("Uhi", [P, KT, S], F32R, U_AT)
        Ulo = sb("Ulo", [P, KT, S], F32R, U_AT + 32 * KB)
        wraw = sb("wraw", [P, 2, KT, P], F32, W_AT)
        whi = sb("whi", [P, 2, KT, P], F32R, W_AT + 8 * KB)
        wlo = sb("wlo", [P, 2, KT, P], F32R, W_AT + 16 * KB)
        T = sb("T", [P, 2, S], F32, R_AT)
        MK = sb("MK", [P, MEM_HEADS, MEM], F32, R_AT + 8 * KB)
        MV = sb("MV", [P, 2, MEM_HEADS, P], F32, R_AT + 12 * KB)
        vecs = sb("vecs", [P, N_VEC], F32, R_AT + 16 * KB)
        cst = sb("cst", [P, N_CONST], F32, R_AT + 17 * KB)
        stat = sb("stat", [P, 48], F32, R_AT + 19 * KB + 640)
        O_sb = sb("O_sb", [P, 2, P], F32, R_AT + 19 * KB + 832)
        probsT = sb("probsT", [P, 2, 3 * P], F32, R_AT + 20 * KB + 832)
        squares = sb("squares", [P, 2, S], F32, H_AT + 48 * KB)
        acc = sb("acc", [P, S], F32, H_AT + 56 * KB)
        rstd = sb("rstd", [P, S], F32, H_AT + 60 * KB)
        eps_col = stat[:, 30:31]
        mraw = sb("mraw", [P, KT, MEM], F32, U_AT)
        MT = sb("MT", [P, 2, MEM], F32, U_AT + 8 * KB)
        MK1 = sb("MK1", [P, MEM_HEADS, MEM], F32, U_AT + 12 * KB)
        MV1 = sb("MV1", [P, 2, MEM_HEADS, P], F32, U_AT + 16 * KB)
        mixed = sb("mixed", [P, KT, S], F32, U_AT + 32 * KB)
        mo = sb("mo", [P, MEM_HEADS, S], F32, X_AT)
        MOhi = sb("MOhi", [P, MEM_HEADS, S], F32R, U_AT)
        MOlo = sb("MOlo", [P, MEM_HEADS, S], F32R, U_AT + 16 * KB)
        keys = sb("keys", [P, KV, S + 2 * P], F32, U_AT)
        vals = sb("vals", [P, NBLK + 2, KV * HD], F32, U_AT + 20 * KB)
        cos = sb("cos", [P, S], F32, X_AT + 16 * KB)
        sin = sb("sin", [P, S], F32, X_AT + 20 * KB)
        wmask = sb("wmask", [P, 3, 3 * P], F32, X_AT + 24 * KB)
        probs = sb("probs", [P, 2, 3 * P], F32, X_AT + 29 * KB)
        lw = sb("lw", [P, 2, 4, P], F32, U_AT)
        xb = sb("xb", [P, S + 8], F32, U_AT + 4 * KB)
        xc = [sb("xc0", [P, S], F32, U_AT + 9 * KB), sb("xc1", [P, S], F32, X_AT + 28 * KB)]
        rg = sb("rg", [P, 2, S], F32, U_AT + 13 * KB)
        ig = sb("ig", [P, 2, S], F32, U_AT + 21 * KB)
        decay_c = sb("decay_c", [P, 96], F32, U_AT + 29 * KB)
        av = sb("av", [P, 2, S], F32, X_AT + 16 * KB)
        gl = sb("gl", [P, S], F32, X_AT + 24 * KB)

        gsum = sb("gsum", [P, KV, S], F32, U_AT)
        gq = sb("gq", [P, S], F32, U_AT + 16 * KB)
        gk = sb("gk", [P, S], F32, U_AT + 20 * KB)
        dec = sb("dec", [P, S], F32, U_AT + 24 * KB)
        dq = sb("dq", [P, S], F32, U_AT + 28 * KB)
        dk = sb("dk", [P, S], F32, U_AT + 32 * KB)
        vtok = sb("vtok", [P, NBLK, 2 * P], F32, U_AT + 36 * KB)
        results = sb("results", [P, 2, 2, S // 2], F32, U_AT + 36 * KB)
        ktok = sb("ktok", [P, NBLK, P], F32, U_AT + 44 * KB)
        wts = sb("wts", [P, NBLK, P], F32, U_AT + 48 * KB)
        state = sb("state", [P, 2, 2 * P], F32, U_AT + 52 * KB)
        pmask = sb("pmask", [P, LEVELS + 1, P], I32, U_AT + 54 * KB)
        chunk_decay = sb("chunk_decay", [P, S // CHUNK], F32, U_AT + 57 * KB + 512)
        alow_w = sb("alow_w", [P, KT, RANK], F32, U_AT + 58 * KB)
        aup_w = sb("aup_w", [RANK, KV * P], F32, U_AT + 59 * KB)
        alow = sb("alow", [RANK, S], F32, U_AT + 28 * KB)
        zmin = sb("zmin", [P, 2, S], F32, U_AT + 36 * KB)
        starts = sb("starts", [P, S], F32, U_AT + 24 * KB)
        ya = sb("ya", [P, KT, S], F32, X_AT)
        yb = sb("yb", [P, KT, S], F32, U_AT + 32 * KB)
        unit = sb("unit", [P, S], F32, U_AT)
        csum = sb("csum", [P, 16 + S], F32, U_AT + 4 * KB)
        pooled = sb("pooled", [P, 2, S], F32, U_AT + 9 * KB)
        pool_m = sb("pool_m", [P, 2, 2 * P], F32, U_AT + 17 * KB)
        inv_cnt = sb("inv_cnt", [P, KV, 16], F32, U_AT + 19 * KB)
        X2 = sb("X2", [P, KT, S], F32, H_AT)
        ya_hi = sb("ya_hi", [P, KT, S], F32R, U_AT)
        ya_lo = sb("ya_lo", [P, KT, S], F32R, X_AT)
        yb_hi = sb("yb_hi", [P, KT, S], F32R, H_AT + 32 * KB)
        yb_lo = sb("yb_lo", [P, KT, S], F32R, U_AT + 32 * KB)
        both = sb("both", [P, KT, S], F32, H_AT)
        both_hi = sb("both_hi", [P, KT, S], F32R, U_AT)
        both_lo = sb("both_lo", [P, KT, S], F32R, X_AT)
        ln_acc = sb("ln_acc", [P, S], F32, H_AT + 32 * KB)
        ln_stat = sb("ln_stat", [P, S], F32, H_AT + 36 * KB)

        G = ctx.enter_context(nc.psum_tensor("G", [P, 2, S], F32))
        AUX = ctx.enter_context(nc.psum_tensor("AUX", [P, 4, 512], F32))
        ident = cst[:, CCOLS["ident"]:CCOLS["ident"] + P]
        ones = cst[:, CCOLS["ones"]:CCOLS["ones"] + P]
        perm = cst[:, CCOLS["perm"]:CCOLS["perm"] + P]
        freq = cst[:, CCOLS["freq"]:CCOLS["freq"] + 1]

        def vcol(name, i):
            return vecs[:, VCOLS[name] + i:VCOLS[name] + i + 1]

        def dcol(name, i, width=1):
            return vecs[:, bass.ds(VCOLS[name] + i, width)]

        w_loaded = [sem("w_loaded0"), sem("w_loaded1")]
        w_hi = sem("w_hi")
        w_split = sem("w_split")
        job_done = sem("job_done")
        evac = {"act": sem("evac_act"), "dve": sem("evac_dve")}
        act_chain, dve_chain, pool_chain = sem("act_chain"), sem("dve_chain"), sem("pool_chain")
        tables = sem("tables")
        x_loaded = sem("x_loaded")
        x_back = [sem("x_back0"), sem("x_back1")]
        x_saved = sem("x_saved")
        mem_in, mem_ready = sem("mem_in"), sem("mem_ready")
        kv_saved, kv_in = sem("kv_saved"), sem("kv_in")
        pos_in, masks_in, pads = sem("pos_in"), sem("masks_in"), sem("pads")
        out_done = sem("out_done")

        norm_s = {k: sem(f"norm_{k}") for k in ("sq", "acc", "ssq", "var", "r", "t", "hi", "lo")}

        def attn_sems(name):
            return {k: sem(f"{name}_{k}") for k in ("sc", "mx", "pr", "pt", "pc", "pv", "os", "ot", "oc")}

        attns = {n: attn_sems(n) for n in ("am", "aw")}
        mvt, mvc = sem("mvt"), sem("mvc")
        trig, rot_sw, rot_ok = sem("trig"), sem("rot_sw"), sem("rot_ok")
        kdup, kcopied, vt, vcopied = sem("kdup"), sem("kcopied"), sem("vt"), sem("vcopied")
        split_hi, split_lo = [sem("split_hi0"), sem("split_hi1")], [sem("split_lo0"), sem("split_lo1")]
        up_hi, up_lo, up_sq = [sem("up_hi0"), sem("up_hi1")], [sem("up_lo0"), sem("up_lo1")], [sem("up_sq0"), sem("up_sq1")]
        early_hi, early_lo = sem("early_hi"), sem("early_lo")
        lw_in = [sem("lw_in0"), sem("lw_in1")]
        l_dec, l_xc, l_mm, l_sig, l_exp, l_a2, l_e, l_sq, l_ix, l_h, l_sum, l_y = (
            sem("l_" + k) for k in ("dec", "xc", "mm", "sig", "exp", "a2", "e", "sq", "ix", "h", "sum", "y"))
        l_dx, l_de = sem("l_dx"), sem("l_de")
        g_in, g_low, g_lowc, g_z, g_abs, g_min, g_zero = (sem("g_" + k) for k in ("in", "low", "lowc", "z", "abs", "min", "zero"))
        g_diff, g_exp, g_dq, g_dk, g_w, g_keep = (sem("g_" + k) for k in ("diff", "exp", "dq", "dk", "w", "keep"))
        g_vt, g_vc, g_kt, g_kc, g_up, g_st, g_o, g_oc = (sem("g_" + k) for k in ("vt", "vc", "kt", "kc", "up", "st", "o", "oc"))
        g_s0 = sem("g_s0")
        g_cd, g_sq, g_ss, g_ssq, g_r, g_y = (sem("g_" + k) for k in ("cd", "sq", "ss", "ssq", "r", "y"))
        p_in, p_m, p_pool, p_mm, p_used = sem("p_in"), sem("p_m"), sem("p_pool"), sem("p_mm"), sem("p_used")
        b_y = sem("b_y")
        gates_out, gates_in = [sem("gates_out0"), sem("gates_out1")], [sem("gates_in0"), sem("gates_in1")]
        s_hi, s_lo, merged = sem("s_hi"), sem("s_lo"), sem("merged")
        x2_saved, x2_back = sem("x2_saved"), sem("x2_back")
        n_sum, n_mean, n_cent, n_sq, n_acc, n_ssq, n_r, n_y, n_b = (
            sem("n_" + k) for k in ("sum", "mean", "cent", "sq", "acc", "ssq", "r", "y", "b"))

        def sums(width):
            return AUX[:, 0, 0:width] if width <= 512 else AUX[:, 0:2, :].rearrange("p a n -> p (a n)")

        def tile_of(t, m):
            return t[:, bass.ds(m, 1), :].rearrange("p a n -> p (a n)")

        def tile_at(t, m):
            return t[bass.ds(m, 1)].rearrange("a p n -> (a p) n")

        stood = {nc.scalar: sem("act_stood"), nc.vector: sem("dve_stood"), nc.gpsimd: sem("pool_stood")}

        def wait_apart(eng, semaphore, value):
            eng.wait_ge(semaphore, value)
            eng.sem_inc(stood[eng], 1)

        def scored(par, u, width):
            return G[:, par, 0:width] if u % 3 == 2 else AUX[:, u % 3, 0:width]

        block = ctx.enter_context(nc.Block())

        @block.sync
        def _(sp):
            for par in range(2):
                sp.dma_start(wraw[:, par], wjobs[par]).then_inc(w_loaded[par], 16)
            for first, last, free in ((1, MEM_JOBS // 2 + 1, job_done), (MEM_JOBS // 2 + 1, N_JOBS // 2, w_split)):
                with sp.Fori(first, last) as i:
                    for par in range(2):
                        sp.wait_ge(free, i * 2 + (par - 1))
                        sp.dma_start(wraw[:, par], wjobs[bass.ds(i * 2 + par, 1)].rearrange("a p n -> (a p) n"))\
                          .then_inc(w_loaded[par], 16)

        @block.gpsimd
        def _(pool):
            def split(n, i, par, started, kt=KT):
                pool.wait_ge(w_loaded[par], i * 16 + 16)
                if started:
                    wait_apart(pool, job_done, n - 1)
                pool.tensor_copy(whi[:, par, 0:kt], wraw[:, par, 0:kt]).then_inc(w_hi, 1)
                pool.wait_ge(w_hi, n + 1)
                pool.tensor_tensor(wlo[:, par, 0:kt], wraw[:, par, 0:kt], whi[:, par, 0:kt], ALU.subtract)\
                    .then_inc(w_split, 1)

            def splits(first, last, kt=KT):
                with pool.Fori(first // 2, last // 2) as i:
                    for par in range(2):
                        split(i * 2 + par, i, par, True, kt)

            pool.nop().then_inc(w_hi, MEM_JOBS)
            pool.nop().then_inc(w_split, MEM_JOBS)
            for par in range(2):
                split(MEM_JOBS + par, MEM_JOBS // 2, par, False)
            splits(MEM_JOBS + 2, START["k"])
            pool.wait_ge(kv_saved, 32)
            pool.memset(keys[:, :, 0:P], 0.0)
            pool.memset(keys[:, :, S + P:S + 2 * P], 0.0)
            pool.memset(vals[:, 0, :], 0.0)
            pool.memset(vals[:, NBLK + 1, :], 0.0).then_inc(pads, 1)
            splits(START["k"], START["wo_mixed0"] + 2)

            def split_mixed(l, k, made, value):
                pool.wait_ge(made, value)
                pool.tensor_copy(Hhi[:, k, :], mixed[:, k, :]).then_inc(early_hi, 1)
                pool.wait_ge(early_hi, EARLY * l + k + 1)
                pool.tensor_tensor(Hlo[:, k, :], mixed[:, k, :], Hhi[:, k, :], ALU.subtract).then_inc(early_lo, 1)

            pool.wait_ge(job_done, START["wo_mixed0"])
            for k in range(EARLY):
                split_mixed(0, k, attns["aw"]["oc"], (k + 1) * NBLK)
            splits(START["wo_mixed0"] + 2, START["wo_mem0"])
            splits(START["wo_mem0"], START["up00"], kt=KT // 2)
            splits(START["up00"], START["lru"] + 4)
            pool.memset(xb[:, 0:1], 0.0)
            pool.memset(xb[:, S + 1:S + 3], 0.0).then_inc(pads, 1)

            def lru_block(j, par, last=False):
                if not last:
                    split(j * 2 + (START["lru"] + 4), j + (START["lru"] // 2 + 2), 0, True)
                for dr in range(2):
                    pool.wait_ge(l_sig, j * 4 + (2 * dr + 2))
                    pool.tensor_tensor(ig[:, dr], ig[:, dr], xc[par][:], ALU.mult).then_inc(l_ix, 1)
                for dr in range(2):
                    pool.wait_ge(l_exp, j * 4 + (2 * dr + 2))
                    pool.tensor_tensor(T[:, dr], av[:, dr], av[:, dr], ALU.mult).then_inc(l_a2, 1)
                if not last:
                    split(j * 2 + (START["lru"] + 5), j + (START["lru"] // 2 + 2), 1, True)

            with pool.Fori(0, 3) as i:
                for par in range(2):
                    lru_block(i * 2 + par, par)
            lru_block(6, 0)
            pool.wait_ge(job_done, START["wo_mixed1"])
            for k in range(3):
                split_mixed(1, k, l_y, k + 1)
            lru_block(7, 1, last=True)
            for k in range(3, EARLY):
                split_mixed(1, k, l_y, k + 1)
            splits(START["wo_mixed1"] + 2, START["wo_mem1"])
            splits(START["wo_mem1"], START["up10"], kt=KT // 2)
            splits(START["up10"], START["gla"] + 4)
            with pool.Fori(0, KV) as h:
                def decayed(step, n):
                    pool.wait_ge(g_exp, h * 8 + step)
                    if n:
                        pool.wait_ge(g_w, h * 7 + (6 if step == 8 else step))
                    pool.tensor_tensor(dq[:], gq[:], dec[:], ALU.mult).then_inc(g_dq, 1)

                for n in (1, 2, -4, 3, -5, 4, 5, -6, 6, -7, 8, -8, -9):
                    if n > 0:
                        decayed(n, True)
                    else:
                        split(h * 6 + (START["gla"] - n), h * 3 + (START["gla"] // 2 + -n // 2), -n % 2, True)
            splits(START["gla"] + 28, N_JOBS)

        @block.tensor
        def _(pe):
            def psum_waits(name, l, par):
                e, o = EVAC[name], PREV[name]
                pe.wait_ge(evac[e], l + (1 + BASE[name][e]))
                if o not in (None, e):
                    pe.wait_ge(evac[o], 2 + BASE[name][o] - (par == 0))

            def job_part(q, n, par, hi, lo, ready, kt=KT, width=S):
                half = min(width, 512)
                halves = width // half
                k, c = q // halves, q % halves
                if q == 0:
                    pe.wait_ge(w_split, n + 1)
                if c == 0 and ready is not None:
                    pe.wait_ge(*(ready(k) if callable(ready) else (ready[0], ready[1] + (k + 1))))
                cols = slice(c * half, (c + 1) * half)
                for j, (w, x) in enumerate(((whi, hi), (whi, lo), (wlo, hi))):
                    mm = pe.matmul(G[:, par, cols], w[:, par, k, :], x[:, k, cols],
                                   start=(k == 0 and j == 0), stop=(k == kt - 1 and j == 2))
                if q == kt * halves - 1:
                    mm.then_inc(job_done, 1)

            def job(n, par, hi, lo, ready, kt=KT, width=S):
                for q in range(kt * (width // min(width, 512))):
                    job_part(q, n, par, hi, lo, ready, kt, width)

            def next_part(q, n, par, shift):
                if q == 0:
                    pe.wait_ge(evac["act"], n + shift)
                job_part(q, n, par, Hhi, Hlo, None)

            def jobs(name, count, hi, lo, ready, **kw):
                with pe.Fori(0, count // 2) as i:
                    for par in range(2):
                        psum_waits(name, i * 2 + par, par)
                        job(i * 2 + (START[name] + par), par, hi, lo, ready, **kw)

            def sum_squares(name, width):
                r = NORMS.index(name)
                pe.wait_ge(norm_s["acc"], KT * r + KT)
                half = min(width, 512)
                for c in range(width // half):
                    mm = pe.matmul(AUX[:, c, 0:half], ones, acc[:, c * half:(c + 1) * half], start=True, stop=True)
                mm.then_inc(norm_s["ssq"], 1)

            def mem_phase(l):
                name = f"mem{l}"
                for half in range(2):
                    with pe.Fori(0, 2) as i:
                        for par in range(2):
                            m = 4 * half + par
                            pe.wait_ge(evac["act"], i * 2 + (START[name] + m + 1))
                            pe.wait_ge(w_loaded[par], i * 16 + (START[name] + 4 * half + 2) * 8)
                            for k in range(KT):
                                mm = pe.matmul(G[:, par, 0:MEM], wraw[:, par, k, :], mraw[:, k, :], start=(k == 0),
                                               stop=(k == KT - 1))
                            mm.then_inc(job_done, 1)
                            if half:
                                pe.wait_ge(evac["act"], i * 2 + (START[name] + m + 3))
                                if l or par:
                                    pe.wait_ge(mvc, i * 2 + (4 * l + par))
                                for t in range(2):
                                    tr = pe.transpose(AUX[:, 2, t * P:(t + 1) * P], MT[:, par, t * P:(t + 1) * P], ident)
                                tr.then_inc(mvt, 1)
                                pe.wait_ge(mvc, i * 2 + (4 * l + 1 + par))

            def attention(s, i, par, subs, nk, kop, vop, between):
                U = NBLK * subs
                dim = P // subs

                def scores(u):
                    b, h = u // subs, u % subs
                    if u >= 3:
                        pe.wait_ge(s["pr"], i * U + (u - 2))
                    pe.matmul(scored(par, u, nk * P), T[:, h, b * P:(b + 1) * P], kop(b),
                              start=True, stop=True).then_inc(s["sc"], 1)

                def turn(u):
                    pe.wait_ge(s["pr"], i * U + (u + 1))
                    if u:
                        pe.wait_ge(s["pc"], i * U + u)
                    for t in range(nk):
                        tr = pe.transpose(AUX[:, 2, t * P:(t + 1) * P], probs[:, u % 2, t * P:(t + 1) * P], ident)
                    tr.then_inc(s["pt"], 1)

                def weigh(u):
                    b, h = u // subs, u % subs
                    pe.wait_ge(s["pc"], i * U + (u + 1))
                    if h == 0 and b:
                        pe.wait_ge(s["os"], i * NBLK + b)
                    for t in range(nk):
                        mm = pe.matmul(AUX[:, 3, h * dim:(h + 1) * dim], probsT[:, u % 2, t * P:(t + 1) * P],
                                       vop(b, t), start=(t == 0), stop=(t == nk - 1))
                    mm.then_inc(s["pv"], 1)

                def turn_result(b):
                    pe.wait_ge(s["os"], i * NBLK + (b + 1))
                    if b:
                        pe.wait_ge(s["oc"], i * NBLK + b)
                    pe.transpose(G[:, par, 512:512 + P], O_sb[:, b % 2, :], ident).then_inc(s["ot"], 1)

                scores(0)
                scores(1)
                for u in range(U):
                    if u + 2 < U:
                        scores(u + 2)
                    between(u)
                    turn(u)
                    if u >= 2 and (u - 1) % subs == 0:
                        turn_result((u - 2) // subs)
                    if u:
                        weigh(u - 1)
                if (U - 2) % subs == subs - 1:
                    turn_result((U - 2) // subs)
                weigh(U - 1)
                turn_result(NBLK - 1)

            def mem_attention(l):
                s, name = attns["am"], f"mq{l}"
                shift = 1 + BASE[name]["act"] - START[name]
                if l:
                    pe.wait_ge(kv_in, 32)
                psum_waits(name, 0, 0)
                job(START[name], 0, Hhi, Hlo, (norm_s["lo"], tiles_before(f"nmix{l}")))
                with pe.Fori(0, 2) as i:
                    for par in range(2):
                        head = i * 2 + par
                        after = head + (START[name] + 1)
                        pe.wait_ge(evac["act"], i * 2 + (3 + BASE[name]["act"] + par))
                        next_part(0, after, 1 - par, shift)
                        next_part(1, after, 1 - par, shift)

                        def between(u):
                            for q in range(2 + 2 * u, min(4 + 2 * u, 16)):
                                next_part(q, after, 1 - par, shift)

                        attention(s, head + MEM_HEADS * l, par, 1, 2,
                                  lambda b: MK[:, bass.ds(head, 1), :].rearrange("p a n -> p (a n)"),
                                  lambda b, t: MV[:, t, bass.ds(head, 1), :].rearrange("p a n -> p (a n)"), between)

            def rotate(r, e, between):
                pe.wait_ge(evac["act"], e)
                for c in range(2):
                    mm = pe.matmul(AUX[:, c, :], perm, T[:, 0, c * 512:(c + 1) * 512], start=True, stop=True)
                mm.then_inc(rot_sw, 1)
                between()
                pe.wait_ge(rot_ok, r + 1)

            def window():
                shift = 1 + BASE["k"]["act"] - START["k"]
                for par in range(2):
                    after = START["k"] + par + 1

                    def between():
                        for q in range(16):
                            next_part(q, after, 1 - par, shift)

                    rotate(par, 3 + BASE["k"]["act"] + par, between)
                    for h in range(2):
                        if h:
                            pe.wait_ge(kcopied, 2 * par + h)
                        at = CCOLS["dup"] + h * P
                        for c in range(2):
                            mm = pe.matmul(AUX[:, c, :], cst[:, at:at + P], T[:, 0, c * 512:(c + 1) * 512],
                                           start=True, stop=True)
                        mm.then_inc(kdup, 1)
                    pe.wait_ge(kcopied, 2 * par + 2)
                for par in range(2):
                    for q in range(16):
                        next_part(q, START["v"] + par + 1, 1 - par, shift)
                    pe.wait_ge(evac["act"], 3 + BASE["v"]["act"] + par)
                    if par:
                        pe.wait_ge(vcopied, 1)
                    for b in range(NBLK):
                        at = (b % 4) * P
                        tr = pe.transpose(AUX[:, b // 4, at:at + P], T[:, 0, b * P:(b + 1) * P], ident)
                    tr.then_inc(vt, 1)
                pe.wait_ge(vcopied, 2)
                pe.wait_ge(pads, 1)

                def tile(g, par, last=False):
                    p = g * 2 + par
                    after = p + (START["q"] + 1)

                    def turning():
                        if not last:
                            for q in range(6):
                                next_part(q, after, 1 - par, shift)

                    def between(u):
                        if not last and 1 <= u <= 10:
                            next_part(5 + u, after, 1 - par, shift)

                    rotate(p + 2, p + (3 + BASE["q"]["act"]), turning)
                    attention(attns["aw"], p, par, 2, 3,
                              lambda b: keys[:, bass.ds(g, 1), b * P:(b + 3) * P].rearrange("p a n -> p (a n)"),
                              lambda b, t: vals[:, b + t, bass.ds(g * HD, HD)], between)

                with pe.Fori(0, KV - 1) as g:
                    for par in range(2):
                        tile(g, par)
                for par in range(2):
                    tile(KV - 1, par, last=(par == 1))

            def project_out(l):
                jobs(f"wo_mixed{l}", 8, Hhi, Hlo,
                     lambda k: (early_lo, EARLY * l + k + 1) if k < EARLY else (split_lo[l], k - EARLY + 1))
                jobs(f"wo_mem{l}", 8, MOhi, MOlo, (split_lo[l], KT - EARLY), kt=4)

            def mlp(l):
                sum_squares(f"nmlp{l}", S)
                n0, a0, d0 = START[f"up{l}0"], BASE[f"up{l}0"]["act"], BASE[f"up{l}0"]["dve"]
                with pe.Fori(0, 4) as c:
                    with pe.Fori(0, 4) as i:
                        for par in range(2):
                            pe.wait_ge(evac["act"], c * 8 + i * 2 + (a0 + par + 1))
                            pe.wait_ge(evac["dve"], c * 8 + (d0 + 2 - (par == 0)))
                            job(c * 16 + i * 2 + (n0 + par), par, Hhi, Hlo, (norm_s["lo"], tiles_before(f"nmlp{l}")))
                    with pe.Fori(0, 4) as i:
                        for par in range(2):
                            pe.wait_ge(evac["dve"], c * 8 + i * 2 + (d0 + par + 1))
                            pe.wait_ge(evac["act"], c * 8 + (a0 + 8 + 2 - (par == 0)))
                            job(c * 16 + i * 2 + (n0 + 8 + par), par, Uhi, Ulo, (up_lo[l], c * 8))

            def lru():
                pe.wait_ge(attns["am"]["oc"], 2 * MEM_HEADS * NBLK)
                shift = 1 + BASE["lru"]["act"] - START["lru"]

                def gates(par, dr):
                    for g in range(2):
                        for c in range(2):
                            mm = pe.matmul(AUX[:, 2 * g + c, :], lw[:, par, 2 * dr + g, :], xc[par][:, c * 512:(c + 1) * 512],
                                           start=True, stop=True)
                    mm.then_inc(l_mm, 1)

                def first_gates(j, lw_count, par):
                    pe.wait_ge(l_xc, j + 1)
                    pe.wait_ge(lw_in[par], lw_count * 16 + 16)
                    gates(par, 0)

                def block_of(j, i, par, ahead=True):
                    pe.wait_ge(l_sig, j * 4 + 2)
                    gates(par, 1)
                    for q in range(16):
                        next_part(q, j * 2 + (START["lru"] + 3), 1, shift)
                    if ahead:
                        for q in range(16):
                            next_part(q, j * 2 + (START["lru"] + 4), 0, shift)
                    pe.wait_ge(l_sig, j * 4 + 4)
                    first_gates(j + 1, i + par, 1 - par)

                for n in (1, 2):
                    for q in range(16):
                        next_part(q, START["lru"] + n, n % 2, shift)
                first_gates(0, 0, 0)
                with pe.Fori(0, 3) as i:
                    for par in range(2):
                        block_of(i * 2 + par, i, par)
                block_of(6, 3, 0, ahead=False)
                pe.wait_ge(l_sig, 30)
                gates(1, 1)

            def gla():
                pe.wait_ge(g_in, 48)
                psum_waits("gla", 0, 0)
                for k in range(KT):
                    for q in range(2 * k, 2 * k + 2):
                        job_part(q, START["gla"], 0, Hhi, Hlo, (norm_s["lo"], tiles_before("nfin")))
                    for c in range(2):
                        mm = pe.matmul(AUX[0:RANK, c, :], alow_w[:, k, :], X[:, k, c * 512:(c + 1) * 512],
                                       start=(k == 0), stop=(k == KT - 1))
                mm.then_inc(g_low, 1)
                psum_waits("gla", 1, 1)
                job(START["gla"] + 1, 1, Hhi, Hlo, None)
                pe.wait_ge(g_lowc, 1)
                for h in range(KV):
                    for c in range(2):
                        if h >= 2 and c == 0:
                            pe.wait_ge(g_abs, h - 1)
                            pe.wait_ge(g_min, h - 1)
                        mm = pe.matmul(AUX[:, 2 * (h % 2) + c, :], aup_w[:, h * P:(h + 1) * P], alow[:, c * 512:(c + 1) * 512],
                                       start=True, stop=True)
                    mm.then_inc(g_z, 1)
                pe.wait_ge(g_abs, KV)
                pe.wait_ge(g_min, KV)
                a0 = BASE["gla"]["act"]
                shift = 1 + a0 - START["gla"]

                def head(h, last=False):

                    def weights(step):
                        if step:
                            pe.wait_ge(g_dq, h * 7 + step)
                            pe.wait_ge(g_dk, h * 7 + step)
                            pe.wait_ge(g_keep, h * 7 + step)
                            q, k = dq, dk
                        else:
                            pe.wait_ge(evac["act"], h * 6 + (a0 + 4))
                            q, k = gq, gk
                        for b in range(NBLK):
                            cols = slice(b * P, (b + 1) * P)
                            mm = pe.matmul(AUX[:, b // 4, (b % 4) * P:(b % 4 + 1) * P], k[:, cols], q[:, cols],
                                           start=True, stop=True)
                        mm.then_inc(g_w, 1)

                    def turn_values(n):
                        pe.wait_ge(evac["act"], h * 6 + (a0 + 5 + n))
                        if n:
                            pe.wait_ge(g_vc, h * 2 + 1)
                        for b in range(NBLK):
                            tr = pe.transpose(AUX[:, 2 + b // 4, (b % 4) * P:(b % 4 + 1) * P], T[:, n, b * P:(b + 1) * P], ident)
                        tr.then_inc(g_vt, 1)

                    weights(0)
                    step_at = {22: 1, 32: 2, 42: 3, 51: 4, 60: 5}
                    for q in range(64):
                        next_part(q % 16, h * 6 + (START["gla"] + 2 + q // 16), q // 16 % 2, shift)
                        if q + 1 in step_at:
                            weights(step_at[q + 1])
                        if q + 1 == 26:
                            turn_values(0)
                        if q + 1 == 43:
                            turn_values(1)

                    def ahead(first, last_part):
                        if not last:
                            for q in range(first, last_part):
                                next_part(q % 16, h * 6 + (START["gla"] + 6 + q // 16), q // 16, shift)

                    weights(6)
                    ahead(0, 5)
                    pe.wait_ge(g_dk, h * 7 + 7)
                    pe.wait_ge(g_vc, h * 2 + 2)
                    for b in range(NBLK):
                        tr = pe.transpose(AUX[:, 2 + b // 4, (b % 4) * P:(b % 4 + 1) * P], dk[:, b * P:(b + 1) * P], ident)
                    tr.then_inc(g_kt, 1)
                    ahead(5, 10)
                    pe.wait_ge(g_kc, h + 1)
                    pe.wait_ge(g_keep, h * 7 + 7)
                    pe.wait_ge(g_dq, h * 7 + 7)
                    for c in range(S // CHUNK):
                        b, rows = c // 2, slice((c % 2) * CHUNK, (c % 2 + 1) * CHUNK)
                        ahead(*((10 + 2 * c, 12 + 2 * c) if c < 6 else (16 + c, 17 + c)))
                        if c >= 2:
                            pe.wait_ge(g_st, h * 16 + (c - 1))
                        pe.matmul(AUX[:, c % 2, 0:2 * P], ktok[rows, b, :], vtok[rows, b, :], start=True, stop=True)\
                          .then_inc(g_up, 1)
                        if c == 8:
                            pe.wait_ge(g_oc, h * 4 + 2)
                        at = (b % 4) * P
                        for d in range(2):
                            if c % 2 == 0:
                                pe.matmul(AUX[:, 2 + d, at:at + P], vtok[:, b, d * P:(d + 1) * P], wts[:, b, :],
                                          start=True, stop=False)
                            if d == 0 and c == 0:
                                pe.wait_ge(g_s0, h + 1)
                            elif d == 0:
                                pe.wait_ge(g_st, h * 16 + c)
                            mm = pe.matmul(AUX[:, 2 + d, at + (c % 2) * CHUNK:at + (c % 2 + 1) * CHUNK],
                                           state[:, c % 2, d * P:(d + 1) * P], dq[:, c * CHUNK:(c + 1) * CHUNK],
                                           start=False, stop=(c % 2 == 1))
                        if c % 8 == 7:
                            mm.then_inc(g_o, 1)
                    pe.wait_ge(g_st, h * 16 + 16)
                    pe.wait_ge(g_ss, h + 1)
                    for c in range(2):
                        mm = pe.matmul(AUX[:, c, :], ones, T[:, 0, c * 512:(c + 1) * 512], start=True, stop=True)
                    mm.then_inc(g_ssq, 1)
                    pe.wait_ge(g_r, h + 1)

                with pe.Fori(0, KV - 1) as h:
                    head(h)
                head(KV - 1, last=True)

            def pooling():
                def pair(g):
                    for par in range(2):
                        for q in range(16):
                            next_part(q, g * 2 + (START["pool"] + par), par, 1 + BASE["pool"]["act"] - START["pool"])

                def group(g):
                    pe.wait_ge(p_pool, g * 2 + 2)
                    pe.wait_ge(p_m, g * 16 + 16)
                    for m in range(2):
                        for c in range(2):
                            for k in range(2):
                                mm = pe.matmul(AUX[:, 2 * m + c, :], pool_m[:, k, m * P:(m + 1) * P],
                                               pooled[:, k, c * 512:(c + 1) * 512], start=(k == 0), stop=(k == 1))
                    mm.then_inc(p_mm, 1)

                pair(0)
                with pe.Fori(0, KV - 1) as g:
                    pair(g + 1)
                    group(g)
                    pe.wait_ge(p_used, g * 2 + 2)
                group(KV - 1)

            pe.wait_ge(tables, 32)
            sum_squares("nmem", MEM)
            pe.wait_ge(mem_ready, KT)
            mem_phase(0)
            sum_squares("nmix0", S)
            mem_phase(1)
            mem_attention(0)
            window()
            project_out(0)
            mlp(0)
            sum_squares("nmix1", S)
            mem_attention(1)
            lru()
            project_out(1)
            mlp(1)
            sum_squares("nfin", S)
            gla()
            pooling()
            jobs("gate_b", 8, Hhi, Hlo, None)
            jobs("merge", 16, Hhi, Hlo, None)
            jobs("proj_a", 8, ya_hi, ya_lo, (s_lo, 0))
            jobs("proj_b", 8, yb_hi, yb_lo, (s_lo, 8))
            jobs("out", 8, both_hi, both_lo, (s_lo, 16))
            for done, out_sem in ((n_sum, n_mean), (n_acc, n_ssq)):
                pe.wait_ge(done, KT)
                for c in range(2):
                    mm = pe.matmul(AUX[:, c, :], ones, ln_acc[:, c * 512:(c + 1) * 512], start=True, stop=True)
                mm.then_inc(out_sem, 1)

        @block.scalar
        def _(act):
            chain = Chain(act, act_chain)
            act.dma_start(vecs[:], vec).then_inc(tables, 16)
            act.dma_start(cst[:], const).then_inc(tables, 16)
            act.dma_start(mraw[:], memT).then_inc(mem_in, 16)
            act.dma_start(X[:], xT).then_inc(x_loaded, 16)
            act.nop().then_inc(evac["act"], 2)
            act.wait_ge(tables, 32)

            def square(name, k, src, width=S):
                if k >= 2:
                    act.wait_ge(norm_s["acc"], KT * NORMS.index(name) + k - 1)
                act.activation(squares[:, k % 2, 0:width], src[:, k, :], ACT.Square).then_inc(norm_s["sq"], 1)

            def root(name, width=S):
                act.wait_ge(norm_s["ssq"], NORMS.index(name) + 1)
                act.activation(rstd[:, 0:width], sums(width), ACT.Sqrt, bias=eps_col, scale=1.0 / D).then_inc(norm_s["r"], 1)

            def high(name, k):
                act.wait_ge(norm_s["t"], tiles_before(name) + k + 1)
                act.copy(Hhi[:, k, :], T[:, k % 2, :]).then_inc(norm_s["hi"], 1)

            def norm(name, phase):
                for k in range(KT):
                    act.wait_ge(evac["dve"], 3 + BASE[phase]["dve"] + k)
                    square(name, k, X)
                if name == "nmix1":
                    act.dma_start(scratch[0], X[:]).then_inc(x_saved, 16)
                if name == "nfin":
                    act.dma_start(alow_w[:], alpha_w).then_inc(g_in, 16)
                    act.dma_start(aup_w[:], alpha_up).then_inc(g_in, 16)
                    act.dma_start(pmask[:], pair_masks).then_inc(g_in, 16)
                root(name)
                for k in range(KT):
                    high(name, k)

            def empty(n, par, dst, width=S):
                wait_apart(act, job_done, n + 1)
                act.copy(dst, G[:, par, 0:width]).then_inc(evac["act"], 1)

            def start():
                act.wait_ge(mem_in, 16)
                for k in range(KT):
                    square("nmem", k, mraw, MEM)
                root("nmem", MEM)
                for m in range(4):
                    empty(START["mem0"] + m, m % 2, MK[:, m, :], MEM)
                act.wait_ge(x_loaded, 16)
                for k in range(KT):
                    square("nmix0", k, X)
                for m in range(4):
                    empty(START["mem0"] + 4 + m, m % 2, MT[:, m % 2, :], MEM)
                root("nmix0")
                for k in range(KT):
                    empty(START["mem1"] + k, k % 2, MK1[:, k, :] if k < 4 else MT[:, k % 2, :], MEM)
                    high("nmix0", k)
                act.wait_ge(mvc, 8)
                act.wait_ge(evac["act"], 2 + MEM_JOBS)
                act.dma_start(kv_tiles[0], MK1[:].rearrange("p a n -> p (a n)")).then_inc(kv_saved, 16)
                act.dma_start(kv_tiles[1], MV1[:].rearrange("p t a n -> p (t a n)")).then_inc(kv_saved, 16)

            def attention(s, i, par, subs, nk, dst, scale, sink=None):
                U = NBLK * subs

                def exp(u):
                    if u >= 2:
                        act.wait_ge(s["pt"], i * U + (u - 1))
                    if u >= 4:
                        act.wait_ge(s["os"], i * NBLK + ((u - 4) // subs + 1))
                    wait_apart(act, s["mx"], i * U + (u + 1))
                    t = u % 4
                    negm = stat[:, 4 + t:5 + t]
                    if sink:
                        act.activation(stat[:, 12 + t:13 + t], sink(u % subs), ACT.Exp, bias=negm)
                        src = probs[:, u % 2, :]
                    else:
                        src = scored(par, u, nk * P)
                    act.activation(probs[:, u % 2, 0:nk * P], src, ACT.Exp, bias=negm, scale=scale,
                                   accum_out=stat[:, 8 + t:9 + t]).then_inc(s["pr"], 1)

                def copies(u):
                    act.wait_ge(s["pt"], i * U + (u + 1))
                    if u >= 2:
                        act.wait_ge(s["pv"], i * U + (u - 1))
                    act.copy(probsT[:, u % 2, 0:nk * P], AUX[:, 2, 0:nk * P]).then_inc(s["pc"], 1)

                def result(b):
                    wait_apart(act, s["ot"], i * NBLK + (b + 1))
                    act.copy(dst(b), G[:, par, 512:512 + P]).then_inc(s["oc"], 1)

                exp(0)
                for u in range(U):
                    if u + 1 < U:
                        exp(u + 1)
                    copies(u)
                    if u >= 2 and (u - 1) % subs == 0:
                        result((u - 2) // subs)
                if (U - 2) % subs == subs - 1:
                    result((U - 2) // subs)
                result(NBLK - 1)

            def mem_attention(l):
                name = f"mq{l}"
                with act.Fori(0, 2) as i:
                    for par in range(2):
                        head = i * 2 + par
                        empty(i * 2 + (START[name] + par), par, T[:, 0, :])
                        attention(attns["am"], head + MEM_HEADS * l, par, 1, 2,
                                  lambda b: mo[:, bass.ds(head, 1), b * P:(b + 1) * P].rearrange("p a n -> p (a n)"),
                                  MEM_SCALE)

            def window():
                act.wait_ge(kv_saved, 32)
                for n, t in enumerate((sin, cos)):
                    act.wait_ge(trig, n + 1)
                    chain.link(act.activation(t[:], t[:], ACT.Sin))
                for par in range(2):
                    empty(START["k"] + par, par, T[:, 0, :])
                    for h in range(2):
                        act.wait_ge(kdup, 2 * par + h + 1)
                        act.copy(keys[:, 2 * par + h, P:P + S], AUX[:, 0:2, :].rearrange("p a n -> p (a n)"))\
                           .then_inc(kcopied, 1)
                for par in range(2):
                    if par:
                        act.wait_ge(vt, par)
                    empty(START["v"] + par, par, T[:, 0, :])
                act.wait_ge(vt, 2)
                with act.Fori(0, KV) as g:
                    for par in range(2):
                        empty(g * 2 + (START["q"] + par), par, T[:, 0, :])
                        attention(attns["aw"], g * 2 + par, par, 2, 3,
                                  lambda b: mixed[:, bass.ds(g * 2 + par, 1), b * P:(b + 1) * P].rearrange("p a n -> p (a n)"),
                                  SINK_SCALE, lambda h: dcol("sinks", g * 4 + (2 * par + h)))

            def project_out(l):
                if l == 0:
                    act.wait_ge(attns["aw"]["oc"], KT * NBLK)
                act.wait_ge(attns["am"]["oc"], (l + 1) * MEM_HEADS * NBLK)
                if l == 0:
                    act.dma_start(MK[:].rearrange("p a n -> p (a n)"), kv_tiles[0]).then_inc(kv_in, 16)
                    act.dma_start(MV[:].rearrange("p t a n -> p (t a n)"), kv_tiles[1]).then_inc(kv_in, 16)
                for k in range(EARLY, KT):
                    act.copy(Hhi[:, k, :], mixed[:, k, :]).then_inc(split_hi[l], 1)
                for k in range(MEM_HEADS):
                    act.copy(MOhi[:, k, :], mo[:, k, :]).then_inc(split_hi[l], 1)
                act.wait_ge(split_lo[l], KT - EARLY + MEM_HEADS)
                act.dma_start(X[:], xT if l == 0 else scratch[0]).then_inc(x_back[l], 16)

            def mlp(l):
                norm(f"nmlp{l}", f"wo_mem{l}")
                n0 = START[f"up{l}0"]
                with act.Fori(0, 4) as c:
                    with act.Fori(0, 4) as i:
                        for par in range(2):
                            act.wait_ge(job_done, c * 16 + i * 2 + (n0 + par + 1))
                            act.activation(T[:, par, :], G[:, par, :], ACT.Relu).then_inc(evac["act"], 1)
                            wait_apart(act, evac["act"], c * 8 + i * 2 + (3 + BASE[f"up{l}0"]["act"] + par))
                            act.activation(Uhi[:, bass.ds(i * 2 + par, 1), :].rearrange("p a n -> p (a n)"), T[:, par, :],
                                           ACT.Square).then_inc(up_hi[l], 1)
                        act.wait_ge(up_lo[l], c * 8 + i * 2 + 2)

            def lru():
                act.wait_ge(l_dec, 1)
                act.activation(decay_c[:, 16:32], decay_c[:, 0:16], ACT.Exp, scale=-1.0).then_inc(l_de, 1)
                def input_of(j, par):
                    wait_apart(act, job_done, j * 2 + (START["lru"] + 1))
                    act.copy(xb[:, 1:S + 1], G[:, 0, :]).then_inc(evac["act"], 1)
                    block = lru_w[bass.ds(j, 1)].rearrange("a p g n -> (a p) g n")
                    act.dma_start(lw[:, par], block).then_inc(lw_in[par], 16)

                def block_of(j, par, last=False):
                    wait_apart(act, job_done, j * 2 + (START["lru"] + 2))
                    act.activation(gl[:], G[:, 1, :], ACT.Gelu_apprx_tanh).then_inc(evac["act"], 1)
                    for dr in range(2):
                        wait_apart(act, l_mm, j * 2 + (dr + 1))
                        for g, (dst, b) in enumerate(((rg, "lru_ba"), (ig, "lru_bx"))):
                            act.activation(dst[:, dr], AUX[:, 2 * g:2 * g + 2, :].rearrange("p a n -> p (a n)"),
                                           ACT.Sigmoid, bias=dcol(b, j + 8 * dr)).then_inc(l_sig, 1)
                    if not last:
                        input_of(j + 1, 1 - par)
                    wait_apart(act, l_sig, j * 4 + 4)
                    for dr in range(2):
                        c = decay_c[:, bass.ds(j + (80 + 8 * dr), 1)]
                        act.activation(av[:, dr], rg[:, dr], ACT.Exp, scale=c).then_inc(l_exp, 1)
                        act.activation(rg[:, dr], rg[:, dr], ACT.Tanh, scale=c).then_inc(l_exp, 1)
                    for dr in range(2):
                        act.wait_ge(l_e, j * 2 + (dr + 1))
                        act.activation(T[:, dr], T[:, dr], ACT.Sqrt, scale=-1.0).then_inc(l_sq, 1)
                    act.wait_ge(l_y, j + 1)

                input_of(0, 0)
                with act.Fori(0, 3) as i:
                    for par in range(2):
                        block_of(i * 2 + par, par)
                block_of(6, 0)
                block_of(7, 1, last=True)

            def gla():
                def queries(n0):
                    act.wait_ge(job_done, n0 + 1)
                    act.activation(gq[:], G[:, 0, :], ACT.Copy, scale=P ** -0.5).then_inc(evac["act"], 1)
                    empty(n0 + 1, 1, gk[:])

                act.wait_ge(g_low, 1)
                act.copy(alow[:], AUX[0:RANK, 0:2, :].rearrange("p a n -> p (a n)")).then_inc(g_lowc, 1)
                queries(START["gla"])
                for h in range(KV):
                    act.wait_ge(g_z, h + 1)
                    if h >= 2:
                        act.wait_ge(g_zero, h - 1)
                    t = T[:, h % 2, :]
                    act.activation(t, AUX[:, 2 * (h % 2):2 * (h % 2) + 2, :].rearrange("p a n -> p (a n)"),
                                   ACT.Abs, bias=vcol("b_alpha", h)).then_inc(g_abs, 1)
                    act.wait_ge(g_abs, h + 1)
                    chain.link(act.activation(t, t, ACT.Exp, scale=-1.0))
                    chain.link(act.activation(t, t, ACT.Ln, bias=1.0))
                act.wait_ge(g_zero, KV)
                act.wait_ge(x2_saved, 16)
                def head(h, last=False):
                    n0 = h * 6 + START["gla"]
                    head = gsum[:, bass.ds(h, 1), :].rearrange("p a n -> p (a n)")

                    def decay(step):
                        act.wait_ge(g_diff, h * 7 + step)
                        if step < 7:
                            chain.link(act.activation(dec[:], dec[:], ACT.Abs))
                        act.activation(dec[:], dec[:], ACT.Exp, scale=-1.0 / TAU).then_inc(g_exp, 1)

                    def values(n):
                        act.wait_ge(g_vt, h * 2 + (n + 1))
                        act.copy(vtok[:, :, n * P:(n + 1) * P], AUX[:, 2:4, :].rearrange("p a (b n) -> p (a b) n", n=P))\
                           .then_inc(g_vc, 1)

                    def gate(n):
                        wait_apart(act, job_done, n0 + (5 + n))
                        act.activation(ya[:, bass.ds(h * 2 + n, 1), :].rearrange("p a n -> p (a n)"), G[:, n, :], ACT.Silu)\
                           .then_inc(evac["act"], 1)

                    decay(1)
                    decay(2)
                    empty(n0 + 2, 0, T[:, 0, :])
                    decay(3)
                    values(0)
                    empty(n0 + 3, 1, T[:, 1, :])
                    decay(4)
                    values(1)
                    decay(5)
                    gate(0)
                    decay(6)
                    gate(1)
                    decay(7)
                    act.wait_ge(g_kt, h + 1)
                    act.copy(ktok[:], AUX[:, 2:4, :].rearrange("p a (b n) -> p (a b) n", n=P)).then_inc(g_kc, 1)
                    wait_apart(act, g_dk, h * 7 + 7)
                    act.activation(chunk_decay[:], gsum[:, bass.ds(h, 1), CHUNK - 1::CHUNK].rearrange("p a n -> p (a n)"),
                                   ACT.Exp, scale=1.0 / TAU).then_inc(g_cd, 1)
                    act.activation(dec[:], head, ACT.Exp, scale=1.0 / TAU).then_inc(g_exp, 1)
                    act.wait_ge(g_dq, h * 7 + 7)
                    for half in range(2):
                        act.wait_ge(g_o, h * 2 + (half + 1))
                        for d in range(2):
                            act.copy(results[:, half, d, :], AUX[:, 2 + d, :]).then_inc(g_oc, 1)
                    if not last:
                        queries(n0 + 6)
                    act.wait_ge(g_oc, h * 4 + 4)
                    for d in range(2):
                        act.activation(T[:, d, :].rearrange("p (a n) -> p a n", a=2), results[:, :, d, :], ACT.Square)\
                           .then_inc(g_sq, 1)
                    act.wait_ge(g_ssq, h + 1)
                    act.activation(dec[:], sums(S), ACT.Sqrt, bias=stat[:, 31:32], scale=1.0 / (2 * P)).then_inc(g_r, 1)

                with chain.loop(KV - 1, 6) as h:
                    head(h)
                chain.turn = None
                head(KV - 1, last=True)
                act.wait_ge(g_y, KV)

            def pooling():
                act.dma_start(inv_cnt[:], inv_count).then_inc(p_in, 16)

                def pair(g):
                    for par in range(2):
                        empty(g * 2 + (START["pool"] + par), par, T[:, par, :])

                def group(g):
                    for m in range(2):
                        wait_apart(act, p_mm, g + 1)
                        act.activation(yb[:, bass.ds(g * 2 + m, 1), :].rearrange("p a n -> p (a n)"),
                                       AUX[:, 2 * m:2 * m + 2, :].rearrange("p a n -> p (a n)"),
                                       ACT.Copy, scale=dcol("pool_scale", g * 2 + m)).then_inc(p_used, 1)

                act.dma_start(pool_m[:], pool_w[0]).then_inc(p_m, 16)
                pair(0)
                with act.Fori(0, KV - 1) as g:
                    act.wait_ge(p_pool, g * 2 + 2)
                    pair(g + 1)
                    group(g)
                    act.dma_start(pool_m[:], pool_w[bass.ds(g + 1, 1)].rearrange("a p k n -> (a p) k n")).then_inc(p_m, 16)
                group(KV - 1)
                act.wait_ge(p_used, KT)

            def gates():
                with act.Fori(0, 4) as i:
                    for par in range(2):
                        act.wait_ge(job_done, i * 2 + (START["gate_b"] + par + 1))
                        act.activation(T[:, par, :], G[:, par, :], ACT.Silu).then_inc(evac["act"], 1)
                    act.wait_ge(b_y, i * 2 + 2)
                with act.Fori(0, 8) as i:
                    for par in range(2):
                        wait_apart(act, job_done, i * 2 + (START["merge"] + par + 1))
                        act.activation(T[:, par, :], G[:, par, :], ACT.Sigmoid, bias=dcol("b_merge", i * 2 + par))\
                           .then_inc(evac["act"], 1)
                        act.wait_ge(evac["act"], i * 2 + (BASE["merge"]["act"] + par + 3))
                        act.dma_start(gate_tiles[bass.ds(i * 2 + par, 1)].rearrange("a p n -> (a p) n"),
                                      T[:, par, :]).then_inc(gates_out[par], 16)
                    act.copy(tile_of(ya_hi, i), tile_of(ya, i)).then_inc(s_hi, 1)
                    for par in range(2):
                        act.wait_ge(gates_out[par], i * 16 + 16)

            def projections():
                for par in range(2):
                    act.dma_start(T[:, par, :], gate_tiles[par]).then_inc(gates_in[par], 16)
                act.wait_ge(job_done, START["proj_a"])
                with act.Fori(0, 4) as i:
                    for par in range(2):
                        act.copy(tile_of(yb_hi, i * 2 + par), tile_of(yb, i * 2 + par)).then_inc(s_hi, 1)
                        act.wait_ge(merged, i * 2 + (par + 1))
                        act.dma_start(T[:, par, :], tile_at(gate_tiles, i * 2 + (2 + par))).then_inc(gates_in[par], 16)

                def both_high(m, par, i=None):
                    wait_apart(act, merged, m + 9)
                    if i is not None:
                        act.dma_start(T[:, par, :], tile_at(gate_tiles, m + 10)).then_inc(gates_in[par], 16)
                    act.copy(tile_of(both_hi, m), tile_of(both, m)).then_inc(s_hi, 1)
                    act.wait_ge(s_lo, m + 17)
                    act.dma_start(tile_of(X2, m), tile_of(scratch[0], m)).then_inc(x2_back, 16)

                with act.Fori(0, 3) as i:
                    for par in range(2):
                        both_high(i * 2 + par, par, i)
                for par in range(2):
                    both_high(6 + par, par)

            def layer_norm():
                for k in range(KT):
                    act.wait_ge(n_cent, k + 1)
                    if k >= 2:
                        act.wait_ge(n_acc, k - 1)
                    act.activation(T[:, k % 2, :], X2[:, k, :], ACT.Square).then_inc(n_sq, 1)
                act.wait_ge(n_ssq, 1)
                act.activation(ln_stat[:], sums(S), ACT.Sqrt, bias=stat[:, 31:32], scale=1.0 / D).then_inc(n_r, 1)
                for k in range(KT):
                    act.wait_ge(n_y, k + 1)
                    act.activation(X2[:, k, :], X2[:, k, :], ACT.Identity, bias=vcol("ln_b", k)).then_inc(n_b, 1)
                    act.wait_ge(n_b, k + 1)
                    act.dma_start(out[:, k, :], X2[:, k, :]).then_inc(out_done, 16)

            start()
            act.wait_ge(norm_s["lo"], tiles_before("nmix0") + KT)
            act.dma_start(sin[:].bitcast(I32), pos).then_inc(pos_in, 16)
            act.dma_start(wmask[:], masks).then_inc(masks_in, 16)
            mem_attention(0)
            window()
            project_out(0)
            mlp(0)
            norm("nmix1", "down03")
            act.wait_ge(norm_s["lo"], tiles_before("nmix1") + KT)
            act.wait_ge(x_saved, 16)
            mem_attention(1)
            lru()
            project_out(1)
            mlp(1)
            norm("nfin", "down13")
            act.wait_ge(norm_s["lo"], tiles_before("nfin") + KT)
            act.dma_start(scratch[0], X[:]).then_inc(x2_saved, 16)
            gla()
            pooling()
            gates()
            projections()
            layer_norm()
            act.wait_ge(out_done, 16 * KT)

        @block.vector
        def _(dve):
            chain = Chain(dve, dve_chain)
            dve.nop().then_inc(evac["dve"], 2)
            dve.memset(eps_col, EPS)
            dve.memset(stat[:, 31:32], EPS_2)
            dve.wait_ge(tables, 32)

            def add_square(name, k, width=S):
                r = KT * NORMS.index(name)
                dve.wait_ge(norm_s["sq"], r + k + 1)
                if k == 0:
                    dve.tensor_copy(acc[:, 0:width], squares[:, 0, 0:width]).then_inc(norm_s["acc"], 1)
                else:
                    dve.tensor_tensor(acc[:, 0:width], acc[:, 0:width], squares[:, k % 2, 0:width], ALU.add)\
                       .then_inc(norm_s["acc"], 1)
                dve.wait_ge(norm_s["acc"], r + k + 1)

            def invert(name, width=S):
                r = NORMS.index(name)
                dve.wait_ge(norm_s["r"], r + 1)
                dve.reciprocal(rstd[:, 0:width], rstd[:, 0:width]).then_inc(norm_s["var"], 1)
                dve.wait_ge(norm_s["var"], r + 1)

            def split_norm(name, gain, inplace=False, also=None):
                s, r = norm_s, tiles_before(name)

                def scaled(k):
                    if k >= 2:
                        dve.wait_ge(s["lo"], r + k - 1)
                    if inplace:
                        chain.link(dve.scalar_tensor_tensor(X[:, k, :], X[:, k, :], gain(k), rstd[:], ALU.mult, ALU.mult))
                        dve.tensor_copy(T[:, k % 2, :], X[:, k, :]).then_inc(s["t"], 1)
                    else:
                        dve.scalar_tensor_tensor(T[:, k % 2, :], X[:, k, :], gain(k), rstd[:], ALU.mult, ALU.mult)\
                           .then_inc(s["t"], 1)

                scaled(0)
                for k in range(KT):
                    if k + 1 < KT:
                        scaled(k + 1)
                    if also:
                        also(k)
                    dve.wait_ge(s["hi"], r + k + 1)
                    dve.tensor_tensor(Hlo[:, k, :], T[:, k % 2, :], Hhi[:, k, :], ALU.subtract).then_inc(s["lo"], 1)

            def norm(name, gain, inplace=False):
                invert(name)
                split_norm(name, gain, inplace)

            def start():
                for k in range(KT):
                    add_square("nmem", k, MEM)
                invert("nmem", MEM)
                for k in range(KT):
                    dve.scalar_tensor_tensor(mraw[:, k, :], mraw[:, k, :], vcol("mem_norm", k), rstd[:, 0:MEM],
                                             ALU.mult, ALU.mult).then_inc(mem_ready, 1)

                def values(dst, m, turn):
                    dve.wait_ge(mvt, turn + 1)
                    dve.tensor_copy(dst[:, :, m, :], AUX[:, 2, 0:MEM].rearrange("p (t n) -> p t n", t=2)).then_inc(mvc, 1)

                for k in range(KT):
                    add_square("nmix0", k)
                for m in range(4):
                    values(MV, m, m)
                invert("nmix0")
                split_norm("nmix0", lambda k: vcol("mix_norm", k), also=lambda k: values(MV1, k - 4, k) if k >= 4 else None)

            def attention(s, i, par, subs, nk, scale, sink):
                U = NBLK * subs
                dim = P // subs

                def peak(u):
                    t = u % 4
                    mx, negm = stat[:, t:t + 1], stat[:, 4 + t:5 + t]
                    if sink and u >= 2:
                        dve.wait_ge(s["pt"], i * U + (u - 1))
                    wait_apart(dve, s["sc"], i * U + (u + 1))
                    if sink:
                        m = {0: 0, NBLK - 1: 2}.get(u // subs, 1)
                        chain.link(dve.tensor_tensor_reduce(probs[:, u % 2, :], scored(par, u, nk * P), wmask[:, m, :],
                                                            1.0, -3e38, ALU.add, ALU.max, mx))
                        dve.tensor_scalar(negm, mx, -scale, stat[:, 20 + u % subs:21 + u % subs], ALU.mult, ALU.min)\
                           .then_inc(s["mx"], 1)
                    else:
                        chain.link(dve.reduce_max(mx, scored(par, u, nk * P), AX_X))
                        dve.tensor_scalar(negm, mx, -scale, None, ALU.mult).then_inc(s["mx"], 1)

                def scale_out(b):
                    dve.wait_ge(s["pr"], i * U + (b + 1) * subs)
                    t = b * subs % 4
                    total = stat[:, 8 + t:8 + t + subs]
                    if sink:
                        chain.link(dve.tensor_tensor(total, total, stat[:, 12 + t:12 + t + subs], ALU.add))
                    inv = stat[:, 16 + t:16 + t + subs]
                    chain.link(dve.reciprocal(inv, total))
                    dve.wait_ge(s["pv"], i * U + (b + 1) * subs)
                    if b >= 2:
                        dve.wait_ge(s["ot"], i * NBLK + (b - 1))
                    dve.tensor_tensor(O_sb[:, b % 2, :].rearrange("p (h d) -> p h d", h=subs),
                                      AUX[:, 3, 0:P].rearrange("p (h d) -> p h d", h=subs),
                                      inv.rearrange("p (h a) -> p h a", a=1).broadcast_to([P, subs, dim]), ALU.mult)\
                       .then_inc(s["os"], 1)

                if sink:
                    for h in range(subs):
                        chain.link(dve.tensor_scalar(stat[:, 20 + h:21 + h], sink(h), -1.0, None, ALU.mult))
                peak(0)
                peak(1)
                for u in range(U):
                    if u and u % subs == 0:
                        scale_out(u // subs - 1)
                    if u + 2 < U:
                        peak(u + 2)
                scale_out(NBLK - 1)

            def mem_attention(l):
                with chain.loop(2, 2 * NBLK * 2) as i:
                    for par in range(2):
                        attention(attns["am"], i * 2 + (par + MEM_HEADS * l), par, 1, 2, MEM_SCALE, None)

            def angles():
                dve.wait_ge(pos_in, 16)
                turn = 2 * np.pi
                c1 = 6.28125
                c2 = float((np.array(turn - c1, np.float32).view(np.uint32) & np.uint32(0xFFFFF000)).view(np.float32))
                c3 = float(np.float32(turn - c1 - c2))
                big = 1.5 * 2.0 ** 23
                a, k = mixed[:, 0, :], mixed[:, 1, :]
                chain.link(dve.tensor_copy(k, sin[:].bitcast(I32)))
                chain.link(dve.tensor_scalar(a, k, freq, None, ALU.mult))
                for n, (t, quarter) in enumerate(((sin, 0.0), (cos, 0.25))):
                    chain.link(dve.tensor_scalar(k, a, float(1.0 / turn), quarter, ALU.mult, ALU.add))
                    chain.link(dve.tensor_scalar(k, k, big, None, ALU.add))
                    chain.link(dve.tensor_scalar(k, k, -big, None, ALU.add))
                    chain.link(dve.scalar_tensor_tensor(t[:], k, -c1, a, ALU.mult, ALU.add))
                    chain.link(dve.scalar_tensor_tensor(t[:], k, -c2, t[:], ALU.mult, ALU.add))
                    chain.link(dve.scalar_tensor_tensor(t[:], k, -c3, t[:], ALU.mult, ALU.add))
                    chain.link(dve.tensor_scalar(t[:], t[:], float(quarter * turn), float(np.float32(3.1415925)), ALU.add, ALU.min))
                    dve.tensor_scalar(t[:], t[:], -float(np.float32(3.1415925)), None, ALU.max).then_inc(trig, 1)
                    dve.wait_ge(trig, n + 1)

            def rotate(r, heads=False):
                dve.wait_ge(rot_sw, r + 1)
                chain.link(dve.tensor_tensor(T[:, 1, :], AUX[:, 0:2, :].rearrange("p a n -> p (a n)"), sin[:], ALU.mult))
                chain.link(dve.tensor_tensor(T[:, 0, :], T[:, 0, :], cos[:], ALU.mult))
                if not heads:
                    dve.tensor_tensor(T[:, 0, :], T[:, 0, :], T[:, 1, :], ALU.add).then_inc(rot_ok, 1)
                    return
                chain.link(dve.tensor_tensor(T[:, 0, :], T[:, 0, :], T[:, 1, :], ALU.add))
                at = CCOLS["half"]
                chain.link(dve.tensor_scalar(T[:, 1, :], T[:, 0, :], cst[:, at + 1:at + 2], None, ALU.mult))
                dve.tensor_scalar(T[:, 0, :], T[:, 0, :], cst[:, at:at + 1], None, ALU.mult).then_inc(rot_ok, 1)

            def window():
                dve.wait_ge(masks_in, 16)
                dve.wait_ge(act_chain, 2)
                for r in range(2):
                    rotate(r)
                dve.wait_ge(rot_ok, 2)
                for par in range(2):
                    dve.wait_ge(vt, par + 1)
                    dve.tensor_copy(vals[:, 1:NBLK + 1, par * P:(par + 1) * P],
                                    AUX[:, 0:2, :].rearrange("p a (b n) -> p (a b) n", n=P)).then_inc(vcopied, 1)
                with chain.loop(KV, 2 * (4 + 2 + 16 + 2 * NBLK)) as g:
                    for par in range(2):
                        rotate(g * 2 + (2 + par), True)
                        attention(attns["aw"], g * 2 + par, par, 2, 3, SINK_SCALE,
                                  lambda h: dcol("sinks", g * 4 + (2 * par + h)))

            def add_last_to_x(phase, name):
                for m in range(KT):
                    dve.wait_ge(job_done, START[phase] + m + 1)
                    dve.tensor_tensor(X[:, m, :], G[:, m % 2, :], X[:, m, :], ALU.add).then_inc(evac["dve"], 1)
                    if m:
                        add_square(name, m - 1)
                add_square(name, KT - 1)
                dve.wait_ge(evac["dve"], 2 + BASE[phase]["dve"] + KT)

            def add_to_x(name):
                with dve.Fori(0, 4) as i:
                    for par in range(2):
                        m = i * 2 + par
                        dve.wait_ge(job_done, i * 2 + (START[name] + par + 1))
                        xm = X[:, bass.ds(m, 1), :].rearrange("p a n -> p (a n)")
                        dve.tensor_tensor(xm, G[:, par, :], xm, ALU.add).then_inc(evac["dve"], 1)

            def project_out(l):
                for k in range(EARLY, KT):
                    dve.wait_ge(split_hi[l], k - EARLY + 1)
                    dve.tensor_tensor(Hlo[:, k, :], mixed[:, k, :], Hhi[:, k, :], ALU.subtract).then_inc(split_lo[l], 1)
                for k in range(MEM_HEADS):
                    dve.wait_ge(split_hi[l], KT - EARLY + k + 1)
                    dve.tensor_tensor(MOlo[:, k, :], mo[:, k, :], MOhi[:, k, :], ALU.subtract).then_inc(split_lo[l], 1)
                dve.wait_ge(x_back[l], 16)
                add_to_x(f"wo_mixed{l}")
                dve.wait_ge(evac["dve"], 2 + BASE[f"wo_mem{l}"]["dve"])
                add_last_to_x(f"wo_mem{l}", f"nmlp{l}")

            def mlp(l):
                norm(f"nmlp{l}", lambda k: vcol("mlp_norm", 8 * l + k))
                n0 = START[f"up{l}0"]
                a0, d0 = BASE[f"up{l}0"]["act"], BASE[f"up{l}0"]["dve"]

                def chunk(c):
                    with dve.Fori(0, 4) as i:
                        for par in range(2):
                            dve.wait_ge(evac["act"], i * 2 + c * 8 + (a0 + par + 3))
                            dve.wait_ge(up_hi[l], i * 2 + c * 8 + (par + 1))
                            dve.tensor_tensor(T[:, par, :], T[:, par, :], T[:, par, :], ALU.mult).then_inc(up_sq[l], 1)
                            dve.wait_ge(up_sq[l], i * 2 + c * 8 + (par + 1))
                            m = bass.ds(i * 2 + par, 1)
                            dve.tensor_tensor(Ulo[:, m, :].rearrange("p a n -> p (a n)"), T[:, par, :],
                                              Uhi[:, m, :].rearrange("p a n -> p (a n)"), ALU.subtract).then_inc(up_lo[l], 1)

                with dve.Fori(0, 3) as c:
                    chunk(c)
                    with dve.Fori(0, 4) as i:
                        for par in range(2):
                            dve.wait_ge(job_done, c * 16 + i * 2 + (n0 + 8 + par + 1))
                            xm = X[:, bass.ds(i * 2 + par, 1), :].rearrange("p a n -> p (a n)")
                            dve.tensor_tensor(xm, G[:, par, :], xm, ALU.add).then_inc(evac["dve"], 1)
                    dve.wait_ge(evac["dve"], c * 8 + (d0 + 8 + 2))
                chunk(3)
                add_last_to_x(f"down{l}3", "nmix1" if l == 0 else "nfin")

            def lru():
                lam = vecs[:, VCOLS["lam"]:VCOLS["lam"] + 16]
                e, z, z2, s = (decay_c[:, 16 * n:16 * n + 16] for n in (1, 2, 3, 4))
                c = decay_c[:, 80:96]
                dve.tensor_scalar(s, lam, -1.0, None, ALU.mult).then_inc(l_dx, 1)
                dve.wait_ge(l_dx, 1)
                dve.tensor_tensor(decay_c[:, 0:16], lam, s, ALU.max).then_inc(l_dec, 1)
                chain.link(dve.tensor_scalar(c, s, 0.0, None, ALU.max))
                dve.wait_ge(l_de, 1)
                chain.link(dve.tensor_scalar(z, e, 2.0, None, ALU.add))
                chain.link(dve.reciprocal(z, z))
                chain.link(dve.tensor_tensor(z, z, e, ALU.mult))
                chain.link(dve.tensor_tensor(z2, z, z, ALU.mult))
                chain.link(dve.memset(s, 1.0 / 19))
                for n in range(8, -1, -1):
                    chain.link(dve.tensor_tensor(s, s, z2, ALU.mult))
                    chain.link(dve.tensor_scalar(s, s, 1.0 / (2 * n + 1), None, ALU.add))
                chain.link(dve.tensor_tensor(s, s, z, ALU.mult))
                chain.link(dve.scalar_tensor_tensor(c, s, 2.0, c, ALU.mult, ALU.add))
                dve.tensor_scalar(c, c, -8.0, None, ALU.mult).then_inc(l_dx, 1)
                dve.wait_ge(l_dx, 2)
                dve.wait_ge(pads, 2)

                def convolve(j, par):
                    dve.wait_ge(evac["act"], j * 2 + (BASE["lru"]["act"] + 3))
                    x = xc[par][:]
                    chain.link(dve.tensor_scalar(x, xb[:, 0:S], dcol("conv_w", j), dcol("conv_b", j), ALU.mult, ALU.add))
                    for tap in range(1, 4):
                        ins = dve.scalar_tensor_tensor(x, xb[:, tap:tap + S], dcol("conv_w", j + 8 * tap), x, ALU.mult, ALU.add)
                        if tap < 3:
                            chain.link(ins)
                        else:
                            ins.then_inc(l_xc, 1)

                def block_of(j, par, last=False):
                    if not last:
                        convolve(j + 1, 1 - par)
                    for dr in range(2):
                        dve.wait_ge(l_exp, j * 4 + (2 * dr + 2))
                        dve.wait_ge(l_a2, j * 2 + (dr + 1))
                        dve.scalar_tensor_tensor(T[:, dr], T[:, dr], 1.0, rg[:, dr], ALU.add, ALU.mult).then_inc(l_e, 1)
                    for dr in range(2):
                        dve.wait_ge(l_sq, j * 2 + (dr + 1))
                        dve.wait_ge(l_ix, j * 2 + (dr + 1))
                        chain.link(dve.tensor_tensor(ig[:, dr], ig[:, dr], T[:, dr], ALU.mult))
                        if dr == 0:
                            chain.link(dve.tensor_tensor_scan(rg[:, 0], av[:, 0], ig[:, 0], 0.0, ALU.mult, ALU.add))
                        else:
                            chain.link(dve.tensor_tensor_scan(rg[:, 1, ::-1], av[:, 1, ::-1], ig[:, 1, ::-1], 0.0,
                                                              ALU.mult, ALU.add))
                    dve.tensor_tensor(rg[:, 0], rg[:, 0], rg[:, 1], ALU.add).then_inc(l_h, 1)
                    dve.wait_ge(l_h, j + 1)
                    dve.wait_ge(evac["act"], j * 2 + (BASE["lru"]["act"] + 4))
                    dve.tensor_tensor(mixed[:, bass.ds(j, 1), :].rearrange("p a n -> p (a n)"), rg[:, 0], gl[:], ALU.mult)\
                       .then_inc(l_y, 1)

                convolve(0, 0)
                with chain.loop(3, 14) as i:
                    for par in range(2):
                        block_of(i * 2 + par, par)
                block_of(6, 0)
                block_of(7, 1, last=True)
                dve.wait_ge(l_y, 8)

            def gla():
                dve.wait_ge(job_done, START["gla"])
                chain.link(dve.memset(starts[:], 1.0))
                chain.link(dve.memset(starts[:, ::CHUNK], 0.0))
                for h in range(KV):
                    dve.wait_ge(g_abs, h + 1)
                    low = zmin[:, h % 2, :]
                    dve.tensor_scalar(low, AUX[:, 2 * (h % 2):2 * (h % 2) + 2, :].rearrange("p a n -> p (a n)"),
                                      vcol("b_alpha", h), 0.0, ALU.add, ALU.min).then_inc(g_min, 1)
                    dve.wait_ge(g_min, h + 1)
                    dve.wait_ge(act_chain, 2 + 2 * (h + 1))
                    chain.link(dve.tensor_tensor(low, low, T[:, h % 2, :], ALU.subtract))
                    dve.tensor_tensor_scan(gsum[:, h, :], starts[:], low, 0.0, ALU.mult, ALU.add).then_inc(g_zero, 1)
                    dve.wait_ge(g_zero, h + 1)
                chain.link(dve.memset(wts[:], 0.0))
                dve.wait_ge(g_in, 48)
                with chain.loop(KV, 4) as h:
                    def difference(step):
                        size = CHUNK >> (step - 1) if step < 7 else CHUNK
                        ref = size // 2 - 1 if step < 7 else size - 1
                        if step > 1:
                            dve.wait_ge(g_dq, h * 7 + (min(step - 1, 6)))
                        g3 = gsum[:, bass.ds(h, 1), :].rearrange("p a (b n) -> p (a b) n", n=size)
                        dve.tensor_tensor(dec[:].rearrange("p (b n) -> p b n", n=size), g3,
                                          g3[:, :, ref:ref + 1].broadcast_to([P, S // size, size]), ALU.subtract)\
                           .then_inc(g_diff, 1)

                    def keep(step):
                        wait_apart(dve, g_w, h * 7 + (step + 1))
                        mask = pmask[:, step:step + 1, :].broadcast_to([P, NBLK, P])
                        dve.copy_predicated(wts[:], mask, AUX[:, 0:2, :].rearrange("p a (b n) -> p (a b) n", n=P))\
                           .then_inc(g_keep, 1)

                    for step in range(1, 8):
                        difference(step)
                        keep(step - 1)
                        dve.wait_ge(g_exp, h * 8 + step)
                        dve.tensor_tensor(dk[:], gk[:], dec[:], ALU.mult).then_inc(g_dk, 1)
                        dve.wait_ge(g_dk, h * 7 + step)
                    dve.memset(state[:, 0, :], 0.0).then_inc(g_s0, 1)
                    dve.wait_ge(g_s0, h + 1)
                    dve.wait_ge(g_cd, h + 1)
                    for c in range(S // CHUNK):
                        dve.wait_ge(g_up, h * 16 + (c + 1))
                        dve.scalar_tensor_tensor(state[:, (c + 1) % 2, :], state[:, c % 2, :], chunk_decay[:, c:c + 1],
                                                 AUX[:, c % 2, 0:2 * P], ALU.mult, ALU.add).then_inc(g_st, 1)
                        dve.wait_ge(g_st, h * 16 + (c + 1))
                    dve.wait_ge(g_sq, h * 2 + 2)
                    dve.tensor_tensor(T[:, 0, :], T[:, 0, :], T[:, 1, :], ALU.add).then_inc(g_ss, 1)
                    dve.wait_ge(g_r, h + 1)
                    chain.link(dve.reciprocal(dec[:], dec[:]))
                    for d in range(2):
                        o = results[:, :, d, :]
                        halves = dec[:].rearrange("p (a n) -> p a n", a=2)
                        chain.link(dve.scalar_tensor_tensor(o, o, dcol("gla_norm", h * 2 + d), halves, ALU.mult, ALU.mult))
                        m = ya[:, bass.ds(h * 2 + d, 1), :].rearrange("p b (a n) -> p (b a) n", a=2)
                        ins = dve.tensor_tensor(m, m, o, ALU.mult)
                        if d:
                            ins.then_inc(g_y, 1)
                        else:
                            chain.link(ins)
                dve.wait_ge(g_y, KV)

            def pooling():
                chain.link(dve.memset(unit[:], 1.0))
                chain.link(dve.memset(csum[:, 0:16], 0.0))
                dve.wait_ge(p_in, 16)
                for g, w in enumerate(WINDOWS):
                    for par in range(2):
                        u = T[:, par, :]
                        dve.wait_ge(evac["act"], 2 * g + par + 3 + BASE["pool"]["act"])
                        if g:
                            dve.wait_ge(p_mm, g)
                        chain.link(dve.tensor_tensor_scan(csum[:, 16:16 + S], unit[:], u, 0.0, ALU.mult, ALU.add))
                        chain.link(dve.tensor_tensor(pooled[:, par, :], csum[:, 16:16 + S], csum[:, 16 - w:16 - w + S],
                                                     ALU.subtract))
                        chain.link(dve.tensor_tensor(pooled[:, par, 0:16], pooled[:, par, 0:16], inv_cnt[:, g, :], ALU.mult))
                        chain.link(dve.tensor_tensor(pooled[:, par, 0:16], pooled[:, par, 0:16], u[:, 0:16], ALU.subtract))
                        dve.scalar_tensor_tensor(pooled[:, par, 16:S], pooled[:, par, 16:S], 1.0 / w, u[:, 16:S],
                                                 ALU.mult, ALU.subtract).then_inc(p_pool, 1)
                        dve.wait_ge(p_pool, 2 * g + par + 1)

            def gates():
                dve.wait_ge(p_used, 8)
                with dve.Fori(0, 4) as i:
                    for par in range(2):
                        dve.wait_ge(evac["act"], i * 2 + (BASE["gate_b"]["act"] + par + 3))
                        m = yb[:, bass.ds(i * 2 + par, 1), :].rearrange("p a n -> p (a n)")
                        dve.tensor_tensor(m, m, T[:, par, :], ALU.mult).then_inc(b_y, 1)
                dve.wait_ge(b_y, 8)

            def projections():
                with dve.Fori(0, KT) as k:
                    dve.wait_ge(s_hi, k + 1)
                    dve.tensor_tensor(tile_of(ya_lo, k), tile_of(ya, k), tile_of(ya_hi, k), ALU.subtract).then_inc(s_lo, 1)
                with dve.Fori(0, 4) as i:
                    for par in range(2):
                        m = i * 2 + par
                        dve.wait_ge(gates_in[par], i * 16 + 16)
                        dve.wait_ge(job_done, i * 2 + (START["proj_a"] + par + 1))
                        dve.tensor_tensor(tile_of(both, m), G[:, par, :], T[:, par, :], ALU.mult).then_inc(evac["dve"], 1)
                        dve.wait_ge(evac["dve"], i * 2 + (BASE["proj_a"]["dve"] + par + 3))
                        dve.memset(stat[:, 24:25], 0.0).then_inc(merged, 1)
                        dve.wait_ge(s_hi, i * 2 + (KT + par + 1))
                        dve.tensor_tensor(tile_of(yb_lo, m), tile_of(yb, m), tile_of(yb_hi, m), ALU.subtract).then_inc(s_lo, 1)
                with dve.Fori(0, 4) as i:
                    for par in range(2):
                        m = i * 2 + par
                        dve.wait_ge(gates_in[par], i * 16 + (64 + 16))
                        dve.wait_ge(job_done, i * 2 + (START["proj_b"] + par + 1))
                        dve.tensor_tensor(T[:, par, :], G[:, par, :], T[:, par, :], ALU.mult).then_inc(evac["dve"], 1)
                        dve.wait_ge(evac["dve"], i * 2 + (BASE["proj_b"]["dve"] + par + 3))
                        dve.tensor_tensor(tile_of(both, m), tile_of(both, m), T[:, par, :], ALU.add).then_inc(merged, 1)
                        dve.wait_ge(merged, i * 2 + (KT + par + 1))
                        dve.wait_ge(s_hi, i * 2 + (2 * KT + par + 1))
                        dve.tensor_tensor(tile_of(both_lo, m), tile_of(both, m), tile_of(both_hi, m), ALU.subtract)\
                           .then_inc(s_lo, 1)

            def layer_norm():
                dve.wait_ge(x2_back, KT * 16)
                for m in range(KT):
                    dve.wait_ge(job_done, START["out"] + m + 1)
                    dve.scalar_tensor_tensor(X2[:, m, :], X2[:, m, :], ALPHA, G[:, m % 2, :], ALU.mult, ALU.add)\
                       .then_inc(evac["dve"], 1)
                    dve.wait_ge(evac["dve"], 2 + BASE["out"]["dve"] + m + 1)
                    if m == 0:
                        dve.tensor_copy(ln_acc[:], X2[:, 0, :]).then_inc(n_sum, 1)
                    else:
                        dve.tensor_tensor(ln_acc[:], ln_acc[:], X2[:, m, :], ALU.add).then_inc(n_sum, 1)
                    dve.wait_ge(n_sum, m + 1)
                dve.wait_ge(n_mean, 1)
                chain.link(dve.tensor_scalar(ln_stat[:], AUX[:, 0:2, :].rearrange("p a n -> p (a n)"), 1.0 / D, None, ALU.mult))
                for k in range(KT):
                    dve.tensor_tensor(X2[:, k, :], X2[:, k, :], ln_stat[:], ALU.subtract).then_inc(n_cent, 1)
                for k in range(KT):
                    dve.wait_ge(n_sq, k + 1)
                    if k == 0:
                        dve.tensor_copy(ln_acc[:], T[:, 0, :]).then_inc(n_acc, 1)
                    else:
                        dve.tensor_tensor(ln_acc[:], ln_acc[:], T[:, k % 2, :], ALU.add).then_inc(n_acc, 1)
                    dve.wait_ge(n_acc, k + 1)
                dve.wait_ge(n_r, 1)
                chain.link(dve.reciprocal(ln_stat[:], ln_stat[:]))
                for k in range(KT):
                    dve.scalar_tensor_tensor(X2[:, k, :], X2[:, k, :], vcol("ln_g", k), ln_stat[:], ALU.mult, ALU.mult)\
                       .then_inc(n_y, 1)

            start()
            angles()
            mem_attention(0)
            window()
            project_out(0)
            mlp(0)
            norm("nmix1", lambda k: vcol("mix_norm", 8 + k))
            mem_attention(1)
            lru()
            project_out(1)
            mlp(1)
            norm("nfin", lambda k: vcol("final_norm", k), inplace=True)
            gla()
            pooling()
            gates()
            projections()
            layer_norm()



def feature_major(a):
    return np.ascontiguousarray(a.T.reshape(-1, P, a.shape[0]).transpose(1, 0, 2))


def vector_cols(a):
    return a.reshape(-1, P).T


def weight_jobs(w, rows=None):
    k, m = w.shape
    j = w.reshape(k // P, P, m // P, P).transpose(2, 1, 0, 3)
    if k < D:
        full = np.zeros((m // P, P, KT, P), w.dtype)
        full[:, :, :k // P] = j
        j = full
    return list(j.reshape(m // P, P, KT * P))


def constants():
    c = np.zeros((P, N_CONST), np.float32)
    c[:, CCOLS["ident"]:CCOLS["ident"] + P] = np.eye(P)
    c[:, CCOLS["ones"]:CCOLS["ones"] + P] = 1
    perm = np.zeros((P, P), np.float32)
    dup = np.zeros((P, 2, P), np.float32)
    for h in range(2):
        for f in range(8):
            perm[64 * h + 8 + f, 64 * h + f] = -1
            perm[64 * h + f, 64 * h + 8 + f] = 1
            c[64 * h + f, CCOLS["freq"]] = c[64 * h + 8 + f, CCOLS["freq"]] = np.float32(500000.0 ** (-2.0 * f / 16))
        c[64 * h:64 * h + 64, CCOLS["half"] + h] = 1
        for f in range(64):
            dup[64 * h + f, h, f] = dup[64 * h + f, h, 64 + f] = 1
    c[:, CCOLS["perm"]:CCOLS["perm"] + P] = perm
    c[:, CCOLS["dup"]:CCOLS["dup"] + 2 * P] = dup.reshape(P, 2 * P)
    q, k = np.arange(P)[:, None], np.arange(3 * P)[None, :]
    band = np.abs(k - P - q) <= 128
    masks = np.stack([np.where(band & ok, 0.0, NEG) for ok in (k >= P, k >= 0, k < 2 * P)], 1).astype(np.float32)
    t = np.arange(P)
    pairs = [np.eye(P, dtype=bool)]
    for level in range(LEVELS):
        size = CHUNK >> level
        pairs.append((t[:, None] // size == t // size) & (t[:, None] // (size // 2) != t // (size // 2)))
    counts = [1.0 / np.minimum(np.arange(1, 17), w) for w in WINDOWS]
    return (c, masks, np.ascontiguousarray(np.stack(pairs, 1).astype(np.int32)),
            np.ascontiguousarray(np.broadcast_to(np.array(counts, np.float32), (P, KV, 16))))


def kernel(**inputs):
    import concourse.bacc as bacc
    from concourse.bass_utils import run_bass_kernel_spmd as run

    a = {k: np.asarray(v) for k, v in inputs.items()}
    jobs = weight_jobs(a["w_mem_kv"][0]) + weight_jobs(a["w_mem_kv"][1])
    for l in range(2):
        w = a["attn_w_in"][0] if l == 0 else a["lru_w_in"][0]
        if l == 0:
            q, k, v, mq = np.split(w, [1024, 1280, 1536], axis=1)
            jobs += weight_jobs(mq) + weight_jobs(k) + weight_jobs(v) + weight_jobs(q)
        else:
            xb, gate, mq = np.split(w, [1024, 2048], axis=1)
            jobs += weight_jobs(mq)
            for x, g in zip(weight_jobs(xb), weight_jobs(gate)):
                jobs += [x, g]
        jobs += weight_jobs(a["w_out"][l][:D]) + weight_jobs(a["w_out"][l][D:])
        for c in range(4):
            jobs += weight_jobs(a["w_up"][l][:, c * D:(c + 1) * D]) + weight_jobs(a["w_down"][l][c * D:(c + 1) * D])
    q, k, v, gate_a, low, pool_in, gate_b, merge = np.split(
        a["w_in_2"][0], [512, 1024, 2048, 3072, 3088, 4112, 5136], axis=1)
    for h in range(KV):
        for w in (q[:, h * P:(h + 1) * P], k[:, h * P:(h + 1) * P], v[:, h * 2 * P:(h + 1) * 2 * P],
                  gate_a[:, h * 2 * P:(h + 1) * 2 * P]):
            jobs += weight_jobs(w)
    for w in (pool_in, gate_b, merge, a["w_proj_a_2"][0], a["w_proj_b_2"][0], a["w_out_2"][0]):
        jobs += weight_jobs(w)
    wj = np.stack(jobs)
    vec = np.concatenate([
        vector_cols(a["mix_norm"]), vector_cols(a["mlp_norm"]), vector_cols(a["mem_norm"]), vector_cols(a["final_norm"]),
        np.broadcast_to(a["attn_sinks"], (P, HEADS)), vector_cols(a["lru_conv_w"]), vector_cols(a["lru_conv_b"]),
        vector_cols(a["lru_ba"]), vector_cols(a["lru_bx"]), vector_cols(a["lru_lambda"]),
        vector_cols(a["b_alpha_2"]), vector_cols(a["gla_norm_g_2"]), vector_cols(a["pool_scale_2"]),
        vector_cols(a["b_merge_2"]), vector_cols(a["ln_g_2"]), vector_cols(a["ln_b_2"])], axis=1)
    lw = np.stack([a["lru_wa"][0, 0], a["lru_wx"][0, 0], a["lru_wa"][0, 1], a["lru_wx"][0, 1]], 2)
    const, masks, pair_masks, inv_count = constants()
    arrays = {
        "xT": feature_major(a["x"][0]), "memT": feature_major(a["mem"][0]),
        "pos": np.ascontiguousarray(np.broadcast_to(a["positions"], (P, S))),
        "wjobs": wj, "lru_w": np.ascontiguousarray(lw), "vec": np.ascontiguousarray(vec), "const": const, "masks": masks,
        "pair_masks": pair_masks, "inv_count": inv_count,
        "alpha_w": np.ascontiguousarray(low.reshape(KT, P, RANK).transpose(1, 0, 2)),
        "alpha_up": a["w_alpha_up_2"][0],
        "pool_w": np.ascontiguousarray(a["w_pool_grp_2"][0].reshape(KV, 2, P, 2 * P).transpose(0, 2, 1, 3)),
    }
    nc = bacc.Bacc("TRN2", target_bir_lowering=False, num_devices=1)
    t = {k: nc.dram_tensor(k, v.shape, mybir.dt.from_np(v.dtype), kind="ExternalInput").ap() for k, v in arrays.items()}
    scratch = nc.dram_tensor("scratch", (1, P, KT, S), F32, kind="Internal").ap()
    out = nc.dram_tensor("out", (P, KT, S), F32, kind="ExternalOutput").ap()
    gate_tiles = nc.dram_tensor("gate_tiles", (16, P, S), F32, kind="Internal").ap()
    kv_tiles = nc.dram_tensor("kv_tiles", (2, P, MEM_HEADS * MEM), F32, kind="Internal").ap()
    build(nc, t["xT"], t["memT"], t["pos"], t["wjobs"], t["lru_w"], t["alpha_w"], t["alpha_up"], t["pool_w"], t["vec"],
          t["const"], t["masks"], t["pair_masks"], t["inv_count"], scratch, gate_tiles, kv_tiles, out)
    r = run(nc, [arrays], core_ids=[0])
    y = r.results[0]["out"]
    return y.transpose(1, 0, 2).reshape(D, S).T[None]
```
